# Optimizing a Trainium2 kernel written in Bass

```python
import math, functools
import jax, jax.numpy as jnp
from jax import lax
import numpy as np

D_MODEL = 1024
BATCH = 1
SEQ = 1024
DEPTH = 1
DEC_BATCH = 8
DEC_SEQ = 8
PAST_LEN = 1024
PAGE_SIZE = 128

N_META = 16
HG_HEADS = 4
HG_DK = 128
HG_DV = 128
HG_CHUNK = 64
HG_WK = HG_HEADS * HG_DK
HG_WV = HG_HEADS * HG_DV
DA_HEADS = 4
DA_DH = 64
DA_DV = 2 * DA_DH
DA_WQK = DA_HEADS * 2 * DA_DH
DA_WV = DA_HEADS * DA_DV
Q_BLOCK = 128
N_BUCKETS = 32
MAX_DISTANCE = 128
N_GROUPS = 4
EXPERTS_PER_GROUP = 4
N_EXPERTS = N_GROUPS * EXPERTS_PER_GROUP
EXPERT_FF = 256
TOP_K = 2
EPS = 1e-6
IN_SPLITS = (HG_WK, HG_WK, HG_WV, HG_WV, DA_WQK, DA_WQK, DA_WV, D_MODEL, D_MODEL)
IN_WIDTH = HG_WK * 2 + HG_WV * 2 + DA_WQK * 2 + DA_WV + 2 * D_MODEL

kernel_name = "hgrn2_diffattn_hier_moe_step"

def rmsnorm(x, w):
    xf = x.astype(jnp.float32)
    y = xf * lax.rsqrt(jnp.mean(xf * xf, axis=-1, keepdims=True) + EPS)
    return (y * w.astype(jnp.float32)).astype(x.dtype)

def split_cols(z):
    outs, start = [], 0
    for width in IN_SPLITS:
        outs.append(z[..., start:start + width])
        start += width
    return outs

def t5_bucket(dist):
    n = jnp.maximum(dist, 0)
    max_exact = N_BUCKETS // 2
    nf = jnp.maximum(n, 1).astype(jnp.float32)
    large = max_exact + (jnp.log(nf / max_exact) / math.log(MAX_DISTANCE / max_exact)
                         * (N_BUCKETS - max_exact)).astype(jnp.int32)
    large = jnp.minimum(large, N_BUCKETS - 1)
    return jnp.where(n < max_exact, n, large)

def hgrn_chunk(S, q, k, v, logf):
    C = q.shape[1]
    b = jnp.cumsum(logf, axis=1)
    o_inter = jnp.einsum('bchk,bhkv->bchv', q * jnp.exp(b), S)
    causal = jnp.tril(jnp.ones((C, C), dtype=bool))[None, :, :, None, None]
    decay = jnp.exp(jnp.where(causal, b[:, :, None] - b[:, None, :], -jnp.inf))
    scores = jnp.sum(q[:, :, None] * k[:, None, :] * decay, axis=-1)
    o_intra = jnp.einsum('btsh,bshv->bthv', scores, v)
    b_last = b[:, -1]
    k_dec = k * jnp.exp(b_last[:, None] - b)
    S_new = jnp.exp(b_last)[..., None] * S + jnp.einsum('bchk,bchv->bhkv', k_dec, v)
    return S_new, o_inter + o_intra

def hgrn_prompt(q, k, v, logf):
    B = q.shape[0]
    S0 = jnp.zeros((B, HG_HEADS, HG_DK, HG_DV), jnp.float32)
    S_meta, o_meta = hgrn_chunk(S0, q[:, :N_META], k[:, :N_META], v[:, :N_META], logf[:, :N_META])

    def to_chunks(a):
        r = a[:, N_META:]
        n_chunks = r.shape[1] // HG_CHUNK
        return jnp.moveaxis(r.reshape(B, n_chunks, HG_CHUNK, *r.shape[2:]), 1, 0)

    def step(S, xs):
        return hgrn_chunk(S, *xs)

    S_fin, o_chunks = lax.scan(step, S_meta, (to_chunks(q), to_chunks(k), to_chunks(v), to_chunks(logf)))
    o_real = jnp.moveaxis(o_chunks, 0, 1).reshape(B, -1, HG_HEADS, HG_DV)
    return jnp.concatenate([o_meta, o_real], axis=1), S_fin

def hgrn_sample(q, k, v, logf, state):
    S_new, o = hgrn_chunk(state.astype(jnp.float32), q, k, v, logf)
    return o, S_new

def diff_attend(q, k, v, q_pos, k_pos, lam, rel_bias):
    logits = jnp.einsum('bqhmd,bkhmd->bhmqk', q, k).astype(jnp.float32) * (DA_DH ** -0.5)
    dist = q_pos[:, None] - k_pos[None, :]
    bias = jnp.transpose(rel_bias[t5_bucket(dist)].astype(jnp.float32), (2, 0, 1))
    logits = jnp.where((dist >= 0)[None, None, None], logits + bias[None, :, None], -1e30)
    p = jax.nn.softmax(logits, axis=-1)
    attn = p[:, :, 0] - lam * p[:, :, 1]
    return jnp.einsum('bhqk,bkhv->bqhv', attn, v.astype(jnp.float32))

def prompt_attn(q, k, v, lam, rel_bias):
    B, T = q.shape[:2]
    L = T - N_META
    k_pos = jnp.arange(T)
    meta_pos = jnp.arange(N_META)
    o_meta = diff_attend(q[:, :N_META], k[:, :N_META], v[:, :N_META], meta_pos, meta_pos, lam, rel_bias)
    n_blocks = L // Q_BLOCK
    q_blocks = jnp.moveaxis(q[:, N_META:].reshape(B, n_blocks, Q_BLOCK, *q.shape[2:]), 1, 0)
    pos_blocks = (N_META + jnp.arange(L)).reshape(n_blocks, Q_BLOCK)
    o_blocks = lax.map(lambda xs: diff_attend(xs[0], k, v, xs[1], k_pos, lam, rel_bias),
                       (q_blocks, pos_blocks))
    o_real = jnp.moveaxis(o_blocks, 0, 1).reshape(B, L, DA_HEADS, DA_DV)
    return jnp.concatenate([o_meta, o_real], axis=1)

def sample_attn(q, k, v, lam, ck, cv, page_table, rel_bias):
    DB, S = q.shape[:2]
    past_k = ck[page_table].reshape(DB, PAST_LEN, DA_HEADS, 2, DA_DH)
    past_v = cv[page_table].reshape(DB, PAST_LEN, DA_HEADS, DA_DV)
    k_all = jnp.concatenate([past_k.astype(k.dtype), k], axis=1)
    v_all = jnp.concatenate([past_v.astype(v.dtype), v], axis=1)
    q_pos = PAST_LEN + jnp.arange(S)
    k_pos = jnp.arange(PAST_LEN + S)
    return diff_attend(q, k_all, v_all, q_pos, k_pos, lam, rel_bias)

def hier_moe(x, w_rg, b_rg, w_re, b_re, w_gate, w_up, w_down):
    B, T, _ = x.shape
    g_logits = (x @ w_rg).astype(jnp.float32) + b_rg.astype(jnp.float32)
    g_prob = jax.nn.softmax(g_logits, axis=-1)
    g_idx = jnp.argmax(g_logits, axis=-1)
    p_g = jnp.take_along_axis(g_prob, g_idx[..., None], axis=-1)
    e_logits = ((x @ w_re).astype(jnp.float32) + b_re.astype(jnp.float32)).reshape(
        B, T, N_GROUPS, EXPERTS_PER_GROUP)
    e_logits = jnp.take_along_axis(e_logits, g_idx[..., None, None], axis=2)[:, :, 0]
    e_prob = jax.nn.softmax(e_logits, axis=-1)
    top_p, top_i = lax.top_k(e_prob, TOP_K)
    gate = p_g * top_p / jnp.sum(top_p, axis=-1, keepdims=True)
    eid = g_idx[..., None] * EXPERTS_PER_GROUP + top_i
    combine = jnp.sum(jax.nn.one_hot(eid, N_EXPERTS, dtype=jnp.float32) * gate[..., None], axis=-2)
    h = jax.nn.silu(jnp.einsum('btd,edf->btef', x, w_gate)) * jnp.einsum('btd,edf->btef', x, w_up)
    return jnp.einsum('btef,efd->btd', h * combine[..., None].astype(h.dtype), w_down)

def hybrid_layer(x, lb, lam_init, hgrn_core, attn_core,
                 norm1_w, w_in, hg_onorm_w, w_hg_out, q_norm_w, k_norm_w, da_lambda,
                 da_onorm_w, w_da_out, w_o, norm2_w, w_router_group, b_router_group,
                 w_router_expert, b_router_expert, w_gate, w_up, w_down):
    B, T, _ = x.shape
    dt = x.dtype
    z = rmsnorm(x, norm1_w) @ w_in
    hq, hf, hi, hg, dq, dk, dv, ga, gb = split_cols(z)
    q_a = jax.nn.silu(hq.astype(jnp.float32)).reshape(B, T, HG_HEADS, HG_DK)
    f = lb + (1.0 - lb) * jax.nn.sigmoid(hf.astype(jnp.float32))
    k_a = (1.0 - f).reshape(B, T, HG_HEADS, HG_DK)
    logf = jnp.log(f).reshape(B, T, HG_HEADS, HG_DK)
    v_a = hi.astype(jnp.float32).reshape(B, T, HG_HEADS, HG_DV)
    o_a, s_new = hgrn_core(q_a, k_a, v_a, logf)
    o_a = rmsnorm(o_a, hg_onorm_w) * jax.nn.silu(hg.astype(jnp.float32)).reshape(B, T, HG_HEADS, HG_DV)
    y_a = o_a.reshape(B, T, HG_WV).astype(dt) @ w_hg_out
    q_b = rmsnorm(dq.reshape(B, T, DA_HEADS, 2, DA_DH), q_norm_w)
    k_b = rmsnorm(dk.reshape(B, T, DA_HEADS, 2, DA_DH), k_norm_w)
    v_b = dv.reshape(B, T, DA_HEADS, DA_DV)
    lp = da_lambda.astype(jnp.float32)
    lam = jnp.exp(jnp.sum(lp[0] * lp[1])) - jnp.exp(jnp.sum(lp[2] * lp[3])) + lam_init
    o_b = attn_core(q_b, k_b, v_b, lam)
    o_b = rmsnorm(o_b, da_onorm_w) * (1.0 - lam_init)
    y_b = o_b.reshape(B, T, DA_WV).astype(dt) @ w_da_out
    merged = jax.nn.sigmoid(ga) * y_a + jax.nn.sigmoid(gb) * y_b
    h = x + merged @ w_o
    out = h + hier_moe(rmsnorm(h, norm2_w), w_router_group, b_router_group,
                       w_router_expert, b_router_expert, w_gate, w_up, w_down)
    return out, k_b.reshape(B, T, DA_HEADS, 2 * DA_DH), v_b, s_new

def setup_inputs(seed: int = 0) -> dict:
    key = jax.random.key(seed)
    ks = jax.random.split(key, 32)
    n_pages = PAST_LEN // PAGE_SIZE
    n_used = DEC_BATCH * n_pages
    n_pool = n_used + n_used // 4
    f32 = jnp.float32

    def nrm(k, shape, scale):
        return jax.random.normal(k, shape, f32) * scale

    page_table = jax.random.permutation(ks[5], n_pool)[:n_used].reshape(DEC_BATCH, n_pages).astype(jnp.int32)
    return {
        "x_prompt": nrm(ks[0], (BATCH, SEQ, D_MODEL), 1.0),
        "x_sample": nrm(ks[1], (DEC_BATCH, DEC_SEQ, D_MODEL), 1.0),
        "cache_k": nrm(ks[2], (DEPTH, n_pool, PAGE_SIZE, DA_HEADS, 2 * DA_DH), 1.0),
        "cache_v": nrm(ks[3], (DEPTH, n_pool, PAGE_SIZE, DA_HEADS, DA_DV), 1.0),
        "state_hgrn": nrm(ks[4], (DEPTH, DEC_BATCH, HG_HEADS, HG_DK, HG_DV), 1.0),
        "page_table": page_table,
        "meta_tokens": nrm(ks[6], (N_META, D_MODEL), 1.0),
        "rel_bias": nrm(ks[7], (N_BUCKETS, DA_HEADS), 0.5),
        "hg_lb_logits": nrm(ks[8], (DEPTH + 1, HG_WK), 0.5),
        "norm1_w": 1.0 + nrm(ks[9], (DEPTH, D_MODEL), 0.1),
        "w_in": nrm(ks[10], (DEPTH, D_MODEL, IN_WIDTH), D_MODEL ** -0.5),
        "hg_onorm_w": 1.0 + nrm(ks[11], (DEPTH, HG_DV), 0.1),
        "w_hg_out": nrm(ks[12], (DEPTH, HG_WV, D_MODEL), HG_WV ** -0.5),
        "q_norm_w": 1.0 + nrm(ks[13], (DEPTH, DA_DH), 0.1),
        "k_norm_w": 1.0 + nrm(ks[14], (DEPTH, DA_DH), 0.1),
        "da_lambda": nrm(ks[15], (DEPTH, 4, DA_DH), 0.1),
        "da_onorm_w": 1.0 + nrm(ks[16], (DEPTH, DA_DV), 0.1),
        "w_da_out": nrm(ks[17], (DEPTH, DA_WV, D_MODEL), DA_WV ** -0.5),
        "w_o": nrm(ks[18], (DEPTH, D_MODEL, D_MODEL), D_MODEL ** -0.5),
        "norm2_w": 1.0 + nrm(ks[19], (DEPTH, D_MODEL), 0.1),
        "w_router_group": nrm(ks[20], (DEPTH, D_MODEL, N_GROUPS), D_MODEL ** -0.5),
        "b_router_group": nrm(ks[21], (DEPTH, N_GROUPS), 0.01),
        "w_router_expert": nrm(ks[22], (DEPTH, D_MODEL, N_EXPERTS), D_MODEL ** -0.5),
        "b_router_expert": nrm(ks[23], (DEPTH, N_EXPERTS), 0.01),
        "w_gate": nrm(ks[24], (DEPTH, N_EXPERTS, D_MODEL, EXPERT_FF), D_MODEL ** -0.5),
        "w_up": nrm(ks[25], (DEPTH, N_EXPERTS, D_MODEL, EXPERT_FF), D_MODEL ** -0.5),
        "w_down": nrm(ks[26], (DEPTH, N_EXPERTS, EXPERT_FF, D_MODEL), EXPERT_FF ** -0.5),
    }

def reference(x_prompt, x_sample, cache_k, cache_v, state_hgrn, page_table, meta_tokens, rel_bias,
              hg_lb_logits, norm1_w, w_in, hg_onorm_w, w_hg_out, q_norm_w, k_norm_w, da_lambda,
              da_onorm_w, w_da_out, w_o, norm2_w, w_router_group, b_router_group,
              w_router_expert, b_router_expert, w_gate, w_up, w_down):
    lb_all = jnp.cumsum(jax.nn.softmax(hg_lb_logits.astype(jnp.float32), axis=0), axis=0)
    xp = jnp.concatenate([jnp.broadcast_to(meta_tokens.astype(x_prompt.dtype)[None],
                                           (x_prompt.shape[0], N_META, D_MODEL)), x_prompt], axis=1)
    xs = x_sample
    kp_rows, vp_rows, sp_rows, ks_rows, vs_rows, ss_rows = [], [], [], [], [], []
    for l in range(DEPTH):
        lam_init = 0.8 - 0.6 * math.exp(-0.3 * l)
        lw = (norm1_w[l], w_in[l], hg_onorm_w[l], w_hg_out[l], q_norm_w[l], k_norm_w[l], da_lambda[l],
              da_onorm_w[l], w_da_out[l], w_o[l], norm2_w[l], w_router_group[l], b_router_group[l],
              w_router_expert[l], b_router_expert[l], w_gate[l], w_up[l], w_down[l])
        xp, kp, vp, sp = hybrid_layer(xp, lb_all[l], lam_init, hgrn_prompt,
                                      functools.partial(prompt_attn, rel_bias=rel_bias), *lw)
        xs, kk, vv, ss = hybrid_layer(xs, lb_all[l], lam_init,
                                      functools.partial(hgrn_sample, state=state_hgrn[l]),
                                      functools.partial(sample_attn, ck=cache_k[l], cv=cache_v[l],
                                                        page_table=page_table, rel_bias=rel_bias), *lw)
        kp_rows.append(kp); vp_rows.append(vp); sp_rows.append(sp)
        ks_rows.append(kk); vs_rows.append(vv); ss_rows.append(ss)
    y_prompt = xp[:, N_META:]
    y_sample = xs
    new_k_prompt = jnp.stack(kp_rows)
    new_v_prompt = jnp.stack(vp_rows)
    new_state_prompt = jnp.stack(sp_rows)
    new_k_sample = jnp.stack(ks_rows)
    new_v_sample = jnp.stack(vs_rows)
    new_state_sample = jnp.stack(ss_rows)
    return (y_prompt, y_sample, new_k_prompt, new_v_prompt, new_state_prompt, new_k_sample, new_v_sample, new_state_sample)


_drawn_inputs = setup_inputs


def setup_inputs(seed=0):
    import zlib

    import numpy as np

    out = dict(_drawn_inputs(seed))
    spreads = {}
    factors = {'b_router_group': 20.373, 'b_router_expert': 2.906}
    for name, (base, spread) in spreads.items():
        noise = np.random.default_rng([zlib.crc32(name.encode()), seed]).standard_normal(out[name].shape)
        drawn = base * np.exp(spread * noise) if base else spread * noise
        out[name] = __import__('jax').numpy.asarray(drawn.astype(out[name].dtype))
    for name, factor in factors.items():
        out[name] = (out[name] * factor).astype(out[name].dtype)
    return out
```

```python
from contextlib import ExitStack

import numpy as np

import concourse.bass as bass
from concourse import mybir

F32 = mybir.dt.float32
I32 = mybir.dt.int32
ALU = mybir.AluOpType
ACT = mybir.ActivationFunctionType
AX_X = mybir.AxisListType.X

P = 128
D = 1024
KC = D // P
SEQ, META, PAST, PAGE = 1024, 16, 1024, 128
DB, DS = 8, 8
NSAMP = DB * DS
HEADS = 4
FIRST = META + NSAMP
TOK = FIRST + SEQ
NT = 1 + SEQ // P
ROWS = [FIRST] + [P] * (NT - 1)
COL = [0] + [FIRST + P * i for i in range(NT - 1)]
CH = TOK // 3
NPG = PAST // PAGE
EPS = 1e-6
LAM_INIT = 0.2
E = 16
FF = 256
SLOTS = (2 * TOK - E) // P + E + 1
BUFFERS = 4
LEVELS = [64, 32, 16, 8, 4, 2, 1]
NEG = -1e30
HQ, HF, HI, HG, DQ, DK, DV, GA, GB = 0, 512, 1024, 1536, 2048, 2560, 3072, 3584, 4608
UNIT_COL = [0, COL[3], COL[6]]
UNIT_W = [COL[3], 3 * P, 3 * P]


def cols(i):
    return slice(COL[i], COL[i] + ROWS[i])


def t5_bucket(n):
    n = np.maximum(n, 0)
    large = 16 + (np.log(np.maximum(n, 1).astype(np.float32) / np.float32(16)) / np.float32(np.log(8.0))
                  * np.float32(16)).astype(np.int32)
    return np.where(n < 16, n, np.minimum(large, 31))


ND = 384
NEAR0 = -127


def constants():
    c = {}
    c["ident"] = np.eye(P, dtype=np.float32)
    s, t = np.arange(P)[:, None], np.arange(P)[None, :]
    lv = np.zeros((P, 8, P), np.float32)
    for n, L in enumerate(LEVELS):
        lv[:, n] = (s // (2 * L) == t // (2 * L)) & (s % (2 * L) < L) & (t % (2 * L) >= L)
    lv[:, 7] = s == t
    c["level_mask"] = lv.reshape(P, 8 * P)
    l0 = lv[:, 3:].copy()
    l0[META:, 0] = 0.0
    c["level_mask0"] = l0[:FIRST].reshape(FIRST, 5 * P)
    seg = np.ones(TOK, np.float32)
    seg[0] = 0
    seg[META:FIRST:DS] = 0
    seg[COL[1]::P] = 0
    c["scan_mask"] = np.broadcast_to(seg[:COL[4]], (P, COL[4])).copy()
    rm = np.zeros((FIRST, 9), np.float32)
    rm[:META, 8] = 1
    for b in range(DB):
        rm[META + DS * b:META + DS * (b + 1), b] = 1
    c["row_mask"] = rm
    dist = np.arange(ND) + NEAR0
    oh = np.zeros((33, ND), np.float32)
    for b in range(32):
        oh[b] = (t5_bucket(dist) == b) & (dist >= 0)
    oh[32] = dist < 0
    c["bucket"] = oh[:, ::-1].copy()
    cm = np.zeros((P, 2 * NSAMP // 2 + 2), np.float32)
    r = np.arange(P)
    b2, h, m, q = r // 64, r // 16 % 4, r // 8 % 2, r % 8
    cm[r, b2 * 32 + h * 8 + q] = 1
    cm[:, 64] = m == 0
    cm[:, 65] = -(m == 1).astype(np.float32)
    c["combine"] = cm
    c["strict"] = (s < t).astype(np.float32)
    c["experts"] = np.broadcast_to(np.concatenate([np.arange(4, 0, -1), 128.0 * np.arange(9), np.arange(40)]).astype(np.float32), (P, 53)).copy()
    c["token_id"] = (np.array(COL)[None, :] + np.arange(P)[:, None]).astype(np.float32)
    c["valid"] = (np.arange(P)[:, None] < np.array(ROWS)[None, :]).astype(np.float32)
    em = np.ones((P, E, NT), np.float32)
    em[:, :, 0] = 0
    c["expert_mask"] = em.reshape(P, E * NT)
    return c


def build(nc, A, out):
    stack = ExitStack()
    with stack:
        arena = stack.enter_context(nc.sbuf_tensor("arena", [P, 53000], F32))
        psum = stack.enter_context(nc.psum_tensor("psum", [P, 8, 512], F32))
        top = [0]

        def sb(*shape):
            n = int(np.prod(shape))
            v = arena[:, top[0]:top[0] + n]
            top[0] += n
            assert top[0] <= 53000, top[0]
            if len(shape) == 2:
                v = v.rearrange("p (a b) -> p a b", b=shape[1])
            if len(shape) == 3:
                v = v.rearrange("p (a b c) -> p a b c", b=shape[1], c=shape[2])
            return v

        K = dict(xT=sb(KC, TOK), oaT=sb(HEADS, TOK))
        kept_end = top[0]
        K.update(
            ident=sb(P), vecT=sb(19), lam=sb(4), lb=sb(12),
            knorm=sb(64), combine=sb(66), half=sb(16), logit=sb(NT, 20), weight=sb(2, NT),
        )
        K["slot"], K["expert"], K["buffer"], K["token"], K["ends"] = (sb(n).bitcast(I32) for n in (2 * NT, SLOTS, SLOTS, SLOTS, E))
        mark = shared = top[0]
        dram = lambda n, s, dt=F32: nc.dram_tensor(n, s, dt, kind="Internal").ap()
        phase_norm1(nc, A, K, sb, psum)
        top[0] = mark
        phase_recurrence(nc, A, K, out, sb, psum)
        top[0] = mark
        K["obT"] = sb(HEADS, TOK)
        after_attention = top[0]
        K["Qs"], K["kS"], K["vS"] = sb(HEADS * DB, 64), sb(HEADS, FIRST), sb(HEADS, P)
        mark = top[0]
        phase_attention(nc, A, K, out, sb, psum, dram)
        top[0] = mark
        phase_sample_attention(nc, A, K, sb, psum)
        top[0] = after_attention
        K["mT"] = sb(KC, TOK)
        K["hn_dram"], K["y_dram"], K["slot_token"] = dram("normed", [TOK, D]), dram("expert_out", [SLOTS * P, D]), dram("slot_token", [SLOTS * P, 1])
        mark = top[0]
        phase_merge(nc, A, K, sb, psum)
        top[0] = 0
        K["h"] = sb(NT, D)
        assert top[0] <= kept_end
        top[0] = mark
        phase_output(nc, A, K, sb, psum)
        top[0] = shared
        K["GU"], K["Wd"] = sb(BUFFERS * KC, 512), sb(BUFFERS * 2, D)
        K["w_in"] = [nc.alloc_semaphore(name=f"expert_w_in{b}") for b in range(BUFFERS)]
        mark = top[0]
        phase_route(nc, A, K, sb, psum)
        top[0] = mark
        phase_experts(nc, A, K, sb, psum)
        top[0] = mark
        phase_combine(nc, A, K, out, sb, psum)


def phase_norm1(nc, A, K, sb, psum):
    with ExitStack() as st:
        st.enter_context(nc.cleanup_on_exit())
        sem = lambda n: nc.alloc_semaphore(name="norm1_" + n)
        const_in, rows_in = sem("const_in"), sem("rows_in")
        x_in = [sem(f"x_in{i}") for i in range(3)]
        ssq_done, rstd_done, xn_done, turned, evacuated = sem("ssq_done"), sem("rstd_done"), sem("xn_done"), sem("turned"), sem("evacuated")
        vec_turned, vec_done, lb_max, lb_exp, setup = sem("vec_turned"), sem("vec_done"), sem("lb_max"), sem("lb_exp"), sem("setup")
        lam_dot, lam_exp = sem("lam_dot"), sem("lam_exp")
        xin, xn, junk = sb(3, D), sb(2, D), sb(D)
        rows, ssq, mean, power, rstd = sb(P), sb(NT), sb(NT), sb(NT), sb(NT)
        lp, lpp, dots, lm = sb(4, 64), sb(2, 64), sb(2), sb(3, HEADS)
        vec = K["vecT"]

        block = st.enter_context(nc.Block())

        @block.sync
        def _(sp):
            sp.dma_start(K["ident"], A["ident"]).then_inc(const_in, 16)
            for r0, n, src in ((0, 8, A["norm1_w"].rearrange("a (r c) -> (a r) c", c=P)),
                               (8, 8, A["hg_lb_logits"].rearrange("a (r c) -> (a r) c", c=P)),
                               (16, 1, A["hg_onorm_w"]), (17, 1, A["da_onorm_w"])):
                sp.dma_start(rows[r0:r0 + n, :], src).then_inc(rows_in, 16)
            for m in range(2):
                sp.dma_start(rows[18:19, 64 * m:64 * m + 64], A["q_norm_w"]).then_inc(rows_in, 16)
            for i in range(NT):
                if i >= 3:
                    sp.wait_ge(xn_done, i - 2)
                if i == 0:
                    sp.dma_start(xin[0:META, 0, :], A["meta_tokens"]).then_inc(x_in[0], 16)
                    sp.dma_start(xin[META:FIRST, 0, :], A["x_sample"].rearrange("a b d -> (a b) d")).then_inc(x_in[0], 16)
                else:
                    sp.dma_start(xin[:, i % 3, :], A["x_prompt"][0, P * (i - 1):P * i, :]).then_inc(x_in[i % 3], 16)
            sp.dma_start(lp.rearrange("p a b -> p (a b)"), A["da_lambda"].rearrange("a b c -> a (b c)").to_broadcast([P, 256])).then_inc(const_in, 16)
            sp.dma_start(K["knorm"], A["k_norm_w"].to_broadcast([P, 64])).then_inc(const_in, 16)
            sp.dma_start(K["combine"], A["combine"]).then_inc(const_in, 16)
            sp.wait_ge(const_in, 64)

        def x_ready(e, i):
            e.wait_ge(x_in[i % 3], 32 if i == 0 else 16 * (i // 3 + (2 if i % 3 == 0 else 1)))

        @block.scalar
        def _(act):
            for i in range(NT):
                x_ready(act, i)
                if i:
                    act.drain()
                act.activation(junk[:ROWS[i], :], xin[:ROWS[i], i % 3, :], ACT.Square,
                               accum_out=ssq[:ROWS[i], i:i + 1]).then_inc(ssq_done, 1)
            act.wait_ge(lb_max, 1)
            act.activation(lm[:, 0:2, :], lm[:, 0:2, :], ACT.Exp).then_inc(lb_exp, 1)
            act.wait_ge(lam_dot, 1)
            act.activation(K["lam"][:, 0:2], dots, ACT.Exp).then_inc(lam_exp, 1)

        @block.gpsimd
        def _(pool):
            pool.memset(power, -0.5).then_inc(setup, 1)
            pool.memset(K["half"], -0.5).then_inc(setup, 1)
            pool.wait_ge(setup, 2)
            for i in range(NT):
                r = ROWS[i]
                pool.wait_ge(ssq_done, i + 1)
                pool.tensor_scalar(mean[:r, i:i + 1], ssq[:r, i:i + 1], 1.0 / D, EPS, ALU.mult, ALU.add)
                pool.drain()
                pool.tensor_tensor(rstd[:r, i:i + 1], mean[:r, i:i + 1], power[:r, i:i + 1], ALU.pow).then_inc(rstd_done, 1)

        @block.vector
        def _(dve):
            def evacuate(i):
                r = ROWS[i]
                dve.wait_ge(turned, i + 1)
                dve.tensor_tensor(K["xT"][:, :, cols(i)], psum[:, 2 * (i % 2):2 * (i % 2) + 2, :].rearrange("p a (b c) -> p (a b) c", c=P)[:, :, :r],
                                  vec[:, 0:8].unsqueeze(2).to_broadcast([P, KC, r]), ALU.mult).then_inc(evacuated, 1)

            for i in range(NT):
                r = ROWS[i]
                x_ready(dve, i)
                dve.wait_ge(rstd_done, i + 1)
                if i >= 2:
                    dve.wait_ge(turned, i - 1)
                dve.tensor_scalar(xn[:r, i % 2, :], xin[:r, i % 3, :], rstd[:r, i:i + 1], None, ALU.mult).then_inc(xn_done, 1)
                if i == 0:
                    dve.wait_ge(vec_turned, 1)
                    dve.tensor_copy(vec, psum[:, 4, 0:19])
                    dve.drain()
                else:
                    evacuate(i - 1)
            evacuate(NT - 1)
            lb, l0, l1 = K["lb"], vec[:, 8:12], vec[:, 12:16]
            dve.tensor_tensor(lm[:, 2, :], l0, l1, ALU.max)
            dve.drain()
            dve.tensor_tensor(lm[:, 0, :], l0, lm[:, 2, :], ALU.subtract)
            dve.tensor_tensor(lm[:, 1, :], l1, lm[:, 2, :], ALU.subtract).then_inc(lb_max, 1)
            dve.wait_ge(lb_exp, 1)
            dve.tensor_tensor(lm[:, 1, :], lm[:, 0, :], lm[:, 1, :], ALU.add)
            dve.drain()
            dve.reciprocal(lm[:, 1, :], lm[:, 1, :])
            dve.drain()
            dve.tensor_tensor(lb[:, 8:12], lm[:, 0, :], lm[:, 1, :], ALU.mult)
            dve.drain()
            dve.tensor_scalar(lb[:, 0:4], lb[:, 8:12], -0.5, 0.5, ALU.mult, ALU.add)
            dve.tensor_scalar(lb[:, 4:8], lb[:, 8:12], 0.5, 0.5, ALU.mult, ALU.add)
            dve.wait_ge(const_in, 64)
            dve.tensor_tensor(lpp, lp[:, 0:4:2, :], lp[:, 1:4:2, :], ALU.mult)
            dve.drain()
            dve.tensor_reduce(dots, lpp, AX_X, ALU.add).then_inc(lam_dot, 1)
            dve.wait_ge(lam_exp, 1)
            lam = K["lam"]
            dve.tensor_tensor(lam[:, 2:3], lam[:, 0:1], lam[:, 1:2], ALU.subtract)
            dve.drain()
            dve.tensor_scalar(lam[:, 3:4], lam[:, 2:3], -1.0, -LAM_INIT, ALU.mult, ALU.add)
            dve.tensor_scalar(vec[:, 17:18], vec[:, 17:18], 1.0 - LAM_INIT, None, ALU.mult)
            dve.tensor_scalar(vec[:, 18:19], vec[:, 18:19], 0.125, None, ALU.mult)

        @block.tensor
        def _(pe):
            pe.wait_ge(const_in, 16)
            pe.wait_ge(rows_in, 96)
            pe.transpose(psum[:, 4, 0:19], rows[0:19, :], K["ident"][0:19, 0:19]).then_inc(vec_turned, 1)
            for i in range(NT):
                r = ROWS[i]
                pe.wait_ge(xn_done, i + 1)
                if i >= 2:
                    pe.wait_ge(evacuated, i - 1)
                for k in range(KC):
                    mm = pe.transpose(psum[:, 2 * (i % 2) + k // 4, P * (k % 4):P * (k % 4) + r],
                                      xn[:r, i % 2, P * k:P * k + P], K["ident"][:r, :r])
                mm.then_inc(turned, 1)


def phase_recurrence(nc, A, K, out, sb, psum):
    W = A["w_in"][0].rearrange("(k p) n -> p k n", p=P)
    channel = lambda h: [("c", h, w, n) for w in "qf" for n in range(3)]
    token = lambda p: [("t", p, "", i) for i in range(NT)]
    STEPS = HEADS * NT
    start = channel(0) + token(0)[:4]
    at_slot = [[] for _ in range(STEPS)]
    for units, slots in ((token(0)[4:], range(3, 8)), (channel(1), range(0, 6)), (channel(2), range(9, 15)),
                         (channel(3), range(18, 24)), (token(1), (8, 15, 16, 17, 20, 22, 23, 24, 25))):
        for u, slot in zip(units, slots):
            at_slot[slot].append(u)
    HEADSTART = len(start)
    proj = start + [u for us in at_slot for u in us]
    jobs = list(proj[:HEADSTART])
    for s in range(STEPS + 2):
        if s < STEPS:
            jobs += at_slot[s] + [("k", s)]
        if 1 <= s <= STEPS:
            jobs += [("o", s - 1)] + [("m", s - 1)] * ((s - 1) % NT == 0)
        if s >= 2:
            jobs += [("g", s - 2)]
    turn_of = {u: n for n, u in enumerate(jobs)}
    index = {u: n for n, u in enumerate(proj)}
    with ExitStack() as st:
        st.enter_context(nc.cleanup_on_exit())
        sem = lambda n: nc.alloc_semaphore(name="recurrence_" + n)
        w_in = [sem("w_in0"), sem("w_in1")]
        c_in, smask_in, projected, tanh_done, q_done, tok_act, tok_dve = sem("c_in"), sem("smask_in"), sem("projected"), sem("tanh_done"), sem("q_done"), sem("tok_act"), sem("tok_dve")
        f_done, logf_done, x_sub, x_exp, unit_done = sem("f_done"), sem("logf_done"), sem("x_sub"), sem("x_exp"), sem("unit_done")
        leveled, kd_turned, kd_copied, at_done, o_done, st_done, s_new = sem("leveled"), sem("kd_turned"), sem("kd_copied"), sem("at_done"), sem("o_done"), sem("st_done"), sem("s_new")
        ssq_done, rstd_done, og_done, og_turned, oa_done = sem("ssq_done"), sem("rstd_done"), sem("og_done"), sem("og_turned"), sem("oa_done")
        setup, state_in, state_out, qz_done, vm_done = sem("setup"), [sem("state_in")], sem("state_out"), sem("qz_done"), sem("vm_done")
        meanw = sem("meanw")
        Wb = sb(2, KC * 512)
        Wb = [Wb[:, j, :].rearrange("p (k n) -> p k n", n=512) for j in range(2)]
        th2 = sb(2, TOK)
        q2 = sb(2, TOK)
        tq = sb(2, CH)
        hi, gate = sb(2 * NT, 256), sb(2 * NT, 256)
        kb, bb, kd, eb, qe = (sb(2, 384) for _ in range(5))
        X = sb(2, 7 * 384)
        lmask, lmask0, smask, rmask = sb(8, P), sb(5, P), sb(COL[4]), sb(9)
        AM, AT, kdT = sb(8 * P), sb(2, P), sb(2, P)
        Vm, QEz = sb(9, P), sb(DB, FIRST)
        S = sb(2, P)
        Sb = sb(DB, P)
        og = sb(2, P)
        junk, ssq, rstd = sb(P), sb(STEPS), sb(STEPS)
        block = st.enter_context(nc.Block())

        def unit_of(s):
            return s // 3

        def bank_of(job):
            return psum[:, (0, 1, 6, 7)[turn_of[job] % 4], :]

        def bank_free(e, job):
            if turn_of[job] < 4:
                return
            last = jobs[turn_of[job] - 4]
            if last[0] == "k":
                return e.wait_ge(kd_copied, last[1] + 1)
            if last[0] == "o":
                return e.wait_ge(og_done, last[1] + 1)
            if last[0] == "g":
                return e.wait_ge(oa_done, last[1] + 1)
            if last[0] == "m":
                return e.wait_ge(s_new, last[1] + 1)
            kind, a, w, _ = last
            n = index[last]
            if kind == "t":
                e.wait_ge(tok_act, sum(u[0] == "t" for u in proj[:n + 1]))
                e.wait_ge(tok_dve, sum(u[0] == "t" for u in proj[:n + 1]))
            elif w == "q":
                e.wait_ge(q_done, sum(u[2] == "q" for u in proj[:n + 1]))
            else:
                e.wait_ge(tanh_done, sum(u[0] == "c" for u in proj[:n + 1]))

        @block.sync
        def _(sp):
            sp.dma_start(smask, A["scan_mask"]).then_inc(smask_in, 16)
            sp.dma_start(Sb, A["state_hgrn"][0, :, 0].rearrange("b k v -> k b v")).then_inc(state_in[0], 16)
            for blk in range(4):
                p = blk // 2
                if blk >= 2:
                    last = [n for n, u in enumerate(proj) if (u[0] == "t") == bool(blk % 2) and (u[1] if u[0] == "t" else u[1] // 2) == p - 1][-1]
                    sp.wait_ge(projected, last + 1)
                for j, base in enumerate((HI, HG) if blk % 2 else (HQ, HF)):
                    sp.dma_start(Wb[blk % 2][:, :, 256 * j:256 * j + 256],
                                 W[:, :, base + 256 * p:base + 256 * p + 256]).then_inc(w_in[blk % 2], 16)
                if blk == 0:
                    sp.dma_start(lmask.rearrange("p a b -> p (a b)"), A["level_mask"]).then_inc(c_in, 16)
                    sp.dma_start(lmask0[:FIRST].rearrange("p a b -> p (a b)"), A["level_mask0"]).then_inc(c_in, 16)
                    sp.dma_start(rmask[:FIRST], A["row_mask"]).then_inc(c_in, 16)
            for h in range(HEADS):
                if h:
                    sp.wait_ge(s_new, NT * h)
                    sp.wait_ge(state_out, 32 * h)
                    sp.dma_start(Sb, A["state_hgrn"][0, :, h].rearrange("b k v -> k b v")).then_inc(state_in[0], 16)
                sp.wait_ge(s_new, NT * h + 1)
                sp.dma_start(out["new_state_sample"][0, :, h].rearrange("b k v -> k b v"), Sb).then_inc(state_out, 16)
                sp.wait_ge(s_new, NT * h + NT)
                sp.dma_start(out["new_state_prompt"][0, 0, h], S[:, (NT - 1) % 2, :]).then_inc(state_out, 16)
            sp.wait_ge(state_out, 32 * HEADS)

        @block.tensor
        def _(pe):
            def product(u):
                n = index[u]
                kind, a, w, i = u
                bank_free(pe, u)
                bank = bank_of(u)
                if kind == "c":
                    pe.wait_ge(w_in[0], 32 * (a // 2 + 1))
                    c0 = 256 * (w == "f") + P * (a % 2)
                    for k in range(KC):
                        mm = pe.matmul(bank[:, 0:CH], Wb[0][:, k, c0:c0 + P], K["xT"][:, k, CH * i:CH * i + CH],
                                       start=(k == 0), stop=(k == KC - 1))
                else:
                    pe.wait_ge(w_in[1], 32 * (a + 1))
                    for k in range(KC):
                        mm = pe.matmul(bank[:ROWS[i], :], K["xT"][:, k, cols(i)], Wb[1][:, k, :],
                                       start=(k == 0), stop=(k == KC - 1))
                mm.then_inc(projected, 1)

            def scores(s):
                i, u = s % NT, s // 3
                r, x0 = ROWS[i], COL[i] - UNIT_COL[u % 3]
                xs = slice(x0, x0 + r)
                lev = psum[:, 2 + 2 * (s % 2):4 + 2 * (s % 2), :].rearrange("p a (b c) -> p (a b) c", c=P)
                pe.wait_ge(unit_done, u + 1)
                if s >= 2:
                    pe.wait_ge(s_new, s - 1)
                Xu = X[:, u % 2, :].rearrange("p (l c) -> p l c", l=7)
                first = 3 if i == 0 else 0
                for l in range(first, 7):
                    pe.matmul(lev[:r, l - first, :r], Xu[:, l, xs], Xu[:, l, xs], start=True, stop=True)
                pe.matmul(lev[:r, 7 - first, :r], kb[:, u % 2, xs], q2[:, s // NT % 2, cols(i)],
                          start=True, stop=True).then_inc(leveled, 1)
                bank_free(pe, ("k", s))
                pe.transpose(bank_of(("k", s))[:r, 0:P], kd[:, u % 2, xs], K["ident"]).then_inc(kd_turned, 1)

            def outputs(s):
                h, i, u = s // NT, s % NT, s // 3
                r, x0 = ROWS[i], COL[i] - UNIT_COL[u % 3]
                v = hi[:r, NT * (h // 2) + i, P * (h % 2):P * (h % 2) + P]
                pe.wait_ge(at_done, s + 1)
                pe.wait_ge(kd_copied, s + 1)
                pe.wait_ge(tok_act, NT * (h // 2) + i + 1)
                bank_free(pe, ("o", s))
                o = bank_of(("o", s))[:r, 0:P]
                pe.matmul(o, AT[:r, s % 2, :r], v, start=True, stop=False)
                if i == 0:
                    pe.wait_ge(state_in[0], 16 * (h + 1))
                    pe.wait_ge(qz_done, h + 1)
                    for b in range(DB):
                        mm = pe.matmul(o, QEz[:, b, :], Sb[:, b, :], start=False, stop=(b == DB - 1))
                    mm.then_inc(o_done, 1)
                    pe.wait_ge(vm_done, h + 1)
                    lev = psum[:, 2 + 2 * (s % 2):4 + 2 * (s % 2), :]
                    for j in range(2):
                        pe.matmul(lev[:, j, :], kdT[:r, s % 2, :], Vm[:r, 4 * j:4 * j + 4, :].rearrange("p a b -> p (a b)"),
                                  start=True, stop=True)
                    bank_free(pe, ("m", s))
                    pe.matmul(bank_of(("m", s))[:, 0:P], kdT[:r, s % 2, :], Vm[:r, 8, :], start=True, stop=True).then_inc(st_done, 1)
                else:
                    pe.wait_ge(s_new, s)
                    pe.matmul(o, qe[:, u % 2, x0:x0 + r], S[:, (i + 1) % 2, :], start=False, stop=True).then_inc(o_done, 1)
                    pe.matmul(psum[:, 3 + 2 * (s % 2), 0:P], kdT[:r, s % 2, :], v, start=True, stop=True).then_inc(st_done, 1)

            def turn(s):
                r = ROWS[s % NT]
                pe.wait_ge(og_done, s + 1)
                bank_free(pe, ("g", s))
                pe.transpose(bank_of(("g", s))[:, 0:r], og[:r, s % 2, :],
                             K["ident"][:r, :r]).then_inc(og_turned, 1)

            for u in proj[:HEADSTART]:
                product(u)
            for s in range(STEPS + 2):
                if s < STEPS:
                    for u in at_slot[s]:
                        product(u)
                    scores(s)
                if 1 <= s <= STEPS:
                    outputs(s - 1)
                if s >= 2:
                    turn(s - 2)

        def act_product(act, u):
            n = index[u]
            kind, a, w, i = u
            bank = bank_of(u)
            act.wait_ge(projected, n + 1)
            if kind == "c" and w == "q":
                nq = sum(x[2] == "q" for x in proj[:n])
                if nq >= 2:
                    act.wait_ge(q_done, nq - 1)
                act.activation(tq[:, nq % 2, :], bank[:, 0:CH], ACT.Tanh, scale=0.5).then_inc(tanh_done, 1)
            elif kind == "c":
                if a >= 2:
                    act.wait_ge(unit_done, 3 * (a - 1))
                act.activation(th2[:, a % 2, CH * i:CH * i + CH], bank[:, 0:CH], ACT.Tanh, scale=0.5).then_inc(tanh_done, 1)
            else:
                r = ROWS[i]
                act.activation(gate[:r, NT * a + i, :], bank[:r, 256:512], ACT.Tanh, scale=0.5)
                act.activation(hi[:r, NT * a + i, :], bank[:r, 0:256], ACT.Copy).then_inc(tok_act, 1)

        @block.scalar
        def _(act):
            def unit_log(u):
                w = UNIT_W[u % 3]
                act.wait_ge(f_done, u + 1)
                act.activation(bb[:, u % 2, :w], bb[:, u % 2, :w], ACT.Ln).then_inc(logf_done, 1)

            def unit_decays(u):
                w = UNIT_W[u % 3]
                act.wait_ge(x_sub, 2 * u + 1)
                act.activation(eb[:, u % 2, :w], bb[:, u % 2, :w], ACT.Exp)
                act.activation(kd[:, u % 2, :w], kd[:, u % 2, :w], ACT.Exp).then_inc(x_exp, 1)

            def unit_levels(u):
                w = UNIT_W[u % 3]
                Xu = X[:, u % 2, :].rearrange("p (l c) -> p l c", l=7)
                act.wait_ge(x_sub, 2 * u + 2)
                if u % 3 == 0:
                    act.activation(Xu[:, 0:3, FIRST:w], Xu[:, 0:3, FIRST:w], ACT.Exp)
                    act.activation(Xu[:, 3:7, 0:w], Xu[:, 3:7, 0:w], ACT.Exp).then_inc(x_exp, 1)
                else:
                    act.activation(Xu[:, :, 0:w], Xu[:, :, 0:w], ACT.Exp).then_inc(x_exp, 1)

            def tile_copy(s):
                r = ROWS[s % NT]
                act.wait_ge(kd_turned, s + 1)
                if s >= 2:
                    act.wait_ge(st_done, s - 1)
                act.activation(kdT[:r, s % 2, :], bank_of(("k", s))[:r, 0:P], ACT.Copy).then_inc(kd_copied, 1)

            def tile_square(s):
                r = ROWS[s % NT]
                act.wait_ge(o_done, s + 1)
                act.drain()
                act.activation(junk[:r], bank_of(("o", s))[:r, 0:P], ACT.Square,
                               accum_out=ssq[:r, s:s + 1]).then_inc(ssq_done, 1)

            def tile_out(s):
                i = s % NT
                act.wait_ge(og_turned, s + 1)
                act.activation(K["oaT"][:, s // NT, cols(i)], bank_of(("g", s))[:, 0:ROWS[i]],
                               ACT.Copy, scale=K["vecT"][:, 16:17]).then_inc(oa_done, 1)

            for u in channel(0):
                act_product(act, u)
            parts = (unit_log, unit_decays, unit_levels)
            for part in parts:
                part(0)
            for u in start[len(channel(0)):]:
                act_product(act, u)
            for s in range(STEPS + 2):
                if s < STEPS:
                    for u in at_slot[s]:
                        act_product(act, u)
                    tile_copy(s)
                if s % 3 == 2 and s < STEPS - 3:
                    unit_levels(s // 3 + 1)
                if 1 <= s <= STEPS:
                    tile_square(s - 1)
                if s >= 2:
                    tile_out(s - 2)
                if s % 3 < 2 and s < STEPS - 3:
                    parts[s % 3](s // 3 + 1)

        @block.gpsimd
        def _(pool):
            pool.memset(QEz, 0.0).then_inc(setup, 1)
            for s in range(STEPS):
                r = ROWS[s % NT]
                if s % NT == 0:
                    h = s // NT
                    pool.wait_ge(tok_act, NT * (h // 2) + 1)
                    pool.wait_ge(c_in, 48)
                    if h:
                        pool.wait_ge(st_done, NT * (h - 1) + 1)
                    pool.tensor_tensor(Vm[:r], hi[:r, NT * (h // 2), P * (h % 2):P * (h % 2) + P].unsqueeze(1).to_broadcast([r, 9, P]),
                                       rmask[:r].unsqueeze(2).to_broadcast([r, 9, P]), ALU.mult).then_inc(vm_done, 1)
                pool.wait_ge(ssq_done, s + 1)
                pool.tensor_scalar(ssq[:r, s:s + 1], ssq[:r, s:s + 1], 16.0 / (4 * P), 16 * EPS, ALU.mult, ALU.add)
                pool.drain()
                pool.tensor_tensor(rstd[:r, s:s + 1], ssq[:r, s:s + 1], K["half"][:r, 0:1], ALU.pow).then_inc(rstd_done, 1)

        @block.vector
        def _(dve):
            def product(u):
                n = index[u]
                kind, a, w, i = u
                bank = bank_of(u)
                if kind == "c" and w == "q":
                    nq = sum(x[2] == "q" for x in proj[:n])
                    dve.wait_ge(tanh_done, sum(x[0] == "c" for x in proj[:n + 1]))
                    if a >= 2:
                        dve.wait_ge(leveled, NT * (a - 1))
                    dve.scalar_tensor_tensor(q2[:, a % 2, CH * i:CH * i + CH], tq[:, nq % 2, :], 1.0, bank[:, 0:CH],
                                             ALU.add, ALU.mult).then_inc(q_done, 1)
                elif kind == "t":
                    r = ROWS[i]
                    g = gate[:r, NT * a + i, :]
                    dve.wait_ge(tok_act, NT * a + i + 1)
                    dve.scalar_tensor_tensor(g, g, 1.0, bank[:r, 256:512], ALU.add, ALU.mult).then_inc(tok_dve, 1)

            def halves(u, L):
                o = FIRST if u % 3 == 0 and L > 8 else 0
                return o, (UNIT_W[u % 3] - o) // (2 * L)

            def unit_gate(u):
                h, w, c0, off = u // 3, UNIT_W[u % 3], UNIT_COL[u % 3], (FIRST if u % 3 == 0 else 0)
                k, b, d = kb[:, u % 2, :], bb[:, u % 2, :], kd[:, u % 2, :]
                lb = K["lb"]
                dve.wait_ge(tanh_done, sum(x[0] == "c" for x in proj[:index[("c", h, "f", 2)] + 1]))
                if u >= 2:
                    dve.wait_ge(leveled, 3 * (u - 1))
                    dve.wait_ge(kd_turned, 3 * (u - 1))
                dve.drain()
                dve.tensor_scalar(b[:, :w], th2[:, h % 2, c0:c0 + w], lb[:, h:h + 1], lb[:, 4 + h:5 + h], ALU.mult, ALU.add)
                dve.drain()
                dve.tensor_scalar(k[:, :w], b[:, :w], -1.0, 1.0, ALU.mult, ALU.add).then_inc(f_done, 1)

            def unit_sums(u):
                h, w, c0, off = u // 3, UNIT_W[u % 3], UNIT_COL[u % 3], (FIRST if u % 3 == 0 else 0)
                k, b, d = kb[:, u % 2, :], bb[:, u % 2, :], kd[:, u % 2, :]
                m0 = 0 if off else COL[1]
                Xu = X[:, u % 2, :].rearrange("p (l c) -> p l c", l=7)
                dve.wait_ge(logf_done, u + 1)
                dve.drain()
                dve.tensor_tensor_scan(b[:, :w], smask[:, m0:m0 + w], b[:, :w], 0.0, ALU.mult, ALU.add)
                dve.drain()
                if off:
                    dve.tensor_tensor(d[:, 0:META], b[:, META - 1:META].to_broadcast([P, META]), b[:, 0:META], ALU.subtract)
                    bs, ds = (x[:, META:FIRST].rearrange("p (n c) -> p n c", c=DS) for x in (b, d))
                    dve.tensor_tensor(ds, bs[:, :, DS - 1:DS].to_broadcast([P, DB, DS]), bs, ALU.subtract)
                n = (w - off) // P
                bs, ds = (x[:, off:w].rearrange("p (n c) -> p n c", c=P) for x in (b, d))
                dve.tensor_tensor(ds, bs[:, :, P - 1:P].to_broadcast([P, n, P]), bs, ALU.subtract).then_inc(x_sub, 1)

                for l, L in enumerate(LEVELS):
                    o, m = halves(u, L)
                    bs = b[:, o:w].rearrange("p (n c) -> p n c", c=2 * L)
                    xs = Xu[:, l, o:w].rearrange("p (n c) -> p n c", c=2 * L)
                    mid = bs[:, :, L - 1:L].to_broadcast([P, m, L])
                    dve.tensor_tensor(xs[:, :, 0:L], mid, bs[:, :, 0:L], ALU.subtract)
                    ins = dve.tensor_tensor(xs[:, :, L:2 * L], bs[:, :, L:2 * L], mid, ALU.subtract)
                ins.then_inc(x_sub, 1)

            def unit_products(u):
                h, w, c0, off = u // 3, UNIT_W[u % 3], UNIT_COL[u % 3], (FIRST if u % 3 == 0 else 0)
                k, b, d = kb[:, u % 2, :], bb[:, u % 2, :], kd[:, u % 2, :]
                q = q2[:, h % 2, c0:c0 + w]
                Xu = X[:, u % 2, :].rearrange("p (l c) -> p l c", l=7)
                dve.wait_ge(x_exp, 2 * u + 1)
                dve.tensor_tensor(d[:, :w], d[:, :w], k[:, :w], ALU.mult)
                dve.tensor_tensor(qe[:, u % 2, :w], eb[:, u % 2, :w], q, ALU.mult)
                if u % 3 == 0:
                    dve.drain()
                    if h:
                        dve.wait_ge(o_done, NT * (h - 1) + 1)
                    else:
                        dve.wait_ge(setup, 1)
                    diag = QEz.rearrange("p a b -> p (a b)")[:, META:]
                    for bt in range(DB):
                        ins = dve.tensor_copy(QEz[:, bt, META + DS * bt:META + DS * bt + DS],
                                              qe[:, u % 2, META + DS * bt:META + DS * bt + DS])
                    ins.then_inc(qz_done, 1)
                dve.wait_ge(x_exp, 2 * u + 2)
                for l, L in enumerate(LEVELS):
                    o, m = halves(u, L)
                    xs = Xu[:, l, o:w].rearrange("p (n c) -> p n c", c=2 * L)
                    ks = k[:, o:w].rearrange("p (n c) -> p n c", c=2 * L)
                    qs = q[:, o:w].rearrange("p (n c) -> p n c", c=2 * L)
                    dve.tensor_tensor(xs[:, :, 0:L], xs[:, :, 0:L], ks[:, :, 0:L], ALU.mult)
                    ins = dve.tensor_tensor(xs[:, :, L:2 * L], xs[:, :, L:2 * L], qs[:, :, L:2 * L], ALU.mult)
                ins.then_inc(unit_done, 1)

            def tile_scores(s):
                i = s % NT
                r, nl = ROWS[i], 5 if i == 0 else 8
                lev = psum[:, 2 + 2 * (s % 2):4 + 2 * (s % 2), :].rearrange("p a (b c) -> p (a b) c", c=P)
                am = AM[:r, 0:nl * r].rearrange("p (l c) -> p l c", l=nl)
                dve.wait_ge(leveled, s + 1)
                if s == 0:
                    dve.wait_ge(c_in, 48)
                if s >= 2:
                    dve.wait_ge(o_done, s - 1)
                dve.drain()
                dve.tensor_tensor(am, lev[:r, 0:nl, :r], (lmask0 if i == 0 else lmask)[:r, :, :r], ALU.mult)
                dve.drain()
                dve.tensor_reduce(AT[:r, s % 2, :r], am.rearrange("p l c -> p c l"), AX_X, ALU.add).then_inc(at_done, 1)

            def tile_state(s):
                h, i, u = s // NT, s % NT, s // 3
                r, x0 = ROWS[i], COL[i] - UNIT_COL[u % 3]
                dve.wait_ge(st_done, s + 1)
                dve.wait_ge(rstd_done, s + 1)
                if s >= 2:
                    dve.wait_ge(og_turned, s - 1)
                e = eb[:, u % 2, :]
                upd = bank_of(("m", s))[:, 0:P] if i == 0 else psum[:, 3 + 2 * (s % 2), 0:P]
                if i == 0:
                    dve.wait_ge(state_in[0], 16 * (h + 1))
                    es = e[:, META:FIRST].rearrange("p (n c) -> p n c", c=DS)[:, :, DS - 1:DS].to_broadcast([P, DB, P])
                    dve.tensor_tensor(Sb, Sb, es, ALU.mult)
                    dve.tensor_copy(S[:, 0, :], upd)
                    dve.drain()
                    lev = psum[:, 2 + 2 * (s % 2):4 + 2 * (s % 2), :].rearrange("p a (b c) -> p (a b) c", c=P)
                    dve.tensor_tensor(Sb, Sb, lev, ALU.add).then_inc(s_new, 1)
                else:
                    dve.scalar_tensor_tensor(S[:, i % 2, :], S[:, (i + 1) % 2, :], e[:, x0 + P - 1:x0 + P], upd,
                                             ALU.mult, ALU.add).then_inc(s_new, 1)
                g = gate[:r, NT * (h // 2) + i, P * (h % 2):P * (h % 2) + P]
                dve.scalar_tensor_tensor(og[:r, s % 2, :], bank_of(("o", s))[:r, 0:P], rstd[:r, s:s + 1], g,
                                         ALU.mult, ALU.mult).then_inc(og_done, 1)

            for u in channel(0):
                product(u)
            dve.wait_ge(smask_in, 16)
            parts = (unit_gate, unit_sums, unit_products)
            for part in parts:
                part(0)
            for u in start[len(channel(0)):]:
                product(u)
            for s in range(STEPS + 1):
                if s < STEPS:
                    for u in at_slot[s]:
                        product(u)
                    tile_scores(s)
                if s:
                    dve.wait_ge(o_done, s)
                    tile_state(s - 1)
                if s < STEPS - 3:
                    parts[s % 3](s // 3 + 1)


def phase_attention(nc, A, K, out, sb, psum, dram):
    W = A["w_in"][0].rearrange("(k p) n -> p k n", p=P)
    NQ = NT
    STEPS = HEADS * NQ
    groups = lambda s: (s % NQ + 4) // 4
    zx = [("z", 0, 0)]
    for i in range(1, NT):
        zx += [("z", 0, i), ("x", 0, i - 1)]
    zx += [("x", 0, NT - 1)]
    slots = []
    for s in range(STEPS + 2):
        h, i = s // NQ, s % NQ
        slot = []
        if 1 <= s <= STEPS:
            slot += [("a", s - 1, g) for g in range(groups(s - 1))]
        if s < STEPS:
            slot += [("L", s, 0), ("L", s, 1)] + ([("e", s, 0)] if i == NQ - 1 else [])
        if 1 <= s <= STEPS:
            slot += [("o", s - 1, 0)]
        if h + 1 < HEADS and s < STEPS:
            slot += [("z", h + 1, i)]
        if 1 <= s <= STEPS and (s - 1) // NQ + 1 < HEADS:
            slot += [("x", (s - 1) // NQ + 1, (s - 1) % NQ)]
        if s >= 2:
            slot += [("g", s - 2, 0)]
        slots.append(slot)
    jobs = zx + [j for slot in slots for j in slot if j[0] != "L"]
    turn_of = {j: n for n, j in enumerate(jobs)}
    a_index = {j: n for n, j in enumerate(j for j in jobs if j[0] == "a")}

    skew = [dram(f"bias_skew{h}", [P * (ND + 1)]) for h in range(HEADS)]
    K["skew"] = skew
    with ExitStack() as st:
        st.enter_context(nc.cleanup_on_exit())
        sem = lambda n: nc.alloc_semaphore(name="attention_" + n)
        w_in = [sem("w_in0"), sem("w_in1")]
        c_in, bk_in, rel_ready, bias_made, bias_row, skewed, bias_in, setup = (sem(n) for n in (
            "c_in", "bk_in", "rel_ready", "bias_made", "bias_row", "skewed", "bias_in", "setup"))
        projected, squared, summed, rstd_done, normed, k_scaled, x_turned, x_done, saved = (sem(n) for n in (
            "projected", "squared", "summed", "rstd_done", "normed", "k_scaled", "x_turned", "x_done", "saved"))
        logits, max_done, exp_done, a_done, a_turned, a_act, a_dve, o_done, ssq_done, orstd_done, og_done, og_turned, ob_done = (sem(n) for n in (
            "logits", "max_done", "exp_done", "a_done", "a_turned", "a_act", "a_dve", "o_done", "ssq_done", "orstd_done", "og_done", "og_turned", "ob_done"))
        kv_out = [sem("kv_out0"), sem("kv_out1")]
        Wb = [sb(KC, 384) for _ in range(2)]
        qz = [sb(2, TOK) for _ in range(2)]
        kT = [sb(TOK) for _ in range(2)]
        kout = [sb(NT, P) for _ in range(2)]
        v = [sb(NT, P) for _ in range(2)]
        sq, zn = sb(256), sb(2, 256)
        zs, zr = sb(NT * HEADS, 4), sb(NT * HEADS, 4)
        Bn = [sb(256) for _ in range(HEADS)]
        rel, rel31, relh, bucket, vecs = sb(HEADS), sb(HEADS), sb(HEADS, P), sb(ND), sb(HEADS, ND)
        Pm = sb(2, SEQ + META)
        Am, aT = sb(SEQ + META), sb(NT, P)
        nmax, sums, coef, ssq, rr, mt = sb(STEPS, 4), sb(STEPS, 4), sb(STEPS, 4), sb(STEPS), sb(STEPS, 2), sb(2, META)
        junk, og = sb(P), sb(2, P)
        block = st.enter_context(nc.Block())
        lg = [psum[:, 2 * m:2 * m + 2, :].rearrange("p a b -> p (a b)") for m in range(2)]
        zn_of = lambda h, i: NT * h + i

        def bank_of(job):
            return psum[:, 4 + turn_of[job] % 4, :]

        def bank_free(e, job):
            if turn_of[job] < 4:
                return
            kind, a, b = jobs[turn_of[job] - 4]
            if kind == "z":
                e.wait_ge(normed, NT * a + b + 1)
            elif kind == "x":
                e.wait_ge(x_done, NT * a + b + 1)
            elif kind == "e":
                e.wait_ge(exp_done, 2 * a + 2)
            elif kind == "a":
                n = a_index[(kind, a, b)]
                e.wait_ge(a_dve if n % 2 else a_act, n // 2 + 1)
            elif kind == "o":
                e.wait_ge(og_done, a + 1)
            else:
                e.wait_ge(ob_done, a + 1)

        def place_turned(copy, s, g):
            i = s % NQ
            r, bank = (P if i else META), bank_of(("a", s, g))
            full = min(4 * g + 4, i) - 4 * g
            if full > 0:
                ins = copy(aT[:, 4 * g:4 * g + full, :r], bank[:, 0:P * full].rearrange("p (a b) -> p a b", b=P)[:, :, :r])
            if i < 4 * g + 4:
                ins = copy(aT[:META, i, :r], bank[:META, P * (i % 4):P * (i % 4) + r])
            return ins

        @block.sync
        def _(sp):
            def weights(h):
                if h >= 2:
                    sp.wait_ge(projected, NT * (h - 1))
                for j, base in enumerate((DQ, DK, DV)):
                    sp.dma_start(Wb[h % 2][:, :, P * j:P * j + P], W[:, :, base + P * h:base + P * h + P]).then_inc(w_in[h % 2], 16)

            sp.dma_start(rel31[0:32], A["rel_bias"][31:32, :].to_broadcast([32, HEADS])).then_inc(c_in, 16)
            sp.dma_start(rel[0:32], A["rel_bias"]).then_inc(c_in, 16)
            sp.dma_start(bucket[0:33], A["bucket"]).then_inc(bk_in, 16)
            weights(0)
            weights(1)
            for h in range(HEADS):
                sp.wait_ge(bias_row, h + 1)
                sp.dma_start(skew[h].rearrange("(p c) -> p c", c=ND + 1)[:, 0:ND], vecs[:, h, :]).then_inc(skewed, 16)
            sp.wait_ge(skewed, 16 * HEADS)
            for h in range(HEADS):
                sp.dma_start(Bn[h], skew[h][P:P + P * ND].rearrange("(p c) -> p c", c=ND)[:, 0:256]).then_inc(bias_in, 16)
            for h in range(HEADS):
                sp.wait_ge(x_done, NT * (h + 1))
                for src, big, small in ((kout[h % 2], out["new_k_prompt"], out["new_k_sample"]),
                                        (v[h % 2], out["new_v_prompt"], out["new_v_sample"])):
                    sp.dma_start(big[0, 0, META:, h, :].rearrange("(i p) c -> p i c", p=P), src[:, 1:, :]).then_inc(kv_out[h % 2], 16)
                    sp.dma_start(big[0, 0, 0:META, h, :], src[0:META, 0, :]).then_inc(kv_out[h % 2], 16)
                    sp.dma_start(small[0, :, :, h, :].rearrange("b s c -> (b s) c"), src[META:FIRST, 0, :]).then_inc(kv_out[h % 2], 16)
                if h + 2 < HEADS:
                    weights(h + 2)
            for j in range(2):
                sp.wait_ge(kv_out[j], 96 * HEADS // 2)

        @block.tensor
        def _(pe):
            def product(h, i):
                bank_free(pe, ("z", h, i))
                pe.wait_ge(w_in[h % 2], 48 * (h // 2 + 1))
                for k in range(KC):
                    mm = pe.matmul(bank_of(("z", h, i))[:ROWS[i], 0:384], K["xT"][:, k, cols(i)], Wb[h % 2][:, k, :],
                                   start=(k == 0), stop=(k == KC - 1))
                mm.then_inc(projected, 1)

            def turn_qk(h, i):
                r, n = ROWS[i], NT * h + i
                pe.wait_ge(k_scaled, n + 1)
                bank_free(pe, ("x", h, i))
                bank = bank_of(("x", h, i))
                pe.transpose(bank[:, 0:r], zn[:r, n % 2, 0:P], K["ident"][:r, :r])
                pe.transpose(bank[:, P:P + r], kout[h % 2][:r, i, :], K["ident"][:r, :r]).then_inc(x_turned, 1)

            def scores(s, m):
                h, i = s // NQ, s % NQ
                r = P if i else META
                q = qz[h % 2][:, m, COL[i]:COL[i] + r]
                if m == 0:
                    pe.wait_ge(x_done, NT * h + i + 1)
                    if s:
                        pe.wait_ge(exp_done, 2 * s)
                n = P * i
                for c in range(0, n, 512):
                    w = min(512, n - c)
                    mm = pe.matmul(lg[m][:r, c:c + w], q, kT[h % 2][:, FIRST + c:FIRST + c + w], start=True, stop=True)
                if n < SEQ:
                    mm = pe.matmul(lg[m][:r, n:n + META], q, kT[h % 2][:, 0:META], start=True, stop=True)
                    mm.then_inc(logits, 1)
                elif m == 0:
                    mm.then_inc(logits, 1)

            def meta_scores(s):
                bank_free(pe, ("e", s, 0))
                h, i = s // NQ, s % NQ
                for m in range(2):
                    mm = pe.matmul(bank_of(("e", s, 0))[:, META * m:META * m + META], qz[h % 2][:, m, cols(i)],
                                   kT[h % 2][:, 0:META], start=True, stop=True)
                mm.then_inc(logits, 1)

            def turn_probabilities(s, g):
                i = s % NQ
                r = P if i else META
                pe.wait_ge(a_done, s + 1)
                bank_free(pe, ("a", s, g))
                for n in range(4 * g, min(4 * g + 4, i + 1)):
                    w = META if n == i else P
                    mm = pe.transpose(bank_of(("a", s, g))[:w, P * (n % 4):P * (n % 4) + r], Am[:r, P * n:P * n + w], K["ident"][:r, :r])
                mm.then_inc(a_turned, 1)

            def outputs(s):
                h, i = s // NQ, s % NQ
                r = P if i else META
                bank_free(pe, ("o", s, 0))
                last = a_index[("a", s, groups(s) - 1)]
                pe.wait_ge(a_act, last // 2 + 1)
                if last:
                    pe.wait_ge(a_dve, (last + 1) // 2)
                pe.wait_ge(squared, NT * h + i + 1)
                for n in range(i + 1):
                    w = META if n == i else P
                    mm = pe.matmul(bank_of(("o", s, 0))[:r, 0:P], aT[:w, n, :r], v[h % 2][:w, 0 if n == i else n + 1, :],
                                   start=(n == 0), stop=(n == i))
                mm.then_inc(o_done, 1)

            def turn_output(s):
                r = P if s % NQ else META
                pe.wait_ge(og_done, s + 1)
                bank_free(pe, ("g", s, 0))
                pe.transpose(bank_of(("g", s, 0))[:, 0:r], og[:r, s % 2, :], K["ident"][:r, :r]).then_inc(og_turned, 1)

            pe.wait_ge(bk_in, 16)
            pe.wait_ge(rel_ready, 1)
            for h in range(HEADS):
                pe.matmul(psum[:, h, 0:ND], relh[0:33, h, :], bucket[0:33], start=True, stop=True).then_inc(bias_made, 1)
            run = {"z": product, "x": turn_qk, "L": scores, "e": lambda s, _: meta_scores(s), "a": turn_probabilities,
                   "o": lambda s, _: outputs(s), "g": lambda s, _: turn_output(s)}
            for kind, a, b in zx:
                run[kind](a, b)
            pe.wait_ge(bias_row, HEADS)
            for slot in slots:
                for kind, a, b in slot:
                    run[kind](a, b)

        @block.scalar
        def _(act):
            def square(h, i):
                r, n = ROWS[i], NT * h + i
                bank = bank_of(("z", h, i))
                act.wait_ge(projected, n + 1)
                if n:
                    act.wait_ge(summed, n)
                if h >= 2:
                    act.wait_ge(o_done, NQ * (h - 1))
                    act.wait_ge(kv_out[h % 2], 96 * (h // 2))
                act.activation(v[h % 2][:r, i, :], bank[:r, 256:384], ACT.Copy)
                if i == 0:
                    act.activation(K["vS"][:r, h, :], bank[:r, 256:384], ACT.Copy)
                act.activation(sq[:r], bank[:r, 0:256], ACT.Square).then_inc(squared, 1)

            def place_qk(h, i):
                r, n = ROWS[i], NT * h + i
                bank = bank_of(("x", h, i))
                act.wait_ge(x_turned, n + 1)
                if n == 0:
                    act.wait_ge(setup, 3)
                if i == 0 and h >= 2:
                    act.wait_ge(saved, h - 1)
                for m in range(2):
                    rows = slice(64 * m, 64 * m + 64)
                    act.activation(qz[h % 2][rows, m, cols(i)], bank[rows, 0:r], ACT.Copy, scale=K["vecT"][rows, 18:19])
                act.activation(kT[h % 2][:, cols(i)], bank[:, P:P + r], ACT.Copy).then_inc(x_done, 1)

            def exps(s):
                i = s % NQ
                r = P if i else META
                n = min(P * i + META, SEQ)
                for m in range(2):
                    act.wait_ge(max_done, 2 * s + (2 if i == NQ - 1 else m + 1))
                    if m == 0 and s:
                        act.wait_ge(a_done, s)
                    if i == NQ - 1:
                        act.activation(Pm[:r, m, n:n + META], bank_of(("e", s, 0))[:r, META * m:META * m + META], ACT.Exp,
                                       bias=nmax[:r, s, m:m + 1], accum_out=sums[:r, s, 2 + m:3 + m])
                    act.activation(Pm[:r, m, 0:n], lg[m][:r, 0:n], ACT.Exp, bias=nmax[:r, s, m:m + 1],
                                   accum_out=sums[:r, s, m:m + 1]).then_inc(exp_done, 1)

            def copy_turned(s, g):
                n = a_index[("a", s, g)]
                if n % 2 == 0:
                    act.wait_ge(a_turned, n + 1)
                    if s:
                        act.wait_ge(o_done, s)
                    place_turned(lambda o, x: act.activation(o, x, ACT.Copy), s, g).then_inc(a_act, 1)

            def square_out(s):
                r = P if s % NQ else META
                act.wait_ge(o_done, s + 1)
                act.drain()
                act.activation(junk[:r], bank_of(("o", s, 0))[:r, 0:P], ACT.Square, scale=coef[:r, s, 2:3],
                               accum_out=ssq[:r, s:s + 1]).then_inc(ssq_done, 1)

            def place_out(s):
                i = s % NQ
                r = P if i else META
                act.wait_ge(og_turned, s + 1)
                act.activation(K["obT"][:, s // NQ, COL[i]:COL[i] + r], bank_of(("g", s, 0))[:, 0:r],
                               ACT.Copy, scale=K["vecT"][:, 17:18]).then_inc(ob_done, 1)

            for h in range(HEADS):
                act.wait_ge(bias_made, h + 1)
                act.activation(vecs[:, h, :], psum[:, h, 0:ND], ACT.Copy).then_inc(bias_row, 1)
            for kind, a, b in zx:
                (square if kind == "z" else place_qk)(a, b)
            for s, slot in enumerate(slots):
                for kind, a, b in slot:
                    if kind == "a":
                        copy_turned(a, b)
                if s < STEPS:
                    exps(s)
                for kind, a, b in slot:
                    if kind == "o":
                        square_out(a)
                    elif kind == "z":
                        square(a, b)
                    elif kind == "x":
                        place_qk(a, b)
                    elif kind == "g":
                        place_out(a)

        @block.gpsimd
        def _(pool):
            for h in range(2):
                pool.memset(qz[h].rearrange("p a b -> p (a b)"), 0.0).then_inc(setup, 1)
            pool.memset(K["Qs"].rearrange("p a b -> p (a b)"), 0.0).then_inc(setup, 1)
            pool.wait_ge(setup, 3)

            def power(n, h, i):
                r = ROWS[i]
                pool.wait_ge(summed, n + 1)
                pool.tensor_scalar(zs[:r, n, :], zs[:r, n, :], 1.0 / 64, EPS, ALU.mult, ALU.add)
                pool.drain()
                pool.tensor_tensor(zr[:r, n, :], zs[:r, n, :], K["half"][:r, 0:4], ALU.pow).then_inc(rstd_done, 1)

            def power_out(s):
                r = P if s % NQ else META
                pool.wait_ge(ssq_done, s + 1)
                pool.tensor_scalar(ssq[:r, s:s + 1], ssq[:r, s:s + 1], 1.0 / P, EPS, ALU.mult, ALU.add)
                pool.drain()
                pool.tensor_tensor(rr[:r, s, 0:1], ssq[:r, s:s + 1], K["half"][:r, 0:1], ALU.pow)
                pool.drain()
                pool.tensor_tensor(rr[:r, s, 1:2], rr[:r, s, 0:1], coef[:r, s, 2:3], ALU.mult).then_inc(orstd_done, 1)

            def save(h):
                pool.wait_ge(x_done, NT * h + 1)
                for m in range(2):
                    pool.tensor_copy(K["Qs"][:, DB * h:DB * h + DB, 16 * h + 8 * m:16 * h + 8 * m + 8],
                                     qz[h % 2][:, m, META:FIRST].rearrange("p (b s) -> p b s", s=DS))
                pool.tensor_copy(K["kS"][:, h, :], kT[h % 2][:, 0:FIRST]).then_inc(saved, 1)

            for kind, a, b in zx:
                if kind == "z":
                    power(NT * a + b, a, b)
            save(0)
            for s, slot in enumerate(slots):
                for kind, a, b in slot:
                    if kind == "o":
                        power_out(a)
                    elif kind == "z":
                        power(NT * a + b, a, b)
                    elif kind == "x" and b == 0:
                        save(a)

        @block.vector
        def _(dve):
            def sum_squares(h, i):
                r, n = ROWS[i], NT * h + i
                dve.wait_ge(squared, n + 1)
                dve.tensor_reduce(zs[:r, n, :], sq[:r].rearrange("p (g c) -> p g c", c=64), AX_X, ALU.add).then_inc(summed, 1)

            def normalise(h, i):
                r, n = ROWS[i], NT * h + i
                dve.wait_ge(rstd_done, n + 1)
                if n >= 2:
                    dve.wait_ge(x_turned, n - 1)
                if h >= 2:
                    dve.wait_ge(kv_out[h % 2], 96 * (h // 2))
                    dve.wait_ge(x_turned, NT * (h - 1))
                dve.tensor_tensor(zn[:r, n % 2, :].rearrange("p (g c) -> p g c", c=64),
                                  bank_of(("z", h, i))[:r, 0:256].rearrange("p (g c) -> p g c", c=64),
                                  zr[:r, n, :].unsqueeze(2).to_broadcast([r, 4, 64]), ALU.mult).then_inc(normed, 1)
                dve.drain()
                dve.tensor_tensor(kout[h % 2][:r, i, :].rearrange("p (m c) -> p m c", c=64),
                                  zn[:r, n % 2, P:2 * P].rearrange("p (m c) -> p m c", c=64),
                                  K["knorm"][:r].unsqueeze(1).to_broadcast([r, 2, 64]), ALU.mult).then_inc(k_scaled, 1)

            def maxima(s, m):
                h, i = s // NQ, s % NQ
                r = P if i else META
                dve.wait_ge(logits, 2 * s + 2 if i == NQ - 1 else 2 * s + m + 1)
                if s % NQ == 0 and m == 0:
                    dve.wait_ge(bias_in, 16 * HEADS)
                x = lg[m]
                if i == 0:
                    dve.tensor_tensor(x[:r, 0:META], x[:r, 0:META], Bn[h][:r, P:P + META], ALU.add)
                else:
                    lo = max(0, P * (i - 2))
                    w = P * i - lo
                    dve.tensor_tensor(x[:, lo:P * i], x[:, lo:P * i], Bn[h][:, 256 - w:256], ALU.add)
                if i == 1:
                    dve.tensor_tensor(x[:, P:P + META], x[:, P:P + META], Bn[h][:, P - META:P], ALU.add)
                dve.drain()
                if i == NQ - 1:
                    dve.tensor_reduce(mt[:, m, 0:1], x[:, 0:SEQ], AX_X, ALU.max, negate=True)
                    dve.tensor_reduce(mt[:, m, 1:2], bank_of(("e", s, 0))[:, META * m:META * m + META], AX_X, ALU.max, negate=True)
                    dve.drain()
                    dve.tensor_tensor(nmax[:, s, m:m + 1], mt[:, m, 0:1], mt[:, m, 1:2], ALU.min).then_inc(max_done, 1)
                else:
                    dve.tensor_reduce(nmax[:r, s, m:m + 1], x[:r, 0:P * i + META], AX_X, ALU.max, negate=True).then_inc(max_done, 1)

            def combine(s):
                i = s % NQ
                r, n = (P if i else META), P * i + META
                dve.wait_ge(exp_done, 2 * s + 2)
                if i == NQ - 1:
                    dve.tensor_tensor(sums[:, s, 0:2], sums[:, s, 0:2], sums[:, s, 2:4], ALU.add)
                    dve.drain()
                dve.reciprocal(coef[:r, s, 2:4], sums[:r, s, 0:2])
                dve.drain()
                dve.tensor_scalar(coef[:r, s, 0:1], sums[:r, s, 0:1], coef[:r, s, 3:4], K["lam"][:r, 3:4], ALU.mult, ALU.mult)
                dve.drain()
                if s:
                    dve.wait_ge(a_turned, a_index[("a", s - 1, groups(s - 1) - 1)] + 1)
                dve.scalar_tensor_tensor(Am[:r, 0:n], Pm[:r, 1, 0:n], coef[:r, s, 0:1], Pm[:r, 0, 0:n],
                                         ALU.mult, ALU.add).then_inc(a_done, 1)

            def scale_out(s):
                r = P if s % NQ else META
                dve.wait_ge(orstd_done, s + 1)
                if s >= 2:
                    dve.wait_ge(og_turned, s - 1)
                dve.tensor_scalar(og[:r, s % 2, :], bank_of(("o", s, 0))[:r, 0:P], rr[:r, s, 1:2], None, ALU.mult).then_inc(og_done, 1)

            def copy_turned(s, g):
                n = a_index[("a", s, g)]
                if n % 2:
                    dve.wait_ge(a_turned, n + 1)
                    if s:
                        dve.wait_ge(o_done, s)
                    place_turned(dve.tensor_copy, s, g).then_inc(a_dve, 1)

            dve.wait_ge(c_in, 32)
            dve.memset(rel[32:33], NEG)
            dve.tensor_tensor(rel[0:32], rel[0:32], rel31[0:32], ALU.subtract)
            dve.drain()
            dve.tensor_copy(relh[0:33], rel[0:33].unsqueeze(2).to_broadcast([33, HEADS, P])).then_inc(rel_ready, 1)
            for kind, a, b in zx:
                if kind == "z":
                    sum_squares(a, b)
                    normalise(a, b)
            for s, slot in enumerate(slots):
                for kind, a, b in slot:
                    if kind == "a":
                        copy_turned(a, b)
                if s < STEPS:
                    maxima(s, 0)
                    maxima(s, 1)
                    combine(s)
                if 1 <= s <= STEPS:
                    scale_out(s - 1)
                for kind, a, b in slot:
                    if kind == "z":
                        sum_squares(a, b)
                        normalise(a, b)


def phase_sample_attention(nc, A, K, sb, psum):
    PAIRS = DB // 2
    NK = PAST + FIRST
    kc, vc = (A[n][0].rearrange("n t h c -> (n t) (h c)") for n in ("cache_k", "cache_v"))
    with ExitStack() as st:
        st.enter_context(nc.cleanup_on_exit())
        sem = lambda n: nc.alloc_semaphore(name="sample_attention_" + n)
        table_in, bs_in, setup, bs_done, lamrow_done, pad_done = (sem(n) for n in ("table_in", "bs_in", "setup", "bs_done", "lamrow_done", "pad_done"))
        k_in = [[sem(f"k_in{b}{q}") for q in range(2)] for b in range(2)]
        v_in = [[sem(f"v_in{b}{q}") for q in range(2)] for b in range(2)]
        turned, t_act, t_dve, scored, max_done, exp_done, c_done, at_done, ats_done, atn_done, o_done, ssq_done, rstd_done, og_done, og_turned, ob_done = (
            sem(n) for n in ("turned", "t_act", "t_dve", "scored", "max_done", "exp_done", "c_done", "at_done", "ats_done", "atn_done", "o_done", "ssq_done", "rstd_done", "og_done", "og_turned", "ob_done"))
        table = sb(64).bitcast(I32)
        Kp = [sb(NPG, 512) for _ in range(2)]
        Vp = [[sb(NPG, 512) for _ in range(2)] for _ in range(2)]
        kTp = sb(2 * HEADS, 512)
        BS, BSn = sb(P + DS), sb(PAIRS, FIRST)
        Pr, C = sb(NK), sb(64)
        aTs, aTn = sb(NPG * 64 + 32), sb(64 + 32)
        lamrow, nmax, sums, rs = sb(2), sb(PAIRS), sb(PAIRS), sb(PAIRS)
        ssq, rr = sb(PAIRS, 2), sb(PAIRS, 2)
        junk, og = sb(P), sb(2, P)
        block = st.enter_context(nc.Block())
        logits = psum[:, 0:3, :].rearrange("p a b -> p (a b)")

        def page(e, b, j):
            r = e.value_load(table[0:1, NPG * b + j:NPG * b + j + 1], min_val=0, max_val=A["cache_k"].shape[1] - 1)
            return bass.ds(r * PAGE, PAGE)

        @block.sync
        def _(sp):
            sp.dma_start(table[0:1, :], A["page_table"].rearrange("a b -> (a b)").unsqueeze(0)).then_inc(table_in, 16)
            for b2 in range(2):
                for h in range(HEADS):
                    for m in range(2):
                        r0 = 64 * b2 + 16 * h + 8 * m
                        sp.dma_start(BS[r0:r0 + DS, :], K["skew"][h][P:P + DS * ND].rearrange("(p c) -> p c", c=ND)[:, 0:P + DS]).then_inc(bs_in, 16)
            sp.wait_ge(table_in, 16)

            for p in range(PAIRS):
                for b2 in range(2):
                    for j in range(NPG):
                        if p and j % 4 == 0:
                            sp.wait_ge(turned, 16 * (p - 1) + 8 * b2 + j + 4)
                        sp.dma_start(Kp[b2][:, j, :], kc[page(sp, 2 * p + b2, j), :]).then_inc(k_in[b2][j // 4], 16)

        @block.tensor
        def _(pe):
            def turn(g):
                pe.wait_ge(k_in[g // 2 % 2][g % 2], 64 * (g // 4 + 1))
                for n in range(4 * g, 4 * g + 4):
                    if n >= 2:
                        pe.wait_ge(t_dve if n % 2 else t_act, n // 2)
                    for h in range(HEADS):
                        mm = pe.transpose(psum[:, 3 + n % 2, P * h:P * h + P], Kp[g // 2 % 2][:, n % NPG, P * h:P * h + P], K["ident"])
                    mm.then_inc(turned, 1)

            def score(g):
                p, b2, half = g // 4, g // 2 % 2, g % 2
                pe.wait_ge(t_act, 2 * g + 2)
                pe.wait_ge(t_dve, 2 * g + 2)
                if p and b2 == 0 and half == 0:
                    pe.wait_ge(exp_done, p)
                for h in range(HEADS):
                    mm = pe.matmul(logits[64 * b2:64 * b2 + 64, 512 * half:512 * half + 512],
                                   K["Qs"][:, DB * h + 2 * p + b2, :], kTp[:, HEADS * half + h, :],
                                   start=(h == 0), stop=(h == HEADS - 1))
                if half == 1:
                    for h in range(HEADS):
                        mm = pe.matmul(logits[64 * b2:64 * b2 + 64, PAST:NK], K["Qs"][:, DB * h + 2 * p + b2, :],
                                       K["kS"][:, h, :], start=(h == 0), stop=(h == HEADS - 1))
                mm.then_inc(scored, 1)

            def turn_and_score(p):
                for g in range(4 * p, 4 * p + 4):
                    if g + 1 < 4 * PAIRS:
                        turn(g + 1)
                    score(g)

            def outputs(p):
                pe.wait_ge(c_done, p + 1)
                if p:
                    pe.wait_ge(ats_done, p)
                    pe.wait_ge(atn_done, p)
                for j in range(NPG):
                    pe.matmul(psum[:, 5, 64 * j:64 * j + 64], Pr[:, P * j:P * j + P], C, start=True, stop=True)
                pe.matmul(psum[0:FIRST, 6, 0:64], Pr[:, PAST:NK], C, start=True, stop=True).then_inc(at_done, 1)
                pe.wait_ge(ats_done, p + 1)
                pe.wait_ge(atn_done, p + 1)
                if p == 0:
                    pe.wait_ge(pad_done, 2)
                for b2 in range(2):
                    pe.wait_ge(v_in[p % 2][b2], 128 * (p // 2 + 1))
                    for j in range(NPG + 1):
                        for h in range(HEADS):
                            c = 32 * b2 + 8 * h
                            o = psum[32 * h:32 * h + 32, 7, P * b2:P * b2 + P]
                            if j < NPG:
                                pe.matmul(o, aTs[:, 64 * j + c:64 * j + c + 32], Vp[p % 2][b2][:, j, P * h:P * h + P],
                                          start=(j == 0), stop=False, skip_group_check=True)
                            else:
                                mm = pe.matmul(o, aTn[0:FIRST, c:c + 32], K["vS"][0:FIRST, h, :], start=False, stop=True,
                                               skip_group_check=True)
                mm.then_inc(o_done, 1)
                pe.wait_ge(og_done, p + 1)
                for b2 in range(2):
                    mm = pe.transpose(psum[:, 6, P + P * b2:2 * P + P * b2], og[:, b2, :], K["ident"])
                mm.then_inc(og_turned, 1)

            turn(0)
            turn_and_score(0)
            for p in range(PAIRS):
                if p + 1 < PAIRS:
                    turn_and_score(p + 1)
                outputs(p)

        def turned_by(p, engine):
            return range((16 * p + 4 if p else 0) + engine, min(16 * p + 20, 16 * PAIRS), 2)

        def place_turned(copy, n):
            half, j = n // 4 % 2, n % 4
            return copy(kTp[:, HEADS * half:HEADS * half + HEADS, P * j:P * j + P],
                        psum[:, 3 + n % 2, :].rearrange("p (h c) -> p h c", c=P))

        def turned_free(e, n):
            if n >= 8:
                e.wait_ge(scored, n // 4 - 1)

        @block.scalar
        def _(act):
            def pages(p):
                for n in turned_by(p, 0):
                    act.wait_ge(turned, n + 1)
                    turned_free(act, n)
                    place_turned(lambda o, x: act.activation(o, x, ACT.Copy), n).then_inc(t_act, 1)

            def exps(p):
                act.wait_ge(max_done, p + 1)
                if p:
                    act.wait_ge(at_done, p)
                act.activation(Pr, logits[:, 0:NK], ACT.Exp, bias=nmax[:, p:p + 1], accum_out=sums[:, p:p + 1]).then_inc(exp_done, 1)

            def rest(p):
                act.wait_ge(at_done, p + 1)
                if p:
                    act.wait_ge(o_done, p)
                act.activation(aTs[:, 0:NPG * 64], psum[:, 5, :], ACT.Copy).then_inc(ats_done, 1)
                act.wait_ge(o_done, p + 1)
                for b2 in range(2):
                    act.drain()
                    ins = act.activation(junk, psum[:, 7, P * b2:P * b2 + P], ACT.Square, accum_out=ssq[:, p, b2:b2 + 1])
                ins.then_inc(ssq_done, 1)
                act.wait_ge(og_turned, p + 1)
                for b2 in range(2):
                    c = META + DS * (2 * p + b2)
                    ins = act.activation(K["obT"][:, :, c:c + DS],
                                         psum[:, 6, P + P * b2:2 * P + P * b2].rearrange("p (h s) -> p h s", s=32)[:, :, 0:DS],
                                         ACT.Copy, scale=K["vecT"][:, 17:18])
                ins.then_inc(ob_done, 1)

            pages(0)
            for p in range(PAIRS):
                exps(p)
                if p + 1 < PAIRS:
                    pages(p + 1)
                rest(p)

        @block.gpsimd
        def _(pool):
            def values(p):
                for b2 in range(2):
                    for j in range(NPG):
                        pool.dma_start(Vp[p % 2][b2][:, j, :], vc[page(pool, 2 * p + b2, j), :]).then_inc(v_in[p % 2][b2], 16)

            pool.memset(BSn.rearrange("p a b -> p (a b)"), NEG).then_inc(setup, 1)
            pool.memset(aTs[:, NPG * 64:], 0.0).then_inc(pad_done, 1)
            pool.memset(aTn[:, 64:], 0.0).then_inc(pad_done, 1)
            pool.wait_ge(table_in, 16)
            values(0)
            values(1)
            for p in range(PAIRS):
                pool.wait_ge(ssq_done, p + 1)
                pool.tensor_scalar(ssq[:, p, :], ssq[:, p, :], 1.0 / P, EPS, ALU.mult, ALU.add)
                pool.drain()
                pool.tensor_tensor(rr[:, p, :], ssq[:, p, :], K["half"][:, 0:2], ALU.pow).then_inc(rstd_done, 1)
                if p + 2 < PAIRS:
                    pool.wait_ge(o_done, p + 1)
                    values(p + 2)

        @block.vector
        def _(dve):
            def pages(p):
                for n in turned_by(p, 1):
                    dve.wait_ge(turned, n + 1)
                    turned_free(dve, n)
                    place_turned(dve.tensor_copy, n).then_inc(t_dve, 1)

            def maxima(p):
                dve.wait_ge(scored, 4 * p + 4)
                near = logits[:, PAST - P:PAST]
                dve.tensor_tensor(near, near, BS[:, 0:P], ALU.add)
                dve.tensor_tensor(logits[:, PAST:NK], logits[:, PAST:NK], BSn[:, p, :], ALU.add)
                dve.drain()
                dve.tensor_reduce(nmax[:, p:p + 1], logits[:, 0:NK], AX_X, ALU.max, negate=True).then_inc(max_done, 1)

            def weights(p):
                dve.wait_ge(exp_done, p + 1)
                dve.reciprocal(rs[:, p:p + 1], sums[:, p:p + 1])
                dve.drain()
                if p:
                    dve.wait_ge(at_done, p)
                dve.tensor_scalar(C, K["combine"][:, 0:64], rs[:, p:p + 1], lamrow[:, 0:1], ALU.mult, ALU.mult).then_inc(c_done, 1)

            def rest(p):
                dve.wait_ge(at_done, p + 1)
                if p:
                    dve.wait_ge(o_done, p)
                dve.tensor_copy(aTn[0:FIRST, 0:64], psum[0:FIRST, 6, 0:64]).then_inc(atn_done, 1)
                dve.wait_ge(rstd_done, p + 1)
                if p:
                    dve.wait_ge(og_turned, p)
                for b2 in range(2):
                    ins = dve.tensor_scalar(og[:, b2, :], psum[:, 7, P * b2:P * b2 + P], rr[:, p, b2:b2 + 1], None, ALU.mult)
                ins.then_inc(og_done, 1)

            dve.tensor_scalar(lamrow[:, 1:2], K["combine"][:, 65:66], K["lam"][:, 3:4], None, ALU.mult)
            dve.wait_ge(bs_in, 16 * 16)
            dve.wait_ge(setup, 1)
            dve.drain()
            dve.tensor_tensor(lamrow[:, 0:1], K["combine"][:, 64:65], lamrow[:, 1:2], ALU.subtract)
            for p in range(PAIRS):
                for b2 in range(2):
                    c = META + DS * (2 * p + b2)
                    dve.tensor_copy(BSn[64 * b2:64 * b2 + 64, p, c:c + DS], BS[64 * b2:64 * b2 + 64, P:P + DS])
            dve.drain()
            pages(0)
            for p in range(PAIRS):
                maxima(p)
                weights(p)
                if p + 1 < PAIRS:
                    pages(p + 1)
                rest(p)


def phase_merge(nc, A, K, sb, psum):
    W = A["w_in"][0].rearrange("(k p) n -> p k n", p=P)
    WA, WB = (A[n][0].rearrange("(k p) n -> p k n", p=P) for n in ("w_hg_out", "w_da_out"))
    UNITS = KC * 3
    with ExitStack() as st:
        st.enter_context(nc.cleanup_on_exit())
        sem = lambda n: nc.alloc_semaphore(name="merge_" + n)
        w_in = [sem("w_in0"), sem("w_in1")]
        produced, gated, merged = sem("produced"), sem("gated"), sem("merged")
        Wg = [sb(KC, 256) for _ in range(2)]
        Wy = [sb(HEADS, 256) for _ in range(2)]
        g = [sb(2, CH) for _ in range(2)]
        block = st.enter_context(nc.Block())

        @block.sync
        def _(sp):
            for c in range(KC):
                if c >= 2:
                    sp.wait_ge(produced, 3 * (c - 1))
                for j, (src, base) in enumerate(((W, GA), (W, GB), (WA, 0), (WB, 0))):
                    dst = (Wg if j < 2 else Wy)[c % 2][:, :, P * (j % 2):P * (j % 2) + P]
                    sp.dma_start(dst, src[:, :, base + P * c:base + P * c + P]).then_inc(w_in[c % 2], 16)

        @block.tensor
        def _(pe):
            for u in range(UNITS):
                c, n = u // 3, slice(CH * (u % 3), CH * (u % 3) + CH)
                banks = [psum[:, 4 * (u % 2) + j, 0:CH] for j in range(4)]
                if n.start == 0:
                    pe.wait_ge(w_in[c % 2], 64 * (c // 2 + 1))
                if u >= 2:
                    pe.wait_ge(merged, u - 1)
                for j in range(2):
                    for k in range(KC):
                        pe.matmul(banks[j], Wg[c % 2][:, k, P * j:P * j + P], K["xT"][:, k, n], start=(k == 0), stop=(k == KC - 1))
                for j, src in enumerate((K["oaT"], K["obT"])):
                    for k in range(HEADS):
                        mm = pe.matmul(banks[2 + j], Wy[c % 2][:, k, P * j:P * j + P], src[:, k, n], start=(k == 0), stop=(k == HEADS - 1))
                mm.then_inc(produced, 1)

        @block.scalar
        def _(act):
            for u in range(UNITS):
                act.wait_ge(produced, u + 1)
                if u >= 2:
                    act.wait_ge(merged, u - 1)
                for j in range(2):
                    ins = act.activation(g[u % 2][:, j, :], psum[:, 4 * (u % 2) + j, 0:CH], ACT.Sigmoid)
                ins.then_inc(gated, 1)

        @block.vector
        def _(dve):
            for u in range(UNITS):
                b = g[u % 2]
                dve.wait_ge(gated, u + 1)
                for j in range(2):
                    dve.tensor_tensor(b[:, j, :], b[:, j, :], psum[:, 4 * (u % 2) + 2 + j, 0:CH], ALU.mult)
                dve.drain()
                dve.tensor_tensor(K["mT"][:, u // 3, CH * (u % 3):CH * (u % 3) + CH], b[:, 0, :], b[:, 1, :], ALU.add).then_inc(merged, 1)


def phase_output(nc, A, K, sb, psum):
    with ExitStack() as st:
        st.enter_context(nc.cleanup_on_exit())
        sem = lambda n: nc.alloc_semaphore(name="output_" + n)
        w_in, wr_in, setup = sem("w_in"), sem("wr_in"), sem("setup")
        x_in = [sem("x_in0"), sem("x_in1")]
        h_made, h_done, ssq_done, rstd_done, scaled, hn_done, turned, t_done, routed, r_done = (
            sem(n) for n in ("h_made", "h_done", "ssq_done", "rstd_done", "scaled", "hn_done", "turned", "t_done", "routed", "r_done"))
        hn_out = [sem("hn_out0"), sem("hn_out1")]
        Wo, wr = sb(KC, D), sb(KC, P)
        w2, x, hs, hn = sb(D), sb(2, D), sb(D), sb(2, D)
        hT = sb(KC, P)
        ssq, rstd, junk = sb(NT), sb(NT), sb(D)
        block = st.enter_context(nc.Block())

        @block.sync
        def _(sp):
            for k in range(2):
                sp.dma_start(Wo[:, 4 * k:4 * k + 4, :], A["w_o"][0].rearrange("(k p) n -> p k n", p=P)[:, 4 * k:4 * k + 4, :]).then_inc(w_in, 16)
            sp.wait_ge(setup, 1)
            sp.dma_start(wr[:, :, 0:4], A["w_router_group"][0].rearrange("(k p) n -> p k n", p=P)).then_inc(wr_in, 16)
            sp.dma_start(wr[:, :, 4:20], A["w_router_expert"][0].rearrange("(k p) n -> p k n", p=P)).then_inc(wr_in, 16)
            sp.dma_start(w2, A["norm2_w"].to_broadcast([P, D])).then_inc(wr_in, 16)
            for i in range(NT):
                if i >= 2:
                    sp.wait_ge(h_done, i - 1)
                if i == 0:
                    sp.dma_start(x[0:META, 0, :], A["meta_tokens"]).then_inc(x_in[0], 16)
                    sp.dma_start(x[META:FIRST, 0, :], A["x_sample"].rearrange("a b d -> (a b) d")).then_inc(x_in[0], 16)
                else:
                    sp.dma_start(x[:, i % 2, :], A["x_prompt"][0, P * (i - 1):P * i, :]).then_inc(x_in[i % 2], 16)
                if i >= 1:
                    j = i - 1
                    sp.wait_ge(hn_done, j + 1)
                    sp.dma_start(K["hn_dram"][cols(j), :], hn[:ROWS[j], j % 2, :]).then_inc(hn_out[j % 2], 16)
            j = NT - 1
            sp.wait_ge(hn_done, j + 1)
            sp.dma_start(K["hn_dram"][cols(j), :], hn[:, j % 2, :]).then_inc(hn_out[j % 2], 16)
            for q in range(2):
                sp.wait_ge(hn_out[q], 16 * (5 - q))

        @block.tensor
        def _(pe):
            def project(i):
                r = ROWS[i]
                if i >= 2:
                    pe.wait_ge(h_done, i - 1)
                for j in range(2):
                    for k in range(KC):
                        mm = pe.matmul(psum[:r, 2 * (i % 2) + j, :], K["mT"][:, k, cols(i)], Wo[:, k, 512 * j:512 * j + 512],
                                       start=(k == 0), stop=(k == KC - 1))
                mm.then_inc(h_made, 1)

            def turn(i):
                r = ROWS[i]
                pe.wait_ge(hn_done, i + 1)
                if i:
                    pe.wait_ge(t_done, i)
                for k in range(KC):
                    mm = pe.transpose(psum[:, 4 + k // 4, P * (k % 4):P * (k % 4) + r], hn[:r, i % 2, P * k:P * k + P], K["ident"][:r, :r])
                mm.then_inc(turned, 1)

            def route(i):
                r = ROWS[i]
                pe.wait_ge(t_done, i + 1)
                if i:
                    pe.wait_ge(r_done, i)
                for k in range(KC):
                    mm = pe.matmul(psum[:r, 6, 0:P], hT[:, k, :r], wr[:, k, :], start=(k == 0), stop=(k == KC - 1))
                mm.then_inc(routed, 1)

            pe.wait_ge(w_in, 32)
            pe.wait_ge(wr_in, 48)
            for i in range(NT + 2):
                if i < NT:
                    project(i)
                if i >= 2:
                    route(i - 2)
                if 1 <= i <= NT:
                    turn(i - 1)

        @block.scalar
        def _(act):
            def norm(i):
                r = ROWS[i]
                act.wait_ge(h_done, i + 1)
                act.drain()
                act.activation(junk[:r], K["h"][:r, i, :], ACT.Square, accum_out=ssq[:r, i:i + 1]).then_inc(ssq_done, 1)
                act.wait_ge(rstd_done, i + 1)
                if i:
                    act.wait_ge(hn_done, i)
                act.activation(hs[:r], K["h"][:r, i, :], ACT.Copy, scale=rstd[:r, i:i + 1]).then_inc(scaled, 1)

            def place(i):
                act.wait_ge(turned, i + 1)
                if i:
                    act.wait_ge(routed, i)
                act.activation(hT[:, :, :ROWS[i]], psum[:, 4:6, :].rearrange("p a (b c) -> p (a b) c", c=P)[:, :, :ROWS[i]], ACT.Copy).then_inc(t_done, 1)

            for i in range(NT + 1):
                if i < NT:
                    norm(i)
                if i >= 1:
                    place(i - 1)

        @block.gpsimd
        def _(pool):
            pool.memset(wr.rearrange("p a b -> p (a b)"), 0.0).then_inc(setup, 1)
            for i in range(NT):
                r = ROWS[i]
                pool.wait_ge(ssq_done, i + 1)
                pool.tensor_scalar(ssq[:r, i:i + 1], ssq[:r, i:i + 1], 1.0 / D, EPS, ALU.mult, ALU.add)
                pool.drain()
                pool.tensor_tensor(rstd[:r, i:i + 1], ssq[:r, i:i + 1], K["half"][:r, 0:1], ALU.pow).then_inc(rstd_done, 1)

        @block.vector
        def _(dve):
            dve.memset(K["logit"].rearrange("p a b -> p (a b)"), 0.0)
            dve.wait_ge(wr_in, 48)
            for i in range(NT + 2):
                if i < NT:
                    r = ROWS[i]
                    dve.wait_ge(h_made, i + 1)
                    dve.wait_ge(x_in[i % 2], 32 if i == 0 else 16 * (i // 2 + (2 if i % 2 == 0 else 1)))
                    dve.tensor_tensor(K["h"][:r, i, :], psum[:r, 2 * (i % 2):2 * (i % 2) + 2, :].rearrange("p a b -> p (a b)"),
                                      x[:r, i % 2, :], ALU.add).then_inc(h_done, 1)
                if 1 <= i <= NT:
                    j = i - 1
                    r = ROWS[j]
                    dve.wait_ge(scaled, j + 1)
                    if j >= 2:
                        dve.wait_ge(turned, j - 1)
                        dve.wait_ge(hn_out[j % 2], 16 * (j // 2))
                    dve.tensor_tensor(hn[:r, j % 2, :], hs[:r], w2[:r], ALU.mult).then_inc(hn_done, 1)
                if i >= 2:
                    j = i - 2
                    dve.wait_ge(routed, j + 1)
                    dve.tensor_copy(K["logit"][:ROWS[j], j, :], psum[:ROWS[j], 6, 0:20]).then_inc(r_done, 1)


def phase_route(nc, A, K, sb, psum):
    G, PE_ = 4, 4
    with ExitStack() as st:
        st.enter_context(nc.cleanup_on_exit())
        sem = lambda n: nc.alloc_semaphore(name="route_" + n)
        c_in, setup, exp_in, exp_out, counted, prefixed, slots_done, zeroed, scattered, table_in, t_turned, experts_done, chosen = (sem(n) for n in (
            "c_in", "setup", "exp_in", "exp_out", "counted", "prefixed", "slots_done", "zeroed", "scattered", "table_in", "t_turned", "experts_done", "chosen"))
        bias, consts, strict, ones, tok, valid, emask = sb(20), sb(53), sb(P), sb(P), sb(NT), sb(NT), sb(E, NT)
        t4, gm, eg, gs = sb(NT, G), sb(NT), sb(NT, G), sb(NT)
        ohg, es16, es, e2 = sb(NT, G), sb(NT, 16), sb(NT, PE_), sb(NT, PE_)
        oh = [sb(NT, PE_) for _ in range(2)]
        mx, tm = sb(2, NT), sb(NT)
        OH = [sb(NT, E) for _ in range(2)]
        M, pre, tot = sb(NT, E), sb(NT, E), sb(E, NT)
        inc, cmp9, ntile, incl, excl, sm, sl = sb(E, NT), sb(E, NT), sb(E), sb(E), sb(E), sb(NT, E), sb(NT)
        lt, eid, eidb, step, zero = sb(SLOTS, E), sb(SLOTS), sb(SLOTS), sb(SLOTS), sb(P)
        rows = sb(P)
        block = st.enter_context(nc.Block())
        pri, steps128, jj = consts[:, 0:4], consts[:, 4:13], consts[:, 13:13 + SLOTS]

        @block.sync
        def _(sp):
            sp.dma_start(bias[:, 0:4], A["b_router_group"].to_broadcast([P, 4])).then_inc(c_in, 16)
            sp.dma_start(bias[:, 4:20], A["b_router_expert"].to_broadcast([P, 16])).then_inc(c_in, 16)
            for dst, n in ((consts, "experts"), (strict, "strict"), (tok, "token_id"), (valid, "valid"), (emask.rearrange("p a b -> p (a b)"), "expert_mask")):
                sp.dma_start(dst, A[n]).then_inc(c_in, 16)
            for e in range(BUFFERS):
                load_expert(sp, A, K, e, e)
            sp.wait_ge(setup, 1)
            sp.dma_start(K["slot_token"].rearrange("(a b) c -> a (b c)", b=P), zero[0:SLOTS, :]).then_inc(zeroed, 16)
            sp.wait_ge(scattered, 2 * 16 * NT)
            sp.dma_start(rows[0:SLOTS, :], K["slot_token"].rearrange("(a b) c -> a (b c)", b=P)).then_inc(table_in, 16)
            sp.wait_ge(table_in, 16)

        @block.gpsimd
        def _(pool):
            pool.wait_ge(c_in, 16 * 7)
            pool.wait_ge(zeroed, 16)
            pool.wait_ge(slots_done, 1)
            for i in range(NT):
                for j in range(2):
                    pool.indirect_dma_start(out=K["slot_token"], out_offset=bass.IndirectOffsetOnAxis(ap=K["slot"][:ROWS[i], NT * j + i:NT * j + i + 1], axis=0),
                                            in_=tok[:ROWS[i], i:i + 1], in_offset=None).then_inc(scattered, 16)

        @block.scalar
        def _(act):
            act.wait_ge(exp_in, 1)
            act.activation(eg, eg, ACT.Exp).then_inc(exp_out, 1)
            act.wait_ge(exp_in, 2)
            act.activation(tm, tm, ACT.Exp).then_inc(exp_out, 1)

        @block.tensor
        def _(pe):
            pe.wait_ge(counted, 1)
            m = M.rearrange("p a b -> p (a b)")
            pe.matmul(psum[:, 0, 0:NT * E], strict, m, start=True, stop=True)
            pe.matmul(psum[:, 1, 0:NT * E], ones, m, start=True, stop=True).then_inc(prefixed, 1)
            pe.wait_ge(table_in, 16)
            pe.transpose(psum[:, 2, 0:SLOTS], rows[0:SLOTS, :], K["ident"][0:SLOTS, 0:SLOTS]).then_inc(t_turned, 1)

        @block.vector
        def _(dve):
            D_ = dve.drain
            dve.memset(zero, 0.0).then_inc(setup, 1)
            dve.memset(ones, 1.0)
            dve.wait_ge(c_in, 16 * 7)
            L = K["logit"]
            dve.tensor_tensor(L, L, bias.unsqueeze(1).to_broadcast([P, NT, 20]), ALU.add)
            D_()

            def first_of(dst, x, m, n):
                dve.tensor_tensor(dst, x, m.unsqueeze(2).to_broadcast([P, NT, n]), ALU.is_equal)
                D_()
                dve.tensor_tensor(dst, dst, pri.unsqueeze(1).to_broadcast([P, NT, n]), ALU.mult)
                D_()
                dve.tensor_reduce(gs, dst, AX_X, ALU.max)
                D_()
                dve.tensor_tensor(dst, dst, gs.unsqueeze(2).to_broadcast([P, NT, n]), ALU.is_equal)
                D_()

            gl = L[:, :, 0:4]
            dve.tensor_reduce(gm, gl, AX_X, ALU.max)
            D_()
            dve.tensor_tensor(eg, gl, gm.unsqueeze(2).to_broadcast([P, NT, G]), ALU.subtract).then_inc(exp_in, 1)
            first_of(ohg, gl, gm, G)
            dve.tensor_tensor(es16.rearrange("p n (g e) -> p n g e", g=G), L[:, :, 4:20].rearrange("p n (g e) -> p n g e", g=G),
                              ohg.unsqueeze(3).to_broadcast([P, NT, G, PE_]), ALU.mult)
            D_()
            dve.tensor_reduce(es, es16.rearrange("p n (g e) -> p n e g", g=G), AX_X, ALU.add)
            D_()
            dve.tensor_reduce(mx[:, 0, :], es, AX_X, ALU.max)
            D_()
            first_of(oh[0], es, mx[:, 0, :], PE_)
            dve.scalar_tensor_tensor(e2, oh[0], NEG, es, ALU.mult, ALU.add)
            D_()
            dve.tensor_reduce(mx[:, 1, :], e2, AX_X, ALU.max)
            D_()
            first_of(oh[1], e2, mx[:, 1, :], PE_)
            dve.tensor_tensor(tm, mx[:, 1, :], mx[:, 0, :], ALU.subtract).then_inc(exp_in, 1)
            dve.tensor_tensor(ohg, ohg, valid.unsqueeze(2).to_broadcast([P, NT, G]), ALU.mult)
            D_()
            for j in range(2):
                dve.tensor_tensor(OH[j].rearrange("p n (g e) -> p n g e", g=G), ohg.unsqueeze(3).to_broadcast([P, NT, G, PE_]),
                                  oh[j].unsqueeze(2).to_broadcast([P, NT, G, PE_]), ALU.mult)
            D_()
            dve.tensor_tensor(M, OH[0], OH[1], ALU.add).then_inc(counted, 1)
            dve.wait_ge(exp_out, 2)
            dve.tensor_reduce(gs, eg, AX_X, ALU.add)
            D_()
            dve.tensor_scalar(gm, tm, 1.0, None, ALU.add)
            D_()
            dve.tensor_tensor(gm, gm, gs, ALU.mult)
            D_()
            dve.reciprocal(K["weight"][:, 0, :], gm)
            D_()
            dve.tensor_tensor(K["weight"][:, 1, :], K["weight"][:, 0, :], tm, ALU.mult)
            dve.wait_ge(prefixed, 1)
            dve.tensor_copy(tot, psum[:, 1, 0:NT * E].rearrange("p (n e) -> p e n", e=E))
            D_()
            flat = lambda x: x.rearrange("p a b -> p (a b)")
            dve.tensor_tensor_scan(flat(inc), flat(emask), flat(tot), 0.0, ALU.mult, ALU.add)
            D_()
            dve.tensor_tensor(cmp9, inc[:, :, NT - 1:NT].to_broadcast([P, E, NT]), steps128.unsqueeze(1).to_broadcast([P, E, NT]), ALU.is_gt)
            D_()
            dve.tensor_reduce(ntile, cmp9, AX_X, ALU.add)
            D_()
            dve.tensor_tensor_scan(incl, ones[:, 0:E], ntile, 0.0, ALU.mult, ALU.add)
            dve.tensor_tensor(inc, inc, tot, ALU.subtract)
            D_()
            dve.tensor_tensor(excl, incl, ntile, ALU.subtract)
            dve.tensor_tensor(sm, psum[:, 0, 0:NT * E].rearrange("p (n e) -> p n e", e=E), inc.rearrange("p e n -> p n e"), ALU.add)
            D_()
            dve.tensor_scalar(excl, excl, float(P), None, ALU.mult)
            D_()
            dve.tensor_tensor(sm, sm, excl.unsqueeze(1).to_broadcast([P, NT, E]), ALU.add)
            D_()
            for j in range(2):
                dve.tensor_tensor(OH[j], OH[j], sm, ALU.mult)
                D_()
                dve.tensor_reduce(sl, OH[j], AX_X, ALU.add)
                D_()
                ins = dve.tensor_copy(K["slot"][:, NT * j:NT * j + NT], sl)
                D_()
            ins.then_inc(slots_done, 1)
            dve.tensor_tensor(lt, incl.unsqueeze(1).to_broadcast([P, SLOTS, E]), jj.unsqueeze(2).to_broadcast([P, SLOTS, E]), ALU.is_le)
            D_()
            dve.tensor_reduce(eid, lt, AX_X, ALU.add)
            D_()
            dve.tensor_scalar(eid, eid, float(E - 1), None, ALU.min)
            D_()
            dve.tensor_copy(K["expert"], eid)
            dve.tensor_copy(K["ends"], incl)
            dve.tensor_copy(eidb, eid)
            D_()
            for n in range(BUFFERS, E, BUFFERS):
                dve.tensor_scalar(step, eid, float(n), -float(BUFFERS), ALU.is_ge, ALU.mult)
                D_()
                dve.tensor_tensor(eidb, eidb, step, ALU.add)
                D_()
            dve.tensor_copy(K["buffer"], eidb)
            dve.wait_ge(t_turned, 1)
            dve.tensor_copy(K["token"], psum[:, 2, 0:SLOTS])


def load_expert(sp, A, K, e, b):
    for c, n in enumerate(("w_gate", "w_up")):
        sp.dma_start(K["GU"][:, KC * b:KC * b + KC, FF * c:FF * c + FF], A[n][0, e].rearrange("(k p) n -> p k n", p=P)).then_inc(K["w_in"][b], 16)
    sp.dma_start(K["Wd"][:, 2 * b:2 * b + 2, :], A["w_down"][0, e].rearrange("(k p) n -> p k n", p=P)).then_inc(K["w_in"][b], 16)


def phase_experts(nc, A, K, sb, psum):
    with ExitStack() as st:
        st.enter_context(nc.cleanup_on_exit())
        sem = lambda n: nc.alloc_semaphore(name="experts_" + n)
        pair = lambda n: [sem(n + "0"), sem(n + "1")]
        x_in, y_out = pair("x_in"), pair("y_out")
        weights_ready = sem("weights_ready")
        turned, xt_done, gu_done, silu_done, h_done, h_turned, ht_done, y_made, y_act, y_dve = (
            sem(n) for n in ("turned", "xt_done", "gu_done", "silu_done", "h_done", "h_turned", "ht_done", "y_made", "y_act", "y_dve"))
        X, XT = [sb(D) for _ in range(2)], [sb(KC, P) for _ in range(2)]
        hg, hT, Y = [sb(FF) for _ in range(2)], [sb(2, P) for _ in range(2)], [sb(D) for _ in range(2)]
        block = st.enter_context(nc.Block())
        PAIRS = SLOTS // 2

        @block.sync
        def _(sp):
            for e in range(E):
                if e >= BUFFERS:
                    ends = sp.value_load(K["ends"][0:1, e - BUFFERS:e - BUFFERS + 1], min_val=0, max_val=SLOTS)
                    sp.wait_ge(y_made, ends + 1)
                    load_expert(sp, A, K, e, e % BUFFERS)
                if e >= BUFFERS - 2:
                    n = e - BUFFERS + 2
                    sp.wait_ge(K["w_in"][n % BUFFERS], 48 * (n // BUFFERS + 1))
                    sp.sem_inc(weights_ready, 1)
            for n in range(E - BUFFERS + 2, E):
                sp.wait_ge(K["w_in"][n % BUFFERS], 48 * (n // BUFFERS + 1))
                sp.sem_inc(weights_ready, 1)

        @block.gpsimd
        def _(pool):
            def gather(j, par):
                pool.indirect_dma_start(out=X[par], out_offset=None, in_=K["hn_dram"],
                                        in_offset=bass.IndirectOffsetOnAxis(ap=K["token"][:, j:j + 1], axis=0)).then_inc(x_in[par], 16)

            def store(j, par):
                pool.wait_ge(y_act, j + 1)
                pool.wait_ge(y_dve, j + 1)
                pool.dma_start(K["y_dram"][P * j:P * j + P, :], Y[par]).then_inc(y_out[par], 16)

            for j in range(2):
                gather(j, j)
            for j in range(2, SLOTS):
                pool.wait_ge(turned, j - 1)
                gather(j, j % 2)
                if j >= 3:
                    store(j - 3, (j - 3) % 2)
            for j in range(SLOTS - 3, SLOTS):
                store(j, j % 2)
            for par in range(2):
                pool.wait_ge(y_out[par], 16 * PAIRS)

        @block.tensor
        def _(pe):
            def buffer_of(j):
                return pe.value_load(K["buffer"][0:1, bass.ds(j, 1)], min_val=0, max_val=BUFFERS - 1)

            def turn_hidden(j, par):
                pe.wait_ge(h_done, j + 1)
                for k in range(2):
                    mm = pe.transpose(psum[:, 4, P * k:P * k + P], hg[par][:, P * k:P * k + P], K["ident"])
                mm.then_inc(h_turned, 1)

            def down(j, par, first, b):
                pe.wait_ge(ht_done, j + 1)
                if not first:
                    pe.wait_ge(y_act, j)
                    pe.wait_ge(y_dve, j)
                for n in range(2):
                    for k in range(2):
                        mm = pe.matmul(psum[:, 5 + n, :], hT[par][:, k, :], K["Wd"][:, bass.ds(2 * b + k, 1), 512 * n:512 * n + 512], start=(k == 0), stop=(k == 1))
                mm.then_inc(y_made, 1)

            def step(i, par, first):
                j = 2 * i + par
                before = not (first and par == 0)
                e = pe.value_load(K["expert"][0:1, bass.ds(j, 1)], min_val=0, max_val=E - 1)
                b = buffer_of(j)
                if before:
                    last = buffer_of(j - 1)
                    pe.wait_ge(xt_done, j)
                pe.wait_ge(x_in[par], 16 * i + 16)
                for k in range(KC):
                    mm = pe.transpose(psum[:, k // 4, P * (k % 4):P * (k % 4) + P], X[par][:, P * k:P * k + P], K["ident"])
                mm.then_inc(turned, 1)
                if before:
                    turn_hidden(j - 1, 1 - par)
                pe.wait_ge(xt_done, j + 1)
                pe.wait_ge(weights_ready, e + 1)
                for k in range(KC):
                    mm = pe.matmul(psum[:, 2 + par, :], XT[par][:, k, :], K["GU"][:, bass.ds(KC * b + k, 1), :], start=(k == 0), stop=(k == KC - 1))
                mm.then_inc(gu_done, 1)
                if before:
                    down(j - 1, 1 - par, first, last)

            pe.sem_inc(y_made, 1)
            for par in range(2):
                step(0, par, True)
            with pe.Fori(1, PAIRS) as i:
                for par in range(2):
                    step(i, par, False)
            last = buffer_of(SLOTS - 1)
            turn_hidden(SLOTS - 1, 1)
            down(SLOTS - 1, 1, False, last)

        @block.scalar
        def _(act):
            def silu(j, par):
                act.wait_ge(gu_done, j + 1)
                act.activation(hg[par], psum[:, 2 + par, 0:FF], ACT.Silu).then_inc(silu_done, 1)

            def result(j, par, i):
                act.wait_ge(y_made, j + 2)
                if i is not None:
                    act.wait_ge(y_out[par], 16 * i)
                act.activation(Y[par][:, 0:512], psum[:, 5, :], ACT.Copy).then_inc(y_act, 1)

            def hidden(j, par):
                act.wait_ge(h_turned, j + 1)
                act.activation(hT[par].rearrange("p a b -> p (a b)"), psum[:, 4, 0:2 * P], ACT.Copy).then_inc(ht_done, 1)

            silu(0, 0)
            hidden(0, 0)
            silu(1, 1)
            result(0, 0, None)
            hidden(1, 1)
            silu(2, 0)
            result(1, 1, None)
            hidden(2, 0)
            with act.Fori(1, PAIRS - 1) as i:
                silu(2 * i + 1, 1)
                result(2 * i, 0, i)
                hidden(2 * i + 1, 1)
                silu(2 * i + 2, 0)
                result(2 * i + 1, 1, i)
                hidden(2 * i + 2, 0)
            silu(SLOTS - 1, 1)
            result(SLOTS - 2, 0, PAIRS - 1)
            hidden(SLOTS - 1, 1)
            result(SLOTS - 1, 1, PAIRS - 1)

        @block.vector
        def _(dve):
            def place(j, par, first):
                dve.wait_ge(turned, j + 1)
                if not first:
                    dve.wait_ge(gu_done, j - 1)
                dve.tensor_copy(XT[par].rearrange("p a b -> p (a b)"), psum[:, 0:2, :].rearrange("p a b -> p (a b)")).then_inc(xt_done, 1)

            def hidden(j, par):
                dve.wait_ge(silu_done, j + 1)
                dve.tensor_tensor(hg[par], hg[par], psum[:, 2 + par, FF:2 * FF], ALU.mult).then_inc(h_done, 1)

            def result(j, par, i):
                dve.wait_ge(y_made, j + 2)
                if i is not None:
                    dve.wait_ge(y_out[par], 16 * i)
                dve.tensor_copy(Y[par][:, 512:], psum[:, 6, :]).then_inc(y_dve, 1)

            place(0, 0, True)
            hidden(0, 0)
            place(1, 1, True)
            hidden(1, 1)
            result(0, 0, None)
            place(2, 0, False)
            hidden(2, 0)
            result(1, 1, None)
            place(3, 1, False)
            with dve.Fori(1, PAIRS - 1) as i:
                hidden(2 * i + 1, 1)
                result(2 * i, 0, i)
                place(2 * i + 2, 0, False)
                hidden(2 * i + 2, 0)
                result(2 * i + 1, 1, i)
                place(2 * i + 3, 1, False)
            hidden(SLOTS - 1, 1)
            result(SLOTS - 2, 0, PAIRS - 1)
            result(SLOTS - 1, 1, PAIRS - 1)


def phase_combine(nc, A, K, out, sb, psum):
    with ExitStack() as st:
        st.enter_context(nc.cleanup_on_exit())
        sem = lambda n: nc.alloc_semaphore(name="combine_" + n)
        y_in, y_out = [sem("y_in0"), sem("y_in1")], [sem("y_out0"), sem("y_out1")]
        halfway, summed = sem("halfway"), sem("summed")
        Y, O = [sb(2, D) for _ in range(2)], [sb(D) for _ in range(2)]
        block = st.enter_context(nc.Block())

        @block.gpsimd
        def _(pool):
            for i in range(NT):
                if i >= 2:
                    pool.wait_ge(summed, i - 1)
                for j in range(2):
                    pool.indirect_dma_start(out=Y[i % 2][:ROWS[i], j, :], out_offset=None, in_=K["y_dram"],
                                            in_offset=bass.IndirectOffsetOnAxis(ap=K["slot"][:ROWS[i], NT * j + i:NT * j + i + 1], axis=0)).then_inc(y_in[i % 2], 16)

        @block.vector
        def _(dve):
            for i in range(NT):
                r, q = ROWS[i], i % 2
                dve.wait_ge(y_in[q], 32 * (i // 2 + 1))
                if i >= 2:
                    dve.wait_ge(y_out[q], 16 * (i // 2))
                dve.scalar_tensor_tensor(O[q][:r], Y[q][:r, 0, :], K["weight"][:r, 0, i:i + 1], K["h"][:r, i, :], ALU.mult, ALU.add)
                dve.drain()
                dve.scalar_tensor_tensor(O[q][:r], Y[q][:r, 1, :], K["weight"][:r, 1, i:i + 1], O[q][:r], ALU.mult, ALU.add).then_inc(summed, 1)

        @block.sync
        def _(sp):
            for i in range(NT):
                sp.wait_ge(summed, i + 1)
                if i == 0:
                    sp.dma_start(out["y_sample"].rearrange("a b d -> (a b) d"), O[0][META:FIRST]).then_inc(y_out[0], 16)
                else:
                    sp.dma_start(out["y_prompt"][0, P * (i - 1):P * i, :], O[i % 2]).then_inc(y_out[i % 2], 16)
            for q in range(2):
                sp.wait_ge(y_out[q], 16 * (5 - q))


INPUTS = ("x_prompt", "x_sample", "cache_k", "cache_v", "state_hgrn", "page_table", "meta_tokens", "rel_bias", "hg_lb_logits",
          "norm1_w", "w_in", "hg_onorm_w", "w_hg_out", "q_norm_w", "k_norm_w", "da_lambda", "da_onorm_w", "w_da_out", "w_o",
          "norm2_w", "w_router_group", "b_router_group", "w_router_expert", "b_router_expert", "w_gate", "w_up", "w_down")
OUTPUTS = {"y_prompt": (1, SEQ, D), "y_sample": (DB, DS, D),
           "new_k_prompt": (1, 1, META + SEQ, HEADS, P), "new_v_prompt": (1, 1, META + SEQ, HEADS, P),
           "new_state_prompt": (1, 1, HEADS, P, P),
           "new_k_sample": (1, DB, DS, HEADS, P), "new_v_sample": (1, DB, DS, HEADS, P),
           "new_state_sample": (1, DB, HEADS, P, P)}


def kernel(**inputs):
    import concourse.bacc as bacc
    from concourse.bass_utils import run_bass_kernel_spmd

    nc = bacc.Bacc("TRN2", target_bir_lowering=False, num_devices=1)
    arrays = {n: np.ascontiguousarray(inputs[n]) for n in INPUTS}
    arrays.update(constants())
    A = {n: nc.dram_tensor(n, a.shape, mybir.dt.from_np(a.dtype), kind="ExternalInput").ap() for n, a in arrays.items()}
    out = {n: nc.dram_tensor(n, shape, F32, kind="ExternalOutput").ap() for n, shape in OUTPUTS.items()}
    build(nc, A, out)
    result = run_bass_kernel_spmd(nc, [arrays], core_ids=[0]).results[0]
    return tuple(result[n] for n in OUTPUTS)
```

```python
from contextlib import ExitStack

import numpy as np

import concourse.bass as bass
from concourse import mybir

F32 = mybir.dt.float32
F32R = mybir.dt.float32r
I32 = mybir.dt.int32
ALU = mybir.AluOpType
ACT = mybir.ActivationFunctionType
AX_X = mybir.AxisListType.X

P = 128
D = 1024
KC = D // P
SEQ, META, PAST, PAGE = 1024, 16, 1024, 128
DB, DS = 8, 8
NSAMP = DB * DS
HEADS = 4
FIRST = META + NSAMP
TOK = FIRST + SEQ
NT = 1 + SEQ // P
ROWS = [FIRST] + [P] * (NT - 1)
COL = [0] + [FIRST + P * i for i in range(NT - 1)]
CH = TOK // 3
NPG = PAST // PAGE
EPS = 1e-6
LAM_INIT = 0.2
E = 16
FF = 256
SLOTS = (2 * TOK - E) // P + E + 1
WORDS = 53200
KEPT = (KC + 2 * HEADS) * TOK + 708
SPLIT = 2 * KC * TOK + 4 * KC * 256
OUTPUT_SPLIT = 2 * KC * D + 4 * KC * P
BUFFERS = 4
FEWEST = -(-2 * TOK // P)
LEVELS = [64, 32, 16, 8, 4, 2, 1]
NEG = -1e30
HQ, HF, HI, HG, DQ, DK, DV, GA, GB = 0, 512, 1024, 1536, 2048, 2560, 3072, 3584, 4608
UNIT_COL = [0, COL[3], COL[6]]
UNIT_W = [COL[3], 3 * P, 3 * P]


def cols(i):
    return slice(COL[i], COL[i] + ROWS[i])


def t5_bucket(n):
    n = np.maximum(n, 0)
    large = 16 + (np.log(np.maximum(n, 1).astype(np.float32) / np.float32(16)) / np.float32(np.log(8.0))
                  * np.float32(16)).astype(np.int32)
    return np.where(n < 16, n, np.minimum(large, 31))


ND = 384
NEAR0 = -127


def constants():
    c = {}
    c["ident"] = np.eye(P, dtype=np.float32)
    s, t = np.arange(P)[:, None], np.arange(P)[None, :]
    lv = np.zeros((P, 8, P), np.float32)
    for n, L in enumerate(LEVELS):
        lv[:, n] = (s // (2 * L) == t // (2 * L)) & (s % (2 * L) < L) & (t % (2 * L) >= L)
    lv[:, 7] = s == t
    c["level_mask"] = lv.reshape(P, 8 * P)
    l0 = lv[:, 3:].copy()
    l0[META:, 0] = 0.0
    c["level_mask0"] = l0[:FIRST].reshape(FIRST, 5 * P)
    seg = np.ones(TOK, np.float32)
    seg[0] = 0
    seg[META:FIRST:DS] = 0
    seg[COL[1]::P] = 0
    c["scan_mask"] = np.broadcast_to(seg[:COL[4]], (P, COL[4])).copy()
    rm = np.zeros((FIRST, 9), np.float32)
    rm[:META, 8] = 1
    for b in range(DB):
        rm[META + DS * b:META + DS * (b + 1), b] = 1
    c["row_mask"] = rm
    dist = np.arange(ND) + NEAR0
    oh = np.zeros((33, ND), np.float32)
    for b in range(32):
        oh[b] = (t5_bucket(dist) == b) & (dist >= 0)
    oh[32] = dist < 0
    c["bucket"] = oh[:, ::-1].copy()
    cm = np.zeros((P, 2 * NSAMP // 2 + 2), np.float32)
    r = np.arange(P)
    b2, h, m, q = r // 64, r // 16 % 4, r // 8 % 2, r % 8
    cm[r, b2 * 32 + h * 8 + q] = 1
    cm[:, 64] = m == 0
    cm[:, 65] = -(m == 1).astype(np.float32)
    c["combine"] = cm
    c["strict"] = (s < t).astype(np.float32)
    c["experts"] = np.broadcast_to(np.concatenate([np.arange(4, 0, -1), 128.0 * np.arange(9), np.arange(40)]).astype(np.float32), (P, 53)).copy()
    c["token_id"] = (np.array(COL)[None, :] + np.arange(P)[:, None]).astype(np.float32)
    c["valid"] = (np.arange(P)[:, None] < np.array(ROWS)[None, :]).astype(np.float32)
    em = np.ones((P, E, NT), np.float32)
    em[:, :, 0] = 0
    c["expert_mask"] = em.reshape(P, E * NT)
    return c


def build(nc, A, out):
    with ExitStack() as stack:
        psum = stack.enter_context(nc.psum_tensor("psum", [P, 8, 512], F32))
        parts = [(stack.enter_context(nc.sbuf_tensor("kept", [P, KEPT], F32)), 0, KEPT)]
        top = [0]

        def sb(*shape):
            n = int(np.prod(shape))
            tensor, start = next((t, max(top[0], a)) for t, a, size in parts if max(top[0], a) + n <= a + size)
            top[0] = start + n
            base = next(a for t, a, size in parts if t is tensor)
            v = tensor[:, start - base:start - base + n]
            if len(shape) == 2:
                v = v.rearrange("p (a b) -> p a b", b=shape[1])
            return v

        K = dict(xT=sb(KC, TOK), oaT=sb(HEADS, TOK))
        K.update(
            ident=sb(P), vecT=sb(19), lam=sb(4), lb=sb(12),
            knorm=sb(64), combine=sb(66), half=sb(16), logit=sb(NT, 20), weight=sb(2, NT),
        )
        K["slot"], K["expert"], K["buffer"], K["token"], K["ends"], K["before_last"] = (sb(n).bitcast(I32) for n in (2 * NT, SLOTS, SLOTS, SLOTS, E, 1))
        K["table"] = sb(NPG * DB).bitcast(I32)
        mark = top[0]
        dram = lambda n, s, dt=F32: nc.dram_tensor(n, s, dt, kind="Internal").ap()
        with nc.sbuf_tensor("branch_part", [P, WORDS - KEPT], F32) as branches:
            parts.append((branches, KEPT, WORDS - KEPT))
            top[0] = KEPT
            K["Wr"] = [sb(KC, 512) for _ in range(2)]
            K["wr_in"] = [nc.alloc_semaphore(name=f"recurrence_w_in{b}") for b in range(2)]
            phase_norm1(nc, A, K, sb, psum)
            top[0] = mark
            phase_recurrence(nc, A, K, out, sb, psum)
            top[0] = mark
            K["obT"] = sb(HEADS, TOK)
            assert top[0] == KEPT
            K["Qs"], K["kS"], K["vS"] = sb(HEADS * DB, 64), sb(HEADS, FIRST), sb(HEADS, P)
            mark = top[0]
            phase_attention(nc, A, K, out, sb, psum, dram)
            top[0] = mark
            phase_sample_attention(nc, A, K, sb, psum)
            parts.pop()
        K["hn_dram"], K["y_dram"], K["slot_token"] = dram("normed", [TOK, D]), dram("expert_out", [SLOTS * P, D]), dram("slot_token", [SLOTS * P, 1])
        with nc.sbuf_tensor("split", [P, SPLIT], F32R) as split, nc.sbuf_tensor("merge_part", [P, WORDS - KEPT - SPLIT], F32) as rest:
            parts.append((rest, KEPT + SPLIT, WORDS - KEPT - SPLIT))
            top[0] = KEPT + SPLIT
            K["mT"] = K["xT"]
            phase_merge(nc, A, K, sb, psum, split)
            parts.pop()
        hidden = stack.enter_context(nc.sbuf_tensor("hidden", [P, NT * D], F32))
        K["h"] = hidden[:, :].rearrange("p (a b) -> p a b", b=D)
        start = KEPT + NT * D
        with nc.sbuf_tensor("output_split", [P, OUTPUT_SPLIT], F32R) as split, nc.sbuf_tensor("output_part", [P, WORDS - start - OUTPUT_SPLIT], F32) as rest:
            parts.append((rest, start + OUTPUT_SPLIT, WORDS - start - OUTPUT_SPLIT))
            top[0] = KC * TOK
            K["Wo"], K["ssq2"], K["rstd2"] = sb(4, D), sb(NT), sb(NT)
            top[0] = KEPT - HEADS * TOK
            phase_output(nc, A, K, sb, psum, split)
            parts.pop()
        experts = stack.enter_context(nc.sbuf_tensor("moe_part", [P, WORDS - start], F32))
        parts.append((experts, start, WORDS - start))
        top[0] = start
        K["GU"], K["Wd"] = sb(BUFFERS * KC, 512), sb(BUFFERS * 2, D)
        K["w_in"] = [nc.alloc_semaphore(name=f"expert_w_in{b}") for b in range(BUFFERS)]
        top[0] = 0
        phase_route(nc, A, K, sb, psum)
        top[0] = 0
        phase_experts(nc, A, K, sb, psum)
        top[0] = 0
        phase_combine(nc, A, K, out, sb, psum)


def load_recurrence_block(sp, A, K, blk):
    W = A["w_in"][0].rearrange("(k p) n -> p k n", p=P)
    for j, base in enumerate((HI, HG) if blk % 2 else (HQ, HF)):
        sp.dma_start(K["Wr"][blk % 2][:, :, 256 * j:256 * j + 256],
                     W[:, :, base + 256 * (blk // 2):base + 256 * (blk // 2) + 256]).then_inc(K["wr_in"][blk % 2], 16)


def phase_norm1(nc, A, K, sb, psum):
    with ExitStack() as st:
        st.enter_context(nc.cleanup_on_exit())
        sem = lambda n: nc.alloc_semaphore(name="norm1_" + n)
        const_in, rows_in = sem("const_in"), sem("rows_in")
        x_in = [sem(f"x_in{i}") for i in range(3)]
        ssq_done, rstd_done, xn_done, turned, evacuated = sem("ssq_done"), sem("rstd_done"), sem("xn_done"), sem("turned"), sem("evacuated")
        vec_turned, lb_max, lb_exp, setup = sem("vec_turned"), sem("lb_max"), sem("lb_exp"), sem("setup")
        lam_dot, lam_exp = sem("lam_dot"), sem("lam_exp")
        xin, xn, junk = sb(3, D), sb(2, D), sb(D)
        rows, ssq, mean, power, rstd = sb(P), sb(NT), sb(NT), sb(NT), sb(NT)
        lp, lpp, dots, lm = sb(4, 64), sb(2, 64), sb(2), sb(3, HEADS)
        vec = K["vecT"]

        block = st.enter_context(nc.Block())

        @block.sync
        def _(sp):
            sp.dma_start(K["ident"], A["ident"]).then_inc(const_in, 16)
            for r0, n, src in ((0, 8, A["norm1_w"].rearrange("a (r c) -> (a r) c", c=P)),
                               (8, 8, A["hg_lb_logits"].rearrange("a (r c) -> (a r) c", c=P)),
                               (16, 1, A["hg_onorm_w"]), (17, 1, A["da_onorm_w"])):
                sp.dma_start(rows[r0:r0 + n, :], src).then_inc(rows_in, 16)
            for m in range(2):
                sp.dma_start(rows[18:19, 64 * m:64 * m + 64], A["q_norm_w"]).then_inc(rows_in, 16)
            for i in range(NT):
                if i >= 3:
                    sp.wait_ge(xn_done, i - 2)
                if i == 0:
                    sp.dma_start(xin[0:META, 0, :], A["meta_tokens"]).then_inc(x_in[0], 16)
                    sp.dma_start(xin[META:FIRST, 0, :], A["x_sample"].rearrange("a b d -> (a b) d")).then_inc(x_in[0], 16)
                else:
                    sp.dma_start(xin[:, i % 3, :], A["x_prompt"][0, P * (i - 1):P * i, :]).then_inc(x_in[i % 3], 16)
            sp.dma_start(lp.rearrange("p a b -> p (a b)"), A["da_lambda"].rearrange("a b c -> a (b c)").to_broadcast([P, 256])).then_inc(const_in, 16)
            sp.dma_start(K["knorm"], A["k_norm_w"].to_broadcast([P, 64])).then_inc(const_in, 16)
            sp.dma_start(K["combine"], A["combine"]).then_inc(const_in, 16)
            sp.dma_start(K["table"][0:1, :], A["page_table"].rearrange("a b -> (a b)").unsqueeze(0)).then_inc(const_in, 16)
            load_recurrence_block(sp, A, K, 0)
            load_recurrence_block(sp, A, K, 1)
            sp.wait_ge(const_in, 80)

        def x_ready(e, i):
            e.wait_ge(x_in[i % 3], 32 if i == 0 else 16 * (i // 3 + (2 if i % 3 == 0 else 1)))

        @block.scalar
        def _(act):
            for i in range(NT):
                x_ready(act, i)
                if i:
                    act.drain()
                act.activation(junk[:ROWS[i], :], xin[:ROWS[i], i % 3, :], ACT.Square,
                               accum_out=ssq[:ROWS[i], i:i + 1]).then_inc(ssq_done, 1)
            act.wait_ge(lb_max, 1)
            act.activation(lm[:, 0:2, :], lm[:, 0:2, :], ACT.Exp).then_inc(lb_exp, 1)
            act.wait_ge(lam_dot, 1)
            act.activation(K["lam"][:, 0:2], dots, ACT.Exp).then_inc(lam_exp, 1)

        @block.gpsimd
        def _(pool):
            pool.memset(power, -0.5).then_inc(setup, 1)
            pool.memset(K["half"], -0.5).then_inc(setup, 1)
            pool.wait_ge(setup, 2)
            for i in range(NT):
                r = ROWS[i]
                pool.wait_ge(ssq_done, i + 1)
                pool.tensor_scalar(mean[:r, i:i + 1], ssq[:r, i:i + 1], 1.0 / D, EPS, ALU.mult, ALU.add)
                pool.drain()
                pool.tensor_tensor(rstd[:r, i:i + 1], mean[:r, i:i + 1], power[:r, i:i + 1], ALU.pow).then_inc(rstd_done, 1)

        @block.vector
        def _(dve):
            def evacuate(i):
                r = ROWS[i]
                dve.wait_ge(turned, i + 1)
                dve.tensor_tensor(K["xT"][:, :, cols(i)], psum[:, 2 * (i % 2):2 * (i % 2) + 2, :].rearrange("p a (b c) -> p (a b) c", c=P)[:, :, :r],
                                  vec[:, 0:8].unsqueeze(2).to_broadcast([P, KC, r]), ALU.mult).then_inc(evacuated, 1)

            for i in range(NT):
                r = ROWS[i]
                x_ready(dve, i)
                dve.wait_ge(rstd_done, i + 1)
                if i >= 2:
                    dve.wait_ge(turned, i - 1)
                dve.tensor_scalar(xn[:r, i % 2, :], xin[:r, i % 3, :], rstd[:r, i:i + 1], None, ALU.mult).then_inc(xn_done, 1)
                if i == 0:
                    dve.wait_ge(vec_turned, 1)
                    dve.tensor_copy(vec, psum[:, 4, 0:19])
                    dve.drain()
                else:
                    evacuate(i - 1)
            evacuate(NT - 1)
            lb, l0, l1 = K["lb"], vec[:, 8:12], vec[:, 12:16]
            dve.tensor_tensor(lm[:, 2, :], l0, l1, ALU.max)
            dve.drain()
            dve.tensor_tensor(lm[:, 0, :], l0, lm[:, 2, :], ALU.subtract)
            dve.tensor_tensor(lm[:, 1, :], l1, lm[:, 2, :], ALU.subtract).then_inc(lb_max, 1)
            dve.wait_ge(lb_exp, 1)
            dve.tensor_tensor(lm[:, 1, :], lm[:, 0, :], lm[:, 1, :], ALU.add)
            dve.drain()
            dve.reciprocal(lm[:, 1, :], lm[:, 1, :])
            dve.drain()
            dve.tensor_tensor(lb[:, 8:12], lm[:, 0, :], lm[:, 1, :], ALU.mult)
            dve.drain()
            dve.tensor_scalar(lb[:, 0:4], lb[:, 8:12], -0.5, 0.5, ALU.mult, ALU.add)
            dve.tensor_scalar(lb[:, 4:8], lb[:, 8:12], 0.5, 0.5, ALU.mult, ALU.add)
            dve.wait_ge(const_in, 80)
            dve.tensor_tensor(lpp, lp[:, 0:4:2, :], lp[:, 1:4:2, :], ALU.mult)
            dve.drain()
            dve.tensor_reduce(dots, lpp, AX_X, ALU.add).then_inc(lam_dot, 1)
            dve.wait_ge(lam_exp, 1)
            lam = K["lam"]
            dve.tensor_tensor(lam[:, 2:3], lam[:, 0:1], lam[:, 1:2], ALU.subtract)
            dve.drain()
            dve.tensor_scalar(lam[:, 3:4], lam[:, 2:3], -1.0, -LAM_INIT, ALU.mult, ALU.add)
            dve.tensor_scalar(vec[:, 17:18], vec[:, 17:18], 1.0 - LAM_INIT, None, ALU.mult)
            dve.tensor_scalar(vec[:, 18:19], vec[:, 18:19], 0.125, None, ALU.mult)

        @block.tensor
        def _(pe):
            pe.wait_ge(const_in, 16)
            pe.wait_ge(rows_in, 96)
            pe.transpose(psum[:, 4, 0:19], rows[0:19, :], K["ident"][0:19, 0:19]).then_inc(vec_turned, 1)
            for i in range(NT):
                r = ROWS[i]
                pe.wait_ge(xn_done, i + 1)
                if i >= 2:
                    pe.wait_ge(evacuated, i - 1)
                for k in range(KC):
                    mm = pe.transpose(psum[:, 2 * (i % 2) + k // 4, P * (k % 4):P * (k % 4) + r],
                                      xn[:r, i % 2, P * k:P * k + P], K["ident"][:r, :r])
                mm.then_inc(turned, 1)


def phase_recurrence(nc, A, K, out, sb, psum):
    W = A["w_in"][0].rearrange("(k p) n -> p k n", p=P)
    channel = lambda h: [("c", h, w, n) for w in "qf" for n in range(3)]
    token = lambda p: [("t", p, "", i) for i in range(NT)]
    STEPS = HEADS * NT
    start = channel(0) + token(0)[:4]
    fq = lambda h: [("c", h, w, n) for n in range(3) for w in "fq"]
    at_slot = [[] for _ in range(STEPS)]
    for units, slots in ((token(0)[4:], range(3, 8)), (fq(1), (0, 1, 2, 8, 9, 11)), (fq(2), (15, 17, 18, 20, 21, 23)),
                         (fq(3), (24, 26, 27, 29, 30, 32)), (token(1), (12, 13, 14, 16, 19, 21, 22, 23, 25))):
        for u, slot in zip(units, slots):
            at_slot[slot].append(u)
    HEADSTART = len(start)
    proj = start + [u for us in at_slot for u in us]
    jobs = list(proj[:HEADSTART])
    for s in range(STEPS + 2):
        if s < STEPS:
            jobs += at_slot[s] + [("k", s)]
        if 1 <= s <= STEPS:
            jobs += [("o", s - 1)] + [("m", s - 1)] * ((s - 1) % NT == 0)
        if s >= 2:
            jobs += [("g", s - 2)]
    turn_of = {u: n for n, u in enumerate(jobs)}
    index = {u: n for n, u in enumerate(proj)}
    with ExitStack() as st:
        st.enter_context(nc.cleanup_on_exit())
        sem = lambda n: nc.alloc_semaphore(name="recurrence_" + n)
        c_in, smask_in, projected, tanh_done, q_done, tok_act, tok_dve = sem("c_in"), sem("smask_in"), sem("projected"), sem("tanh_done"), sem("q_done"), sem("tok_act"), sem("tok_dve")
        f_done, logf_done, x_sub, x_exp, unit_done = sem("f_done"), sem("logf_done"), sem("x_sub"), sem("x_exp"), sem("unit_done")
        leveled, kd_turned, kd_copied, at_done, o_done, st_done, s_new = sem("leveled"), sem("kd_turned"), sem("kd_copied"), sem("at_done"), sem("o_done"), sem("st_done"), sem("s_new")
        ssq_done, rstd_done, og_done, og_turned, oa_done = sem("ssq_done"), sem("rstd_done"), sem("og_done"), sem("og_turned"), sem("oa_done")
        setup, state_in, state_out, qz_done, vm_done = sem("setup"), [sem("state_in")], sem("state_out"), sem("qz_done"), sem("vm_done")
        th2 = sb(2, TOK)
        q2 = sb(2, TOK)
        Wb = [sb(KC, 512) for _ in range(2)]
        w_in = K["wr_in"]
        tq = sb(2, CH)
        hi, gate = sb(2 * NT, 256), sb(2 * NT, 256)
        kb, bb, kd, eb, qe = (sb(2, 384) for _ in range(5))
        X = sb(2, 7 * 384)
        lmask, lmask0, smask, rmask = sb(8, P), sb(5, P), sb(COL[4]), sb(9)
        AM, AT, kdT = sb(8 * P), sb(2, P), sb(2, P)
        Vm, QEz = sb(9, P), sb(DB, FIRST)
        S = sb(2, P)
        Sb = sb(DB, P)
        og = sb(2, P)
        junk, ssq, rstd = sb(P), sb(STEPS), sb(STEPS)
        block = st.enter_context(nc.Block())

        def unit_of(s):
            return s // 3

        def bank_of(job):
            return psum[:, (0, 1, 6, 7)[turn_of[job] % 4], :]

        def bank_free(e, job):
            if turn_of[job] < 4:
                return
            last = jobs[turn_of[job] - 4]
            if last[0] == "k":
                return e.wait_ge(kd_copied, last[1] + 1)
            if last[0] == "o":
                return e.wait_ge(og_done, last[1] + 1)
            if last[0] == "g":
                return e.wait_ge(oa_done, last[1] + 1)
            if last[0] == "m":
                return e.wait_ge(s_new, last[1] + 1)
            kind, a, w, _ = last
            n = index[last]
            if kind == "t":
                e.wait_ge(tok_act, sum(u[0] == "t" for u in proj[:n + 1]))
                e.wait_ge(tok_dve, sum(u[0] == "t" for u in proj[:n + 1]))
            elif w == "q":
                e.wait_ge(q_done, sum(u[2] == "q" for u in proj[:n + 1]))
            else:
                e.wait_ge(tanh_done, sum(u[0] == "c" for u in proj[:n + 1]))

        @block.sync
        def _(sp):
            sp.dma_start(smask, A["scan_mask"]).then_inc(smask_in, 16)
            sp.dma_start(Sb, A["state_hgrn"][0, :, 0].rearrange("b k v -> k b v")).then_inc(state_in[0], 16)
            sp.dma_start(lmask.rearrange("p a b -> p (a b)"), A["level_mask"]).then_inc(c_in, 16)
            sp.dma_start(lmask0[:FIRST].rearrange("p a b -> p (a b)"), A["level_mask0"]).then_inc(c_in, 16)
            sp.dma_start(rmask[:FIRST], A["row_mask"]).then_inc(c_in, 16)
            sp.wait_ge(projected, index[("t", 0, "", NT - 1)] + 1)
            load_recurrence_block(sp, A, K, 3)
            for h in range(HEADS):
                if h:
                    sp.wait_ge(s_new, NT * h)
                    sp.wait_ge(state_out, 32 * h)
                    sp.dma_start(Sb, A["state_hgrn"][0, :, h].rearrange("b k v -> k b v")).then_inc(state_in[0], 16)
                if h == 1:
                    sp.wait_ge(projected, index[fq(1)[-1]] + 1)
                    load_recurrence_block(sp, A, K, 2)
                sp.wait_ge(s_new, NT * h + 1)
                sp.dma_start(out["new_state_sample"][0, :, h].rearrange("b k v -> k b v"), Sb).then_inc(state_out, 16)
                sp.wait_ge(s_new, NT * h + NT)
                sp.dma_start(out["new_state_prompt"][0, 0, h], S[:, (NT - 1) % 2, :]).then_inc(state_out, 16)
            sp.wait_ge(state_out, 32 * HEADS)

        @block.tensor
        def _(pe):
            def product(u):
                n = index[u]
                kind, a, w, i = u
                bank_free(pe, u)
                bank = bank_of(u)
                if kind == "c":
                    pe.wait_ge(w_in[0], 32 * (a // 2 + 1))
                    c0 = 256 * (w == "f") + P * (a % 2)
                    for k in range(KC):
                        mm = pe.matmul(bank[:, 0:CH], Wb[0][:, k, c0:c0 + P], K["xT"][:, k, CH * i:CH * i + CH],
                                       start=(k == 0), stop=(k == KC - 1))
                else:
                    pe.wait_ge(w_in[1], 32 * (a + 1))
                    for k in range(KC):
                        mm = pe.matmul(bank[:ROWS[i], :], K["xT"][:, k, cols(i)], Wb[1][:, k, :],
                                       start=(k == 0), stop=(k == KC - 1))
                mm.then_inc(projected, 1)

            def scores(s):
                i, u = s % NT, s // 3
                r, x0 = ROWS[i], COL[i] - UNIT_COL[u % 3]
                xs = slice(x0, x0 + r)
                lev = psum[:, 2 + 2 * (s % 2):4 + 2 * (s % 2), :].rearrange("p a (b c) -> p (a b) c", c=P)
                pe.wait_ge(unit_done, u + 1)
                if s >= 2:
                    pe.wait_ge(s_new, s - 1)
                Xu = X[:, u % 2, :].rearrange("p (l c) -> p l c", l=7)
                first = 3 if i == 0 else 0
                for l in range(first, 7):
                    pe.matmul(lev[:r, l - first, :r], Xu[:, l, xs], Xu[:, l, xs], start=True, stop=True)
                pe.matmul(lev[:r, 7 - first, :r], kb[:, u % 2, xs], q2[:, s // NT % 2, cols(i)],
                          start=True, stop=True).then_inc(leveled, 1)
                bank_free(pe, ("k", s))
                pe.transpose(bank_of(("k", s))[:r, 0:P], kd[:, u % 2, xs], K["ident"]).then_inc(kd_turned, 1)

            def outputs(s):
                h, i, u = s // NT, s % NT, s // 3
                r, x0 = ROWS[i], COL[i] - UNIT_COL[u % 3]
                v = hi[:r, NT * (h // 2) + i, P * (h % 2):P * (h % 2) + P]
                pe.wait_ge(at_done, s + 1)
                pe.wait_ge(kd_copied, s + 1)
                pe.wait_ge(tok_act, NT * (h // 2) + i + 1)
                bank_free(pe, ("o", s))
                o = bank_of(("o", s))[:r, 0:P]
                pe.matmul(o, AT[:r, s % 2, :r], v, start=True, stop=False)
                if i == 0:
                    pe.wait_ge(state_in[0], 16 * (h + 1))
                    pe.wait_ge(qz_done, h + 1)
                    for b in range(DB):
                        mm = pe.matmul(o, QEz[:, b, :], Sb[:, b, :], start=False, stop=(b == DB - 1))
                    mm.then_inc(o_done, 1)
                    pe.wait_ge(vm_done, h + 1)
                    lev = psum[:, 2 + 2 * (s % 2):4 + 2 * (s % 2), :]
                    for j in range(2):
                        pe.matmul(lev[:, j, :], kdT[:r, s % 2, :], Vm[:r, 4 * j:4 * j + 4, :].rearrange("p a b -> p (a b)"),
                                  start=True, stop=True)
                    bank_free(pe, ("m", s))
                    pe.matmul(bank_of(("m", s))[:, 0:P], kdT[:r, s % 2, :], Vm[:r, 8, :], start=True, stop=True).then_inc(st_done, 1)
                else:
                    pe.wait_ge(s_new, s)
                    pe.matmul(o, qe[:, u % 2, x0:x0 + r], S[:, (i + 1) % 2, :], start=False, stop=True).then_inc(o_done, 1)
                    pe.matmul(psum[:, 3 + 2 * (s % 2), 0:P], kdT[:r, s % 2, :], v, start=True, stop=True).then_inc(st_done, 1)

            def turn(s):
                r = ROWS[s % NT]
                pe.wait_ge(og_done, s + 1)
                bank_free(pe, ("g", s))
                pe.transpose(bank_of(("g", s))[:, 0:r], og[:r, s % 2, :],
                             K["ident"][:r, :r]).then_inc(og_turned, 1)

            for u in proj[:HEADSTART]:
                product(u)
            for s in range(STEPS + 2):
                if s < STEPS:
                    for u in at_slot[s]:
                        product(u)
                    scores(s)
                if 1 <= s <= STEPS:
                    outputs(s - 1)
                if s >= 2:
                    turn(s - 2)

        def act_product(act, u):
            n = index[u]
            kind, a, w, i = u
            bank = bank_of(u)
            act.wait_ge(projected, n + 1)
            if kind == "c" and w == "q":
                nq = sum(x[2] == "q" for x in proj[:n])
                if nq >= 2:
                    act.wait_ge(q_done, nq - 1)
                act.activation(tq[:, nq % 2, :], bank[:, 0:CH], ACT.Tanh, scale=0.5).then_inc(tanh_done, 1)
            elif kind == "c":
                if a >= 2:
                    act.wait_ge(unit_done, 3 * (a - 1))
                act.activation(th2[:, a % 2, CH * i:CH * i + CH], bank[:, 0:CH], ACT.Tanh, scale=0.5).then_inc(tanh_done, 1)
            else:
                r = ROWS[i]
                act.activation(gate[:r, NT * a + i, :], bank[:r, 256:512], ACT.Tanh, scale=0.5)
                act.activation(hi[:r, NT * a + i, :], bank[:r, 0:256], ACT.Copy).then_inc(tok_act, 1)

        @block.scalar
        def _(act):
            def unit_log(u):
                w = UNIT_W[u % 3]
                act.wait_ge(f_done, u + 1)
                act.activation(bb[:, u % 2, :w], bb[:, u % 2, :w], ACT.Ln).then_inc(logf_done, 1)

            def unit_decays(u):
                w = UNIT_W[u % 3]
                act.wait_ge(x_sub, 2 * u + 1)
                act.activation(eb[:, u % 2, :w], bb[:, u % 2, :w], ACT.Exp)
                act.activation(kd[:, u % 2, :w], kd[:, u % 2, :w], ACT.Exp).then_inc(x_exp, 1)

            def unit_levels(u):
                w = UNIT_W[u % 3]
                Xu = X[:, u % 2, :].rearrange("p (l c) -> p l c", l=7)
                act.wait_ge(x_sub, 2 * u + 2)
                if u % 3 == 0:
                    act.activation(Xu[:, 0:3, FIRST:w], Xu[:, 0:3, FIRST:w], ACT.Exp)
                    act.activation(Xu[:, 3:7, 0:w], Xu[:, 3:7, 0:w], ACT.Exp).then_inc(x_exp, 1)
                else:
                    act.activation(Xu[:, :, 0:w], Xu[:, :, 0:w], ACT.Exp).then_inc(x_exp, 1)

            def tile_copy(s):
                r = ROWS[s % NT]
                act.wait_ge(kd_turned, s + 1)
                if s >= 2:
                    act.wait_ge(st_done, s - 1)
                act.activation(kdT[:r, s % 2, :], bank_of(("k", s))[:r, 0:P], ACT.Copy).then_inc(kd_copied, 1)

            def tile_square(s):
                r = ROWS[s % NT]
                act.wait_ge(o_done, s + 1)
                act.drain()
                act.activation(junk[:r], bank_of(("o", s))[:r, 0:P], ACT.Square,
                               accum_out=ssq[:r, s:s + 1]).then_inc(ssq_done, 1)

            def tile_out(s):
                i = s % NT
                act.wait_ge(og_turned, s + 1)
                act.activation(K["oaT"][:, s // NT, cols(i)], bank_of(("g", s))[:, 0:ROWS[i]],
                               ACT.Copy, scale=K["vecT"][:, 16:17]).then_inc(oa_done, 1)

            for u in channel(0):
                act_product(act, u)
            parts = (unit_log, unit_decays, unit_levels)
            for part in parts:
                part(0)
            for u in start[len(channel(0)):]:
                act_product(act, u)
            for s in range(STEPS + 2):
                if s < STEPS:
                    for u in at_slot[s]:
                        act_product(act, u)
                    tile_copy(s)
                if s % 3 == 2 and s < STEPS - 3:
                    unit_levels(s // 3 + 1)
                if 1 <= s <= STEPS:
                    tile_square(s - 1)
                if s >= 2:
                    tile_out(s - 2)
                if s % 3 < 2 and s < STEPS - 3:
                    parts[s % 3](s // 3 + 1)

        @block.gpsimd
        def _(pool):
            pool.memset(QEz, 0.0).then_inc(setup, 1)
            for s in range(STEPS):
                r = ROWS[s % NT]
                if s % NT == 0:
                    h = s // NT
                    pool.wait_ge(tok_act, NT * (h // 2) + 1)
                    pool.wait_ge(c_in, 48)
                    if h:
                        pool.wait_ge(st_done, NT * (h - 1) + 1)
                    pool.tensor_tensor(Vm[:r], hi[:r, NT * (h // 2), P * (h % 2):P * (h % 2) + P].unsqueeze(1).to_broadcast([r, 9, P]),
                                       rmask[:r].unsqueeze(2).to_broadcast([r, 9, P]), ALU.mult).then_inc(vm_done, 1)
                pool.wait_ge(ssq_done, s + 1)
                pool.tensor_scalar(ssq[:r, s:s + 1], ssq[:r, s:s + 1], 16.0 / (4 * P), 16 * EPS, ALU.mult, ALU.add)
                pool.drain()
                pool.tensor_tensor(rstd[:r, s:s + 1], ssq[:r, s:s + 1], K["half"][:r, 0:1], ALU.pow).then_inc(rstd_done, 1)

        @block.vector
        def _(dve):
            def product(u):
                n = index[u]
                kind, a, w, i = u
                bank = bank_of(u)
                if kind == "c" and w == "q":
                    nq = sum(x[2] == "q" for x in proj[:n])
                    dve.wait_ge(tanh_done, sum(x[0] == "c" for x in proj[:n + 1]))
                    if a >= 2:
                        dve.wait_ge(leveled, NT * (a - 1))
                    dve.scalar_tensor_tensor(q2[:, a % 2, CH * i:CH * i + CH], tq[:, nq % 2, :], 1.0, bank[:, 0:CH],
                                             ALU.add, ALU.mult).then_inc(q_done, 1)
                elif kind == "t":
                    r = ROWS[i]
                    g = gate[:r, NT * a + i, :]
                    dve.wait_ge(tok_act, NT * a + i + 1)
                    dve.scalar_tensor_tensor(g, g, 1.0, bank[:r, 256:512], ALU.add, ALU.mult).then_inc(tok_dve, 1)

            def halves(u, L):
                o = FIRST if u % 3 == 0 and L > 8 else 0
                return o, (UNIT_W[u % 3] - o) // (2 * L)

            def unit_gate(u):
                h, w, c0, off = u // 3, UNIT_W[u % 3], UNIT_COL[u % 3], (FIRST if u % 3 == 0 else 0)
                k, b, d = kb[:, u % 2, :], bb[:, u % 2, :], kd[:, u % 2, :]
                lb = K["lb"]
                dve.wait_ge(tanh_done, sum(x[0] == "c" for x in proj[:index[("c", h, "f", u % 3)] + 1]))
                if u >= 2:
                    dve.wait_ge(leveled, 3 * (u - 1))
                    dve.wait_ge(kd_turned, 3 * (u - 1))
                dve.drain()
                dve.tensor_scalar(b[:, :w], th2[:, h % 2, c0:c0 + w], lb[:, h:h + 1], lb[:, 4 + h:5 + h], ALU.mult, ALU.add)
                dve.drain()
                dve.tensor_scalar(k[:, :w], b[:, :w], -1.0, 1.0, ALU.mult, ALU.add).then_inc(f_done, 1)

            def unit_sums(u):
                h, w, c0, off = u // 3, UNIT_W[u % 3], UNIT_COL[u % 3], (FIRST if u % 3 == 0 else 0)
                k, b, d = kb[:, u % 2, :], bb[:, u % 2, :], kd[:, u % 2, :]
                m0 = 0 if off else COL[1]
                Xu = X[:, u % 2, :].rearrange("p (l c) -> p l c", l=7)
                dve.wait_ge(logf_done, u + 1)
                dve.drain()
                dve.tensor_tensor_scan(b[:, :w], smask[:, m0:m0 + w], b[:, :w], 0.0, ALU.mult, ALU.add)
                dve.drain()
                if off:
                    dve.tensor_tensor(d[:, 0:META], b[:, META - 1:META].to_broadcast([P, META]), b[:, 0:META], ALU.subtract)
                    bs, ds = (x[:, META:FIRST].rearrange("p (n c) -> p n c", c=DS) for x in (b, d))
                    dve.tensor_tensor(ds, bs[:, :, DS - 1:DS].to_broadcast([P, DB, DS]), bs, ALU.subtract)
                n = (w - off) // P
                bs, ds = (x[:, off:w].rearrange("p (n c) -> p n c", c=P) for x in (b, d))
                dve.tensor_tensor(ds, bs[:, :, P - 1:P].to_broadcast([P, n, P]), bs, ALU.subtract).then_inc(x_sub, 1)

                for l, L in enumerate(LEVELS):
                    o, m = halves(u, L)
                    bs = b[:, o:w].rearrange("p (n c) -> p n c", c=2 * L)
                    xs = Xu[:, l, o:w].rearrange("p (n c) -> p n c", c=2 * L)
                    mid = bs[:, :, L - 1:L].to_broadcast([P, m, L])
                    dve.tensor_tensor(xs[:, :, 0:L], mid, bs[:, :, 0:L], ALU.subtract)
                    ins = dve.tensor_tensor(xs[:, :, L:2 * L], bs[:, :, L:2 * L], mid, ALU.subtract)
                ins.then_inc(x_sub, 1)

            def unit_products(u):
                h, w, c0, off = u // 3, UNIT_W[u % 3], UNIT_COL[u % 3], (FIRST if u % 3 == 0 else 0)
                k, b, d = kb[:, u % 2, :], bb[:, u % 2, :], kd[:, u % 2, :]
                q = q2[:, h % 2, c0:c0 + w]
                Xu = X[:, u % 2, :].rearrange("p (l c) -> p l c", l=7)
                dve.wait_ge(x_exp, 2 * u + 1)
                dve.tensor_tensor(d[:, :w], d[:, :w], k[:, :w], ALU.mult)
                dve.tensor_tensor(qe[:, u % 2, :w], eb[:, u % 2, :w], q, ALU.mult)
                if u % 3 == 0:
                    dve.drain()
                    if h:
                        dve.wait_ge(o_done, NT * (h - 1) + 1)
                    else:
                        dve.wait_ge(setup, 1)
                    diag = QEz.rearrange("p a b -> p (a b)")[:, META:]
                    for bt in range(DB):
                        ins = dve.tensor_copy(QEz[:, bt, META + DS * bt:META + DS * bt + DS],
                                              qe[:, u % 2, META + DS * bt:META + DS * bt + DS])
                    ins.then_inc(qz_done, 1)
                dve.wait_ge(x_exp, 2 * u + 2)
                for l, L in enumerate(LEVELS):
                    o, m = halves(u, L)
                    xs = Xu[:, l, o:w].rearrange("p (n c) -> p n c", c=2 * L)
                    ks = k[:, o:w].rearrange("p (n c) -> p n c", c=2 * L)
                    qs = q[:, o:w].rearrange("p (n c) -> p n c", c=2 * L)
                    dve.tensor_tensor(xs[:, :, 0:L], xs[:, :, 0:L], ks[:, :, 0:L], ALU.mult)
                    ins = dve.tensor_tensor(xs[:, :, L:2 * L], xs[:, :, L:2 * L], qs[:, :, L:2 * L], ALU.mult)
                ins.then_inc(unit_done, 1)

            def tile_scores(s):
                i = s % NT
                r, nl = ROWS[i], 5 if i == 0 else 8
                lev = psum[:, 2 + 2 * (s % 2):4 + 2 * (s % 2), :].rearrange("p a (b c) -> p (a b) c", c=P)
                am = AM[:r, 0:nl * r].rearrange("p (l c) -> p l c", l=nl)
                dve.wait_ge(leveled, s + 1)
                if s == 0:
                    dve.wait_ge(c_in, 48)
                if s >= 2:
                    dve.wait_ge(o_done, s - 1)
                dve.drain()
                dve.tensor_tensor(am, lev[:r, 0:nl, :r], (lmask0 if i == 0 else lmask)[:r, :, :r], ALU.mult)
                dve.drain()
                dve.tensor_reduce(AT[:r, s % 2, :r], am.rearrange("p l c -> p c l"), AX_X, ALU.add).then_inc(at_done, 1)

            def tile_state(s):
                h, i, u = s // NT, s % NT, s // 3
                r, x0 = ROWS[i], COL[i] - UNIT_COL[u % 3]
                dve.wait_ge(st_done, s + 1)
                dve.wait_ge(rstd_done, s + 1)
                if s >= 2:
                    dve.wait_ge(og_turned, s - 1)
                e = eb[:, u % 2, :]
                upd = bank_of(("m", s))[:, 0:P] if i == 0 else psum[:, 3 + 2 * (s % 2), 0:P]
                if i == 0:
                    dve.wait_ge(state_in[0], 16 * (h + 1))
                    es = e[:, META:FIRST].rearrange("p (n c) -> p n c", c=DS)[:, :, DS - 1:DS].to_broadcast([P, DB, P])
                    dve.tensor_tensor(Sb, Sb, es, ALU.mult)
                    dve.tensor_copy(S[:, 0, :], upd)
                    dve.drain()
                    lev = psum[:, 2 + 2 * (s % 2):4 + 2 * (s % 2), :].rearrange("p a (b c) -> p (a b) c", c=P)
                    dve.tensor_tensor(Sb, Sb, lev, ALU.add).then_inc(s_new, 1)
                else:
                    dve.scalar_tensor_tensor(S[:, i % 2, :], S[:, (i + 1) % 2, :], e[:, x0 + P - 1:x0 + P], upd,
                                             ALU.mult, ALU.add).then_inc(s_new, 1)
                g = gate[:r, NT * (h // 2) + i, P * (h % 2):P * (h % 2) + P]
                dve.scalar_tensor_tensor(og[:r, s % 2, :], bank_of(("o", s))[:r, 0:P], rstd[:r, s:s + 1], g,
                                         ALU.mult, ALU.mult).then_inc(og_done, 1)

            for u in channel(0):
                product(u)
            dve.wait_ge(smask_in, 16)
            parts = (unit_gate, unit_sums, unit_products)
            for part in parts:
                part(0)
            for u in start[len(channel(0)):]:
                product(u)
            for s in range(STEPS + 1):
                if s < STEPS:
                    for u in at_slot[s]:
                        product(u)
                    tile_scores(s)
                if s:
                    dve.wait_ge(o_done, s)
                    tile_state(s - 1)
                if s < STEPS - 3:
                    parts[s % 3](s // 3 + 1)


def phase_attention(nc, A, K, out, sb, psum, dram):
    W = A["w_in"][0].rearrange("(k p) n -> p k n", p=P)
    NQ = NT
    STEPS = HEADS * NQ
    groups = lambda s: (s % NQ + 4) // 4
    AHEAD = 2
    make = [("z", n // NQ, n % NQ) for n in range(STEPS)]
    place = [("x", n // NQ, n % NQ) for n in range(STEPS)]
    zx = make[:1]
    for n in range(1, AHEAD):
        zx += [make[n], place[n - 1]]
    slots = []
    for s in range(STEPS + 2):
        slot = make[s + AHEAD:s + AHEAD + 1]
        if 1 <= s <= STEPS:
            slot += [("a", s - 1, g) for g in range(groups(s - 1))]
        if s < STEPS:
            slot += [("L", s, 0), ("L", s, 1)] + ([("e", s, 0)] if s % NQ == NQ - 1 else [])
        if 1 <= s <= STEPS:
            slot += [("o", s - 1, 0)]
        slot += place[s + AHEAD - 1:s + AHEAD]
        if s >= 2:
            slot += [("g", s - 2, 0)]
        slots.append(slot)
    jobs = zx + [j for slot in slots for j in slot if j[0] != "L"]
    turn_of = {j: n for n, j in enumerate(jobs)}
    a_index = {j: n for n, j in enumerate(j for j in jobs if j[0] == "a")}

    skew = [dram(f"bias_skew{h}", [P * (ND + 1)]) for h in range(HEADS)]
    K["skew"] = skew
    with ExitStack() as st:
        st.enter_context(nc.cleanup_on_exit())
        sem = lambda n: nc.alloc_semaphore(name="attention_" + n)
        w_in = [sem("w_in0"), sem("w_in1")]
        c_in, bk_in, rel_ready, bias_made, bias_row, skewed, bias_in, setup = (sem(n) for n in (
            "c_in", "bk_in", "rel_ready", "bias_made", "bias_row", "skewed", "bias_in", "setup"))
        projected, squared, summed, rstd_done, normed, k_scaled, x_turned, x_done, saved = (sem(n) for n in (
            "projected", "squared", "summed", "rstd_done", "normed", "k_scaled", "x_turned", "x_done", "saved"))
        logits, max_done, exp_done, a_done, a_turned, a_act, a_dve, o_done, ssq_done, orstd_done, og_done, og_turned, ob_done = (sem(n) for n in (
            "logits", "max_done", "exp_done", "a_done", "a_turned", "a_act", "a_dve", "o_done", "ssq_done", "orstd_done", "og_done", "og_turned", "ob_done"))
        kv_out = [sem("kv_out0"), sem("kv_out1")]
        Wb = [sb(KC, 384) for _ in range(2)]
        qz = [sb(2, TOK) for _ in range(2)]
        kT = [sb(TOK) for _ in range(2)]
        kout = [sb(NT, P) for _ in range(2)]
        v = [sb(NT, P) for _ in range(2)]
        sq, zn = sb(256), sb(2, 256)
        zs, zr = sb(NT * HEADS, 4), sb(NT * HEADS, 4)
        Bn = [sb(256) for _ in range(HEADS)]
        rel, rel31, relh, bucket, vecs = sb(HEADS), sb(HEADS), sb(HEADS, P), sb(ND), sb(HEADS, ND)
        Pm = sb(2, SEQ + META)
        Am, aT = sb(SEQ + META), sb(NT, P)
        nmax, sums, coef, ssq, rr, mt = sb(STEPS, 4), sb(STEPS, 4), sb(STEPS, 4), sb(STEPS), sb(STEPS, 2), sb(2, META)
        junk, og = sb(P), sb(2, P)
        block = st.enter_context(nc.Block())
        lg = [psum[:, 2 * m:2 * m + 2, :].rearrange("p a b -> p (a b)") for m in range(2)]

        def bank_of(job):
            return psum[:, 4 + turn_of[job] % 4, :]

        def bank_free(e, job):
            if turn_of[job] < 4:
                return
            kind, a, b = jobs[turn_of[job] - 4]
            if kind == "z":
                e.wait_ge(normed, NT * a + b + 1)
            elif kind == "x":
                e.wait_ge(x_done, NT * a + b + 1)
            elif kind == "e":
                e.wait_ge(exp_done, 2 * a + 2)
            elif kind == "a":
                n = a_index[(kind, a, b)]
                e.wait_ge(a_dve if n % 2 else a_act, n // 2 + 1)
            elif kind == "o":
                e.wait_ge(og_done, a + 1)
            else:
                e.wait_ge(ob_done, a + 1)

        def place_turned(copy, s, g):
            i = s % NQ
            r, bank = (P if i else META), bank_of(("a", s, g))
            full = min(4 * g + 4, i) - 4 * g
            if full > 0:
                ins = copy(aT[:, 4 * g:4 * g + full, :r], bank[:, 0:P * full].rearrange("p (a b) -> p a b", b=P)[:, :, :r])
            if i < 4 * g + 4:
                ins = copy(aT[:META, i, :r], bank[:META, P * (i % 4):P * (i % 4) + r])
            return ins

        @block.sync
        def _(sp):
            def weights(h):
                if h >= 2:
                    sp.wait_ge(projected, NT * (h - 1))
                for j, base in enumerate((DQ, DK, DV)):
                    sp.dma_start(Wb[h % 2][:, :, P * j:P * j + P], W[:, :, base + P * h:base + P * h + P]).then_inc(w_in[h % 2], 16)

            sp.dma_start(rel31[0:32], A["rel_bias"][31:32, :].to_broadcast([32, HEADS])).then_inc(c_in, 16)
            sp.dma_start(rel[0:32], A["rel_bias"]).then_inc(c_in, 16)
            sp.dma_start(bucket[0:33], A["bucket"]).then_inc(bk_in, 16)
            weights(0)
            weights(1)
            for h in range(HEADS):
                sp.wait_ge(bias_row, h + 1)
                sp.dma_start(skew[h].rearrange("(p c) -> p c", c=ND + 1)[:, 0:ND], vecs[:, h, :]).then_inc(skewed, 16)
            sp.wait_ge(skewed, 16 * HEADS)
            for h in range(HEADS):
                sp.dma_start(Bn[h], skew[h][P:P + P * ND].rearrange("(p c) -> p c", c=ND)[:, 0:256]).then_inc(bias_in, 16)
            for h in range(HEADS):
                sp.wait_ge(x_done, NT * (h + 1))
                for src, big, small in ((kout[h % 2], out["new_k_prompt"], out["new_k_sample"]),
                                        (v[h % 2], out["new_v_prompt"], out["new_v_sample"])):
                    sp.dma_start(big[0, 0, META:, h, :].rearrange("(i p) c -> p i c", p=P), src[:, 1:, :]).then_inc(kv_out[h % 2], 16)
                    sp.dma_start(big[0, 0, 0:META, h, :], src[0:META, 0, :]).then_inc(kv_out[h % 2], 16)
                    sp.dma_start(small[0, :, :, h, :].rearrange("b s c -> (b s) c"), src[META:FIRST, 0, :]).then_inc(kv_out[h % 2], 16)
                if h + 2 < HEADS:
                    weights(h + 2)
            for j in range(2):
                sp.wait_ge(kv_out[j], 96 * HEADS // 2)

        @block.tensor
        def _(pe):
            def product(h, i):
                bank_free(pe, ("z", h, i))
                pe.wait_ge(w_in[h % 2], 48 * (h // 2 + 1))
                for k in range(KC):
                    mm = pe.matmul(bank_of(("z", h, i))[:ROWS[i], 0:384], K["xT"][:, k, cols(i)], Wb[h % 2][:, k, :],
                                   start=(k == 0), stop=(k == KC - 1))
                mm.then_inc(projected, 1)

            def turn_qk(h, i):
                r, n = ROWS[i], NT * h + i
                pe.wait_ge(k_scaled, n + 1)
                bank_free(pe, ("x", h, i))
                bank = bank_of(("x", h, i))
                pe.transpose(bank[:, 0:r], zn[:r, n % 2, 0:P], K["ident"][:r, :r])
                pe.transpose(bank[:, P:P + r], kout[h % 2][:r, i, :], K["ident"][:r, :r]).then_inc(x_turned, 1)

            def scores(s, m):
                h, i = s // NQ, s % NQ
                r = P if i else META
                q = qz[h % 2][:, m, COL[i]:COL[i] + r]
                if m == 0:
                    pe.wait_ge(x_done, NT * h + i + 1)
                    if s:
                        pe.wait_ge(exp_done, 2 * s)
                n = P * i
                for c in range(0, n, 512):
                    w = min(512, n - c)
                    mm = pe.matmul(lg[m][:r, c:c + w], q, kT[h % 2][:, FIRST + c:FIRST + c + w], start=True, stop=True)
                if n < SEQ:
                    mm = pe.matmul(lg[m][:r, n:n + META], q, kT[h % 2][:, 0:META], start=True, stop=True)
                    mm.then_inc(logits, 1)
                elif m == 0:
                    mm.then_inc(logits, 1)

            def meta_scores(s):
                bank_free(pe, ("e", s, 0))
                h, i = s // NQ, s % NQ
                for m in range(2):
                    mm = pe.matmul(bank_of(("e", s, 0))[:, META * m:META * m + META], qz[h % 2][:, m, cols(i)],
                                   kT[h % 2][:, 0:META], start=True, stop=True)
                mm.then_inc(logits, 1)

            def turn_probabilities(s, g):
                i = s % NQ
                r = P if i else META
                pe.wait_ge(a_done, s + 1)
                bank_free(pe, ("a", s, g))
                for n in range(4 * g, min(4 * g + 4, i + 1)):
                    w = META if n == i else P
                    mm = pe.transpose(bank_of(("a", s, g))[:w, P * (n % 4):P * (n % 4) + r], Am[:r, P * n:P * n + w], K["ident"][:r, :r])
                mm.then_inc(a_turned, 1)

            def outputs(s):
                h, i = s // NQ, s % NQ
                r = P if i else META
                bank_free(pe, ("o", s, 0))
                last = a_index[("a", s, groups(s) - 1)]
                pe.wait_ge(a_act, last // 2 + 1)
                if last:
                    pe.wait_ge(a_dve, (last + 1) // 2)
                pe.wait_ge(squared, NT * h + i + 1)
                for n in range(i + 1):
                    w = META if n == i else P
                    mm = pe.matmul(bank_of(("o", s, 0))[:r, 0:P], aT[:w, n, :r], v[h % 2][:w, 0 if n == i else n + 1, :],
                                   start=(n == 0), stop=(n == i))
                mm.then_inc(o_done, 1)

            def turn_output(s):
                r = P if s % NQ else META
                pe.wait_ge(og_done, s + 1)
                bank_free(pe, ("g", s, 0))
                pe.transpose(bank_of(("g", s, 0))[:, 0:r], og[:r, s % 2, :], K["ident"][:r, :r]).then_inc(og_turned, 1)

            pe.wait_ge(bk_in, 16)
            pe.wait_ge(rel_ready, 1)
            for h in range(HEADS):
                pe.matmul(psum[:, h, 0:ND], relh[0:33, h, :], bucket[0:33], start=True, stop=True).then_inc(bias_made, 1)
            run = {"z": product, "x": turn_qk, "L": scores, "e": lambda s, _: meta_scores(s), "a": turn_probabilities,
                   "o": lambda s, _: outputs(s), "g": lambda s, _: turn_output(s)}
            for kind, a, b in zx:
                run[kind](a, b)
            pe.wait_ge(bias_row, HEADS)
            for slot in slots:
                for kind, a, b in slot:
                    run[kind](a, b)

        @block.scalar
        def _(act):
            def square(h, i):
                r, n = ROWS[i], NT * h + i
                bank = bank_of(("z", h, i))
                act.wait_ge(projected, n + 1)
                if n:
                    act.wait_ge(summed, n)
                if h >= 2:
                    act.wait_ge(o_done, NQ * (h - 1))
                    act.wait_ge(kv_out[h % 2], 96 * (h // 2))
                act.activation(v[h % 2][:r, i, :], bank[:r, 256:384], ACT.Copy)
                if i == 0:
                    act.activation(K["vS"][:r, h, :], bank[:r, 256:384], ACT.Copy)
                act.activation(sq[:r], bank[:r, 0:256], ACT.Square).then_inc(squared, 1)

            def place_qk(h, i):
                r, n = ROWS[i], NT * h + i
                bank = bank_of(("x", h, i))
                act.wait_ge(x_turned, n + 1)
                if n == 0:
                    act.wait_ge(setup, 3)
                if i == 0 and h >= 2:
                    act.wait_ge(saved, h - 1)
                for m in range(2):
                    rows = slice(64 * m, 64 * m + 64)
                    act.activation(qz[h % 2][rows, m, cols(i)], bank[rows, 0:r], ACT.Copy, scale=K["vecT"][rows, 18:19])
                act.activation(kT[h % 2][:, cols(i)], bank[:, P:P + r], ACT.Copy).then_inc(x_done, 1)

            def exps(s):
                i = s % NQ
                r = P if i else META
                n = min(P * i + META, SEQ)
                for m in range(2):
                    act.wait_ge(max_done, 2 * s + (2 if i == NQ - 1 else m + 1))
                    if m == 0 and s:
                        act.wait_ge(a_done, s)
                    if i == NQ - 1:
                        act.activation(Pm[:r, m, n:n + META], bank_of(("e", s, 0))[:r, META * m:META * m + META], ACT.Exp,
                                       bias=nmax[:r, s, m:m + 1], accum_out=sums[:r, s, 2 + m:3 + m])
                    act.activation(Pm[:r, m, 0:n], lg[m][:r, 0:n], ACT.Exp, bias=nmax[:r, s, m:m + 1],
                                   accum_out=sums[:r, s, m:m + 1]).then_inc(exp_done, 1)

            def copy_turned(s, g):
                n = a_index[("a", s, g)]
                if n % 2 == 0:
                    act.wait_ge(a_turned, n + 1)
                    if s:
                        act.wait_ge(o_done, s)
                    place_turned(lambda o, x: act.activation(o, x, ACT.Copy), s, g).then_inc(a_act, 1)

            def square_out(s):
                r = P if s % NQ else META
                act.wait_ge(o_done, s + 1)
                act.drain()
                act.activation(junk[:r], bank_of(("o", s, 0))[:r, 0:P], ACT.Square, scale=coef[:r, s, 2:3],
                               accum_out=ssq[:r, s:s + 1]).then_inc(ssq_done, 1)

            def place_out(s):
                i = s % NQ
                r = P if i else META
                act.wait_ge(og_turned, s + 1)
                act.activation(K["obT"][:, s // NQ, COL[i]:COL[i] + r], bank_of(("g", s, 0))[:, 0:r],
                               ACT.Copy, scale=K["vecT"][:, 17:18]).then_inc(ob_done, 1)

            for h in range(HEADS):
                act.wait_ge(bias_made, h + 1)
                act.activation(vecs[:, h, :], psum[:, h, 0:ND], ACT.Copy).then_inc(bias_row, 1)
            for kind, a, b in zx:
                (square if kind == "z" else place_qk)(a, b)
            for s, slot in enumerate(slots):
                for kind, a, b in slot:
                    if kind == "a":
                        copy_turned(a, b)
                    elif kind == "z":
                        square(a, b)
                if s < STEPS:
                    exps(s)
                for kind, a, b in slot:
                    if kind == "o":
                        square_out(a)
                    elif kind == "x":
                        place_qk(a, b)
                    elif kind == "g":
                        place_out(a)

        @block.gpsimd
        def _(pool):
            for h in range(2):
                pool.memset(qz[h].rearrange("p a b -> p (a b)"), 0.0).then_inc(setup, 1)
            pool.memset(K["Qs"].rearrange("p a b -> p (a b)"), 0.0).then_inc(setup, 1)
            pool.wait_ge(setup, 3)

            def power(n, h, i):
                r = ROWS[i]
                pool.wait_ge(summed, n + 1)
                pool.tensor_scalar(zs[:r, n, :], zs[:r, n, :], 1.0 / 64, EPS, ALU.mult, ALU.add)
                pool.drain()
                pool.tensor_tensor(zr[:r, n, :], zs[:r, n, :], K["half"][:r, 0:4], ALU.pow).then_inc(rstd_done, 1)

            def power_out(s):
                r = P if s % NQ else META
                pool.wait_ge(ssq_done, s + 1)
                pool.tensor_scalar(ssq[:r, s:s + 1], ssq[:r, s:s + 1], 1.0 / P, EPS, ALU.mult, ALU.add)
                pool.drain()
                pool.tensor_tensor(rr[:r, s, 0:1], ssq[:r, s:s + 1], K["half"][:r, 0:1], ALU.pow)
                pool.drain()
                pool.tensor_tensor(rr[:r, s, 1:2], rr[:r, s, 0:1], coef[:r, s, 2:3], ALU.mult).then_inc(orstd_done, 1)

            def save(h):
                pool.wait_ge(x_done, NT * h + 1)
                for m in range(2):
                    pool.tensor_copy(K["Qs"][:, DB * h:DB * h + DB, 16 * h + 8 * m:16 * h + 8 * m + 8],
                                     qz[h % 2][:, m, META:FIRST].rearrange("p (b s) -> p b s", s=DS))
                pool.tensor_copy(K["kS"][:, h, :], kT[h % 2][:, 0:FIRST]).then_inc(saved, 1)

            for kind, a, b in zx:
                if kind == "z":
                    power(NT * a + b, a, b)
            save(0)
            for s, slot in enumerate(slots):
                for kind, a, b in slot:
                    if kind == "o":
                        power_out(a)
                    elif kind == "z":
                        power(NT * a + b, a, b)
                    elif kind == "x" and b == 0:
                        save(a)

        @block.vector
        def _(dve):
            def sum_squares(h, i):
                r, n = ROWS[i], NT * h + i
                dve.wait_ge(squared, n + 1)
                dve.tensor_reduce(zs[:r, n, :], sq[:r].rearrange("p (g c) -> p g c", c=64), AX_X, ALU.add).then_inc(summed, 1)

            def normalise(h, i):
                r, n = ROWS[i], NT * h + i
                dve.wait_ge(rstd_done, n + 1)
                if n >= 2:
                    dve.wait_ge(x_turned, n - 1)
                if h >= 2:
                    dve.wait_ge(kv_out[h % 2], 96 * (h // 2))
                    dve.wait_ge(x_turned, NT * (h - 1))
                dve.tensor_tensor(zn[:r, n % 2, :].rearrange("p (g c) -> p g c", c=64),
                                  bank_of(("z", h, i))[:r, 0:256].rearrange("p (g c) -> p g c", c=64),
                                  zr[:r, n, :].unsqueeze(2).to_broadcast([r, 4, 64]), ALU.mult).then_inc(normed, 1)
                dve.drain()
                dve.tensor_tensor(kout[h % 2][:r, i, :].rearrange("p (m c) -> p m c", c=64),
                                  zn[:r, n % 2, P:2 * P].rearrange("p (m c) -> p m c", c=64),
                                  K["knorm"][:r].unsqueeze(1).to_broadcast([r, 2, 64]), ALU.mult).then_inc(k_scaled, 1)

            def maxima(s, m):
                h, i = s // NQ, s % NQ
                r = P if i else META
                dve.wait_ge(logits, 2 * s + m + 1)
                if s % NQ == 0 and m == 0:
                    dve.wait_ge(bias_in, 16 * HEADS)
                x = lg[m]
                if i == 0:
                    dve.tensor_tensor(x[:r, 0:META], x[:r, 0:META], Bn[h][:r, P:P + META], ALU.add)
                else:
                    lo = max(0, P * (i - 2))
                    w = P * i - lo
                    dve.tensor_tensor(x[:, lo:P * i], x[:, lo:P * i], Bn[h][:, 256 - w:256], ALU.add)
                if i == 1:
                    dve.tensor_tensor(x[:, P:P + META], x[:, P:P + META], Bn[h][:, P - META:P], ALU.add)
                dve.drain()
                if i == NQ - 1:
                    dve.tensor_reduce(mt[:, m, 0:1], x[:, 0:SEQ], AX_X, ALU.max, negate=True)
                    if m == 0:
                        dve.wait_ge(logits, 2 * s + 2)
                    dve.tensor_reduce(mt[:, m, 1:2], bank_of(("e", s, 0))[:, META * m:META * m + META], AX_X, ALU.max, negate=True)
                    dve.drain()
                    dve.tensor_tensor(nmax[:, s, m:m + 1], mt[:, m, 0:1], mt[:, m, 1:2], ALU.min).then_inc(max_done, 1)
                else:
                    dve.tensor_reduce(nmax[:r, s, m:m + 1], x[:r, 0:P * i + META], AX_X, ALU.max, negate=True).then_inc(max_done, 1)

            def combine(s):
                i = s % NQ
                r, n = (P if i else META), P * i + META
                dve.wait_ge(exp_done, 2 * s + 2)
                if i == NQ - 1:
                    dve.tensor_tensor(sums[:, s, 0:2], sums[:, s, 0:2], sums[:, s, 2:4], ALU.add)
                    dve.drain()
                dve.reciprocal(coef[:r, s, 2:4], sums[:r, s, 0:2])
                dve.drain()
                dve.tensor_scalar(coef[:r, s, 0:1], sums[:r, s, 0:1], coef[:r, s, 3:4], K["lam"][:r, 3:4], ALU.mult, ALU.mult)
                dve.drain()
                if s:
                    dve.wait_ge(a_turned, a_index[("a", s - 1, groups(s - 1) - 1)] + 1)
                dve.scalar_tensor_tensor(Am[:r, 0:n], Pm[:r, 1, 0:n], coef[:r, s, 0:1], Pm[:r, 0, 0:n],
                                         ALU.mult, ALU.add).then_inc(a_done, 1)

            def scale_out(s):
                r = P if s % NQ else META
                dve.wait_ge(orstd_done, s + 1)
                if s >= 2:
                    dve.wait_ge(og_turned, s - 1)
                dve.tensor_scalar(og[:r, s % 2, :], bank_of(("o", s, 0))[:r, 0:P], rr[:r, s, 1:2], None, ALU.mult).then_inc(og_done, 1)

            def copy_turned(s, g):
                n = a_index[("a", s, g)]
                if n % 2:
                    dve.wait_ge(a_turned, n + 1)
                    if s:
                        dve.wait_ge(o_done, s)
                    place_turned(dve.tensor_copy, s, g).then_inc(a_dve, 1)

            dve.wait_ge(c_in, 32)
            dve.memset(rel[32:33], NEG)
            dve.tensor_tensor(rel[0:32], rel[0:32], rel31[0:32], ALU.subtract)
            dve.drain()
            dve.tensor_copy(relh[0:33], rel[0:33].unsqueeze(2).to_broadcast([33, HEADS, P])).then_inc(rel_ready, 1)
            for kind, a, b in zx:
                if kind == "z":
                    sum_squares(a, b)
                    normalise(a, b)
            for s, slot in enumerate(slots):
                for kind, a, b in slot:
                    if kind == "a":
                        copy_turned(a, b)
                    elif kind == "z":
                        sum_squares(a, b)
                if s < STEPS:
                    maxima(s, 0)
                    maxima(s, 1)
                for kind, a, b in slot:
                    if kind == "z":
                        normalise(a, b)
                if s < STEPS:
                    combine(s)
                if 1 <= s <= STEPS:
                    scale_out(s - 1)


def phase_sample_attention(nc, A, K, sb, psum):
    PAIRS = DB // 2
    NK = PAST + FIRST
    kc, vc = (A[n][0].rearrange("n t h c -> (n t) (h c)") for n in ("cache_k", "cache_v"))
    with ExitStack() as st:
        st.enter_context(nc.cleanup_on_exit())
        sem = lambda n: nc.alloc_semaphore(name="sample_attention_" + n)
        bs_in, setup, pad_done = sem("bs_in"), sem("setup"), sem("pad_done")
        k_in = [[sem(f"k_in{b}{q}") for q in range(2)] for b in range(2)]
        v_in = [[sem(f"v_in{b}{q}") for q in range(2)] for b in range(2)]
        turned, t_act, t_dve, scored, max_done, exp_done, c_done, at_done, ats_done, atn_done, o_done, ssq_done, rstd_done, og_done, og_turned, ob_done = (
            sem(n) for n in ("turned", "t_act", "t_dve", "scored", "max_done", "exp_done", "c_done", "at_done", "ats_done", "atn_done", "o_done", "ssq_done", "rstd_done", "og_done", "og_turned", "ob_done"))
        table = K["table"]
        Kp = [sb(NPG, 512) for _ in range(2)]
        Vp = [[sb(NPG, 512) for _ in range(2)] for _ in range(2)]
        kTp = sb(2 * HEADS, 512)
        BS, BSn = sb(P + DS), sb(PAIRS, FIRST)
        Pr, C = sb(NK), sb(64)
        aTs, aTn = sb(NPG * 64 + 32), sb(64 + 32)
        lamrow, nmax, sums, rs = sb(2), sb(PAIRS), sb(PAIRS), sb(PAIRS)
        ssq, rr = sb(PAIRS, 2), sb(PAIRS, 2)
        junk, og = sb(P), sb(2, P)
        block = st.enter_context(nc.Block())
        logits = psum[:, 0:3, :].rearrange("p a b -> p (a b)")

        def page(e, b, j):
            r = e.value_load(table[0:1, NPG * b + j:NPG * b + j + 1], min_val=0, max_val=A["cache_k"].shape[1] - 1)
            return bass.ds(r * PAGE, PAGE)

        @block.sync
        def _(sp):
            for p in range(PAIRS):
                for b2 in range(2):
                    for j in range(NPG):
                        if p and j % 4 == 0:
                            sp.wait_ge(turned, 16 * (p - 1) + 8 * b2 + j + 4)
                        sp.dma_start(Kp[b2][:, j, :], kc[page(sp, 2 * p + b2, j), :]).then_inc(k_in[b2][j // 4], 16)
                if p == 0:
                    for r0 in range(0, P, DS):
                        near = K["skew"][r0 // (2 * DS) % HEADS][P:P + DS * ND].rearrange("(p c) -> p c", c=ND)
                        sp.dma_start(BS[r0:r0 + DS, :], near[:, 0:P + DS]).then_inc(bs_in, 16)

        @block.tensor
        def _(pe):
            def turn(n):
                b2, half = n // NPG % 2, n // 4 % 2
                if n % 4 == 0:
                    pe.wait_ge(k_in[b2][half], 64 * (n // (2 * NPG) + 1))
                if n >= 2:
                    pe.wait_ge(t_dve if n % 2 else t_act, n // 2)
                for h in range(HEADS):
                    mm = pe.transpose(psum[:, 3 + n % 2, P * h:P * h + P], Kp[b2][:, n % NPG, P * h:P * h + P], K["ident"])
                mm.then_inc(turned, 1)

            def turn_and_score(g):
                p, b2, half = g // 4, g // 2 % 2, g % 2
                for h in range(HEADS):
                    if g + 1 < 4 * PAIRS:
                        turn(4 * g + 4 + h)
                    if h == 0:
                        pe.wait_ge(t_act, 2 * g + 2)
                        pe.wait_ge(t_dve, 2 * g + 2)
                        if p and g % 4 == 0:
                            pe.wait_ge(exp_done, p)
                    mm = pe.matmul(logits[64 * b2:64 * b2 + 64, 512 * half:512 * half + 512],
                                   K["Qs"][:, DB * h + 2 * p + b2, :], kTp[:, HEADS * half + h, :],
                                   start=(h == 0), stop=(h == HEADS - 1))
                if half == 1:
                    for h in range(HEADS):
                        mm = pe.matmul(logits[64 * b2:64 * b2 + 64, PAST:NK], K["Qs"][:, DB * h + 2 * p + b2, :],
                                       K["kS"][:, h, :], start=(h == 0), stop=(h == HEADS - 1))
                mm.then_inc(scored, 1)

            def outputs(p):
                pe.wait_ge(c_done, p + 1)
                if p:
                    pe.wait_ge(ats_done, p)
                    pe.wait_ge(atn_done, p)
                    pe.wait_ge(ob_done, p)
                for j in range(NPG):
                    pe.matmul(psum[:, 5, 64 * j:64 * j + 64], Pr[:, P * j:P * j + P], C, start=True, stop=True)
                pe.matmul(psum[0:FIRST, 6, 0:64], Pr[:, PAST:NK], C, start=True, stop=True).then_inc(at_done, 1)
                pe.wait_ge(ats_done, p + 1)
                pe.wait_ge(atn_done, p + 1)
                if p == 0:
                    pe.wait_ge(pad_done, 2)
                for b2 in range(2):
                    pe.wait_ge(v_in[p % 2][b2], 128 * (p // 2 + 1))
                    for j in range(NPG + 1):
                        for h in range(HEADS):
                            c = 32 * b2 + 8 * h
                            o = psum[32 * h:32 * h + 32, 7, P * b2:P * b2 + P]
                            if j < NPG:
                                pe.matmul(o, aTs[:, 64 * j + c:64 * j + c + 32], Vp[p % 2][b2][:, j, P * h:P * h + P],
                                          start=(j == 0), stop=False, skip_group_check=True)
                            else:
                                mm = pe.matmul(o, aTn[0:FIRST, c:c + 32], K["vS"][0:FIRST, h, :], start=False, stop=True,
                                               skip_group_check=True)
                mm.then_inc(o_done, 1)

            def turn_outputs(p):
                pe.wait_ge(og_done, p + 1)
                for b2 in range(2):
                    mm = pe.transpose(psum[:, 6, P + P * b2:2 * P + P * b2], og[:, b2, :], K["ident"])
                mm.then_inc(og_turned, 1)

            for n in range(4):
                turn(n)
            for g in range(4):
                turn_and_score(g)
            for p in range(PAIRS):
                if p + 1 < PAIRS:
                    turn_and_score(4 * p + 4)
                if p:
                    turn_outputs(p - 1)
                if p + 1 < PAIRS:
                    for g in range(4 * p + 5, 4 * p + 8):
                        turn_and_score(g)
                outputs(p)
            turn_outputs(PAIRS - 1)

        def turned_by(p, engine):
            return range((16 * p + 4 if p else 0) + engine, min(16 * p + 20, 16 * PAIRS), 2)

        def place_turned(copy, n):
            half, j = n // 4 % 2, n % 4
            return copy(kTp[:, HEADS * half:HEADS * half + HEADS, P * j:P * j + P],
                        psum[:, 3 + n % 2, :].rearrange("p (h c) -> p h c", c=P))

        def turned_free(e, n):
            if n >= 8:
                e.wait_ge(scored, n // 4 - 1)

        @block.scalar
        def _(act):
            def pages(ns):
                for n in ns:
                    act.wait_ge(turned, n + 1)
                    turned_free(act, n)
                    place_turned(lambda o, x: act.activation(o, x, ACT.Copy), n).then_inc(t_act, 1)

            def exps(p):
                act.wait_ge(max_done, p + 1)
                if p:
                    act.wait_ge(at_done, p)
                act.activation(Pr, logits[:, 0:NK], ACT.Exp, bias=nmax[:, p:p + 1], accum_out=sums[:, p:p + 1]).then_inc(exp_done, 1)

            def weights(p):
                act.wait_ge(at_done, p + 1)
                if p:
                    act.wait_ge(o_done, p)
                act.activation(aTs[:, 0:NPG * 64], psum[:, 5, :], ACT.Copy).then_inc(ats_done, 1)

            def squares(p):
                act.wait_ge(o_done, p + 1)
                for b2 in range(2):
                    act.drain()
                    ins = act.activation(junk, psum[:, 7, P * b2:P * b2 + P], ACT.Square, accum_out=ssq[:, p, b2:b2 + 1])
                ins.then_inc(ssq_done, 1)

            def place_outputs(p):
                act.wait_ge(og_turned, p + 1)
                for b2 in range(2):
                    c = META + DS * (2 * p + b2)
                    ins = act.activation(K["obT"][:, :, c:c + DS],
                                         psum[:, 6, P + P * b2:2 * P + P * b2].rearrange("p (h s) -> p h s", s=32)[:, :, 0:DS],
                                         ACT.Copy, scale=K["vecT"][:, 17:18])
                ins.then_inc(ob_done, 1)

            pages(turned_by(0, 0))
            exps(0)
            for p in range(PAIRS):
                ns = turned_by(p + 1, 0)
                pages(ns[:2])
                if p:
                    place_outputs(p - 1)
                pages(ns[2:])
                weights(p)
                if p + 1 < PAIRS:
                    exps(p + 1)
                squares(p)
            place_outputs(PAIRS - 1)

        @block.gpsimd
        def _(pool):
            def values(p):
                for b2 in range(2):
                    for j in range(NPG):
                        pool.dma_start(Vp[p % 2][b2][:, j, :], vc[page(pool, 2 * p + b2, j), :]).then_inc(v_in[p % 2][b2], 16)

            pool.memset(BSn.rearrange("p a b -> p (a b)"), NEG).then_inc(setup, 1)
            pool.memset(aTs[:, NPG * 64:], 0.0).then_inc(pad_done, 1)
            pool.memset(aTn[:, 64:], 0.0).then_inc(pad_done, 1)
            pool.wait_ge(k_in[0][1], 64)
            values(0)
            pool.wait_ge(k_in[1][1], 64)
            values(1)
            for p in range(PAIRS):
                pool.wait_ge(ssq_done, p + 1)
                pool.tensor_scalar(ssq[:, p, :], ssq[:, p, :], 1.0 / P, EPS, ALU.mult, ALU.add)
                pool.drain()
                pool.tensor_tensor(rr[:, p, :], ssq[:, p, :], K["half"][:, 0:2], ALU.pow).then_inc(rstd_done, 1)
                if p + 2 < PAIRS:
                    pool.wait_ge(o_done, p + 1)
                    values(p + 2)

        @block.vector
        def _(dve):
            def pages(p):
                for n in turned_by(p, 1):
                    dve.wait_ge(turned, n + 1)
                    turned_free(dve, n)
                    place_turned(dve.tensor_copy, n).then_inc(t_dve, 1)

            def maxima(p):
                dve.wait_ge(scored, 4 * p + 4)
                near = logits[:, PAST - P:PAST]
                dve.tensor_tensor(near, near, BS[:, 0:P], ALU.add)
                dve.tensor_tensor(logits[:, PAST:NK], logits[:, PAST:NK], BSn[:, p, :], ALU.add)
                dve.drain()
                dve.tensor_reduce(nmax[:, p:p + 1], logits[:, 0:NK], AX_X, ALU.max, negate=True).then_inc(max_done, 1)

            def weights(p):
                dve.wait_ge(exp_done, p + 1)
                dve.reciprocal(rs[:, p:p + 1], sums[:, p:p + 1])
                dve.drain()
                if p:
                    dve.wait_ge(at_done, p)
                dve.tensor_scalar(C, K["combine"][:, 0:64], rs[:, p:p + 1], lamrow[:, 0:1], ALU.mult, ALU.mult).then_inc(c_done, 1)

            def own_weights(p):
                dve.wait_ge(at_done, p + 1)
                if p:
                    dve.wait_ge(o_done, p)
                dve.tensor_copy(aTn[0:FIRST, 0:64], psum[0:FIRST, 6, 0:64]).then_inc(atn_done, 1)

            def scale_outputs(p):
                dve.wait_ge(rstd_done, p + 1)
                if p:
                    dve.wait_ge(og_turned, p)
                for b2 in range(2):
                    ins = dve.tensor_scalar(og[:, b2, :], psum[:, 7, P * b2:P * b2 + P], rr[:, p, b2:b2 + 1], None, ALU.mult)
                ins.then_inc(og_done, 1)

            pages(0)
            dve.tensor_scalar(lamrow[:, 1:2], K["combine"][:, 65:66], K["lam"][:, 3:4], None, ALU.mult)
            dve.wait_ge(bs_in, 16 * 16)
            dve.wait_ge(setup, 1)
            dve.drain()
            dve.tensor_tensor(lamrow[:, 0:1], K["combine"][:, 64:65], lamrow[:, 1:2], ALU.subtract)
            for p in range(PAIRS):
                for b2 in range(2):
                    c = META + DS * (2 * p + b2)
                    dve.tensor_copy(BSn[64 * b2:64 * b2 + 64, p, c:c + DS], BS[64 * b2:64 * b2 + 64, P:P + DS])
            dve.drain()
            maxima(0)
            weights(0)
            for p in range(PAIRS):
                if p + 1 < PAIRS:
                    pages(p + 1)
                own_weights(p)
                if p + 1 < PAIRS:
                    maxima(p + 1)
                    weights(p + 1)
                scale_outputs(p)


def phase_merge(nc, A, K, sb, psum, split):
    W = A["w_in"][0].rearrange("(k p) n -> p k n", p=P)
    WA, WB = (A[n][0].rearrange("(k p) n -> p k n", p=P) for n in ("w_hg_out", "w_da_out"))
    UNITS = KC * 3
    with ExitStack() as st:
        st.enter_context(nc.cleanup_on_exit())
        sem = lambda n: nc.alloc_semaphore(name="merge_" + n)
        w_in = [sem("w_in0"), sem("w_in1")]
        produced, gated, merged = sem("produced"), sem("gated"), sem("merged")
        x_rounded, x_split, w_rounded, w_split = sem("x_rounded"), sem("x_split"), sem("w_rounded"), sem("w_split")
        zeroed, zeros_out, zero = sem("zeroed"), sem("zeros_out"), sb(D)
        Wg = [sb(KC, 256) for _ in range(2)]
        Wy = [sb(HEADS, 256) for _ in range(2)]
        g = [sb(2, CH) for _ in range(2)]
        view = lambda start, k, n: split[:, start:start + k * n].rearrange("p (a b) -> p a b", b=n)
        xh, xl = view(0, KC, TOK), view(KC * TOK, KC, TOK)
        wh, wl = ([view(2 * KC * TOK + KC * 256 * (2 * part + b), KC, 256) for b in range(2)] for part in range(2))
        block = st.enter_context(nc.Block())
        chunk = lambda n: slice(CH * n, CH * n + CH)

        @block.sync
        def _(sp):
            for c in range(KC):
                if c >= 2:
                    sp.wait_ge(produced, 3 * (c - 1))
                    sp.wait_ge(w_split, c - 1)
                for j, (src, base) in enumerate(((W, GA), (W, GB), (WA, 0), (WB, 0))):
                    dst = (Wg if j < 2 else Wy)[c % 2][:, :, P * (j % 2):P * (j % 2) + P]
                    sp.dma_start(dst, src[:, :, base + P * c:base + P * c + P]).then_inc(w_in[c % 2], 16)
                if c == 1:
                    sp.wait_ge(zeroed, 1)
                    sp.dma_start(K["y_dram"][P * FEWEST:, :].rearrange("(t p) c -> p t c", p=P),
                                 zero.unsqueeze(1).to_broadcast([P, SLOTS - FEWEST, D])).then_inc(zeros_out, 16)
            sp.wait_ge(zeros_out, 16)

        @block.gpsimd
        def _(pool):
            pool.memset(zero, 0.0).then_inc(zeroed, 1)

        @block.tensor
        def _(pe):
            for u in range(UNITS):
                c, n = u // 3, u % 3
                banks = [psum[:, 4 * (u % 2) + j, 0:CH] for j in range(4)]
                if n == 0:
                    pe.wait_ge(w_in[c % 2], 64 * (c // 2 + 1))
                if u >= 2:
                    pe.wait_ge(merged, u - 1)
                for j, src in enumerate((K["oaT"], K["obT"])):
                    for k in range(HEADS):
                        pe.matmul(banks[2 + j], Wy[c % 2][:, k, P * j:P * j + P], src[:, k, chunk(n)], start=(k == 0), stop=(k == HEADS - 1))
                pe.wait_ge(x_split, n + 1)
                pe.wait_ge(w_split, c + 1)
                for j in range(2):
                    ch = slice(P * j, P * j + P)
                    for k in range(KC):
                        pe.matmul(banks[j], wh[c % 2][:, k, ch], xh[:, k, chunk(n)], start=(k == 0), stop=False)
                        pe.matmul(banks[j], wh[c % 2][:, k, ch], xl[:, k, chunk(n)], start=False, stop=False)
                        mm = pe.matmul(banks[j], wl[c % 2][:, k, ch], xh[:, k, chunk(n)], start=False, stop=(k == KC - 1))
                mm.then_inc(produced, 1)

        @block.scalar
        def _(act):
            def round_x(n):
                act.activation(xh[:, :, chunk(n)], K["xT"][:, :, chunk(n)], ACT.Copy).then_inc(x_rounded, 1)

            def round_w(c):
                act.wait_ge(w_in[c % 2], 64 * (c // 2 + 1))
                if c >= 2:
                    act.wait_ge(produced, 3 * (c - 1))
                act.activation(wh[c % 2], Wg[c % 2], ACT.Copy).then_inc(w_rounded, 1)

            round_x(0)
            round_x(1)
            round_w(0)
            round_x(2)
            for u in range(UNITS):
                act.wait_ge(produced, u + 1)
                if u >= 2:
                    act.wait_ge(merged, u - 1)
                for j in range(2):
                    ins = act.activation(g[u % 2][:, j, :], psum[:, 4 * (u % 2) + j, 0:CH], ACT.Sigmoid)
                ins.then_inc(gated, 1)
                if u % 3 == 0 and u // 3 + 1 < KC:
                    round_w(u // 3 + 1)

        @block.vector
        def _(dve):
            def rest_x(n):
                dve.wait_ge(x_rounded, n + 1)
                dve.tensor_tensor(xl[:, :, chunk(n)], K["xT"][:, :, chunk(n)], xh[:, :, chunk(n)].bitcast(F32), ALU.subtract).then_inc(x_split, 1)

            def rest_w(c):
                dve.wait_ge(w_rounded, c + 1)
                dve.tensor_tensor(wl[c % 2], Wg[c % 2], wh[c % 2].bitcast(F32), ALU.subtract).then_inc(w_split, 1)

            rest_x(0)
            rest_x(1)
            rest_w(0)
            rest_x(2)
            dve.drain()
            for u in range(UNITS):
                b = g[u % 2]
                dve.wait_ge(gated, u + 1)
                for j in range(2):
                    dve.tensor_tensor(b[:, j, :], b[:, j, :], psum[:, 4 * (u % 2) + 2 + j, 0:CH], ALU.mult)
                dve.drain()
                dve.tensor_tensor(K["mT"][:, u // 3, chunk(u % 3)], b[:, 0, :], b[:, 1, :], ALU.add).then_inc(merged, 1)
                if u % 3 == 0 and u // 3 + 1 < KC:
                    rest_w(u // 3 + 1)


def phase_output(nc, A, K, sb, psum, split):
    with ExitStack() as st:
        st.enter_context(nc.cleanup_on_exit())
        sem = lambda n: nc.alloc_semaphore(name="output_" + n)
        w_in, wr_in, setup = [sem(f"w_in{b}") for b in range(4)], sem("wr_in"), sem("setup")
        w_rounded, w_split, m_rounded, m_split = sem("w_rounded"), sem("w_split"), sem("m_rounded"), sem("m_split")
        x_in = [sem("x_in0"), sem("x_in1")]
        h_made, h_done, ssq_done, rstd_done, scaled, hn_done, turned, t_done, routed, r_done = (
            sem(n) for n in ("h_made", "h_done", "ssq_done", "rstd_done", "scaled", "hn_done", "turned", "t_done", "routed", "r_done"))
        hn_out = [sem("hn_out0"), sem("hn_out1")]
        Wo, ssq, rstd = K["Wo"], K["ssq2"], K["rstd2"]
        x, hn, hs, w2, wr, hT, junk = sb(2, D), sb(2, D), sb(D), sb(D), sb(KC, P), sb(KC, P), sb(D)
        view = lambda start, n: split[:, start:start + KC * n].rearrange("p (a b) -> p a b", b=n)
        wh, wl = view(0, D), view(KC * D, D)
        mh, ml = ([view(2 * KC * D + KC * P * (2 * part + b), P) for b in range(2)] for part in range(2))
        block = st.enter_context(nc.Block())

        @block.sync
        def _(sp):
            for k in range(KC):
                if k >= 4:
                    sp.wait_ge(w_split, k - 3)
                sp.dma_start(Wo[:, k % 4, :], A["w_o"][0, P * k:P * k + P, :]).then_inc(w_in[k % 4], 16)
            sp.wait_ge(setup, 1)
            sp.dma_start(wr[:, :, 0:4], A["w_router_group"][0].rearrange("(k p) n -> p k n", p=P)).then_inc(wr_in, 16)
            sp.dma_start(wr[:, :, 4:20], A["w_router_expert"][0].rearrange("(k p) n -> p k n", p=P)).then_inc(wr_in, 16)
            sp.dma_start(w2, A["norm2_w"].to_broadcast([P, D])).then_inc(wr_in, 16)
            for i in range(NT):
                if i >= 2:
                    sp.wait_ge(h_done, i - 1)
                if i == 0:
                    sp.dma_start(x[0:META, 0, :], A["meta_tokens"]).then_inc(x_in[0], 16)
                    sp.dma_start(x[META:FIRST, 0, :], A["x_sample"].rearrange("a b d -> (a b) d")).then_inc(x_in[0], 16)
                else:
                    sp.dma_start(x[:, i % 2, :], A["x_prompt"][0, P * (i - 1):P * i, :]).then_inc(x_in[i % 2], 16)
                if i >= 1:
                    j = i - 1
                    sp.wait_ge(hn_done, j + 1)
                    sp.dma_start(K["hn_dram"][cols(j), :], hn[:ROWS[j], j % 2, :]).then_inc(hn_out[j % 2], 16)
            j = NT - 1
            sp.wait_ge(hn_done, j + 1)
            sp.dma_start(K["hn_dram"][cols(j), :], hn[:, j % 2, :]).then_inc(hn_out[j % 2], 16)
            for q in range(2):
                sp.wait_ge(hn_out[q], 16 * (5 - q))

        @block.tensor
        def _(pe):
            def project(i):
                r = ROWS[i]
                if i >= 2:
                    pe.wait_ge(h_done, i - 1)
                pe.wait_ge(m_split, i + 1)
                for k in range(KC):
                    if i == 0:
                        pe.wait_ge(w_split, k + 1)
                    for j in range(2):
                        bank, c = psum[:r, 2 * (i % 2) + j, :], slice(512 * j, 512 * j + 512)
                        pe.matmul(bank, mh[i % 2][:, k, :r], wh[:, k, c], start=(k == 0), stop=False)
                        pe.matmul(bank, mh[i % 2][:, k, :r], wl[:, k, c], start=False, stop=False)
                        mm = pe.matmul(bank, ml[i % 2][:, k, :r], wh[:, k, c], start=False, stop=(k == KC - 1))
                mm.then_inc(h_made, 1)

            def turn(i):
                r = ROWS[i]
                pe.wait_ge(hn_done, i + 1)
                if i:
                    pe.wait_ge(t_done, i)
                for k in range(KC):
                    mm = pe.transpose(psum[:, 4 + k // 4, P * (k % 4):P * (k % 4) + r], hn[:r, i % 2, P * k:P * k + P], K["ident"][:r, :r])
                mm.then_inc(turned, 1)

            def route(i):
                r = ROWS[i]
                pe.wait_ge(t_done, i + 1)
                if i:
                    pe.wait_ge(r_done, i)
                else:
                    pe.wait_ge(wr_in, 48)
                for k in range(KC):
                    mm = pe.matmul(psum[:r, 6, 0:P], hT[:, k, :r], wr[:, k, :], start=(k == 0), stop=(k == KC - 1))
                mm.then_inc(routed, 1)

            for i in range(NT + 2):
                if i < NT:
                    project(i)
                if i >= 2:
                    route(i - 2)
                if 1 <= i <= NT:
                    turn(i - 1)

        @block.scalar
        def _(act):
            def norm(i):
                r = ROWS[i]
                act.wait_ge(h_done, i + 1)
                act.drain()
                act.activation(junk[:r], K["h"][:r, i, :], ACT.Square, accum_out=ssq[:r, i:i + 1]).then_inc(ssq_done, 1)
                act.wait_ge(rstd_done, i + 1)
                if i:
                    act.wait_ge(hn_done, i)
                act.activation(hs[:r], K["h"][:r, i, :], ACT.Copy, scale=rstd[:r, i:i + 1]).then_inc(scaled, 1)

            def place(i):
                act.wait_ge(turned, i + 1)
                if i:
                    act.wait_ge(routed, i)
                act.activation(hT[:, :, :ROWS[i]], psum[:, 4:6, :].rearrange("p a (b c) -> p (a b) c", c=P)[:, :, :ROWS[i]], ACT.Copy).then_inc(t_done, 1)

            def round_m(i):
                if i >= 2:
                    act.wait_ge(h_made, i - 1)
                act.activation(mh[i % 2][:, :, :ROWS[i]], K["mT"][:, :, cols(i)], ACT.Copy).then_inc(m_rounded, 1)

            round_m(0)
            for k in range(KC):
                act.wait_ge(w_in[k % 4], 16 * (k // 4 + 1))
                act.activation(wh[:, k, :], Wo[:, k % 4, :], ACT.Copy).then_inc(w_rounded, 1)
            round_m(1)
            for i in range(NT + 1):
                if i < NT:
                    norm(i)
                if i + 2 < NT:
                    round_m(i + 2)
                if i >= 1:
                    place(i - 1)

        @block.gpsimd
        def _(pool):
            pool.memset(wr.rearrange("p a b -> p (a b)"), 0.0).then_inc(setup, 1)
            for i in range(NT):
                r = ROWS[i]
                pool.wait_ge(ssq_done, i + 1)
                pool.tensor_scalar(ssq[:r, i:i + 1], ssq[:r, i:i + 1], 1.0 / D, EPS, ALU.mult, ALU.add)
                pool.drain()
                pool.tensor_tensor(rstd[:r, i:i + 1], ssq[:r, i:i + 1], K["half"][:r, 0:1], ALU.pow).then_inc(rstd_done, 1)

        @block.vector
        def _(dve):
            def rest_m(i):
                r = ROWS[i]
                dve.wait_ge(m_rounded, i + 1)
                dve.tensor_tensor(ml[i % 2][:, :, :r], K["mT"][:, :, cols(i)], mh[i % 2][:, :, :r].bitcast(F32), ALU.subtract).then_inc(m_split, 1)

            rest_m(0)
            for k in range(KC):
                dve.wait_ge(w_rounded, k + 1)
                dve.tensor_tensor(wl[:, k, :], Wo[:, k % 4, :], wh[:, k, :].bitcast(F32), ALU.subtract).then_inc(w_split, 1)
            rest_m(1)
            dve.memset(K["logit"].rearrange("p a b -> p (a b)"), 0.0)
            dve.wait_ge(wr_in, 48)
            for i in range(NT + 2):
                if i < NT:
                    r = ROWS[i]
                    dve.wait_ge(h_made, i + 1)
                    dve.wait_ge(x_in[i % 2], 32 if i == 0 else 16 * (i // 2 + (2 if i % 2 == 0 else 1)))
                    dve.tensor_tensor(K["h"][:r, i, :], psum[:r, 2 * (i % 2):2 * (i % 2) + 2, :].rearrange("p a b -> p (a b)"),
                                      x[:r, i % 2, :], ALU.add).then_inc(h_done, 1)
                if 1 <= i <= NT:
                    j = i - 1
                    r = ROWS[j]
                    dve.wait_ge(scaled, j + 1)
                    if j >= 2:
                        dve.wait_ge(turned, j - 1)
                        dve.wait_ge(hn_out[j % 2], 16 * (j // 2))
                    dve.tensor_tensor(hn[:r, j % 2, :], hs[:r], w2[:r], ALU.mult).then_inc(hn_done, 1)
                if i + 2 < NT:
                    rest_m(i + 2)
                if i >= 2:
                    j = i - 2
                    dve.wait_ge(routed, j + 1)
                    dve.tensor_copy(K["logit"][:ROWS[j], j, :], psum[:ROWS[j], 6, 0:20]).then_inc(r_done, 1)


def phase_route(nc, A, K, sb, psum):
    G, PE_ = 4, 4
    with ExitStack() as st:
        st.enter_context(nc.cleanup_on_exit())
        sem = lambda n: nc.alloc_semaphore(name="route_" + n)
        c_in, setup, exp_in, exp_out, counted, prefixed, slots_done, zeroed, scattered, table_in, t_turned = (sem(n) for n in (
            "c_in", "setup", "exp_in", "exp_out", "counted", "prefixed", "slots_done", "zeroed", "scattered", "table_in", "t_turned"))
        bias, consts, strict, ones, tok, valid, emask = sb(20), sb(53), sb(P), sb(P), sb(NT), sb(NT), sb(E, NT)
        gm, eg, gs = sb(NT), sb(NT, G), sb(NT)
        ohg, es16, es, e2 = sb(NT, G), sb(NT, 16), sb(NT, PE_), sb(NT, PE_)
        oh = [sb(NT, PE_) for _ in range(2)]
        mx, tm = sb(2, NT), sb(NT)
        OH = [sb(NT, E) for _ in range(2)]
        M, pre, tot = sb(NT, E), sb(NT, E), sb(E, NT)
        inc, cmp9, ntile, incl, excl, sm, sl = sb(E, NT), sb(E, NT), sb(E), sb(E), sb(E), sb(NT, E), sb(NT)
        lt, eid, eidb, step, last, zero = sb(SLOTS, E), sb(SLOTS), sb(SLOTS), sb(SLOTS), sb(1), sb(P)
        rows = sb(P)
        block = st.enter_context(nc.Block())
        pri, steps128, jj = consts[:, 0:4], consts[:, 4:13], consts[:, 13:13 + SLOTS]

        @block.sync
        def _(sp):
            sp.dma_start(bias[:, 0:4], A["b_router_group"].to_broadcast([P, 4])).then_inc(c_in, 16)
            sp.dma_start(bias[:, 4:20], A["b_router_expert"].to_broadcast([P, 16])).then_inc(c_in, 16)
            for dst, n in ((consts, "experts"), (strict, "strict"), (tok, "token_id"), (valid, "valid"), (emask.rearrange("p a b -> p (a b)"), "expert_mask")):
                sp.dma_start(dst, A[n]).then_inc(c_in, 16)
            sp.wait_ge(setup, 1)
            sp.dma_start(K["slot_token"].rearrange("(a b) c -> a (b c)", b=P), zero[0:SLOTS, :]).then_inc(zeroed, 16)
            for e in range(BUFFERS):
                load_expert(sp, A, K, e, e)
            sp.wait_ge(scattered, 2 * 16 * NT)
            sp.dma_start(rows[0:SLOTS, :], K["slot_token"].rearrange("(a b) c -> a (b c)", b=P)).then_inc(table_in, 16)
            sp.wait_ge(table_in, 16)

        @block.gpsimd
        def _(pool):
            pool.wait_ge(c_in, 16 * 7)
            pool.wait_ge(zeroed, 16)
            pool.wait_ge(slots_done, 1)
            for i in range(NT):
                for j in range(2):
                    pool.indirect_dma_start(out=K["slot_token"], out_offset=bass.IndirectOffsetOnAxis(ap=K["slot"][:ROWS[i], NT * j + i:NT * j + i + 1], axis=0),
                                            in_=tok[:ROWS[i], i:i + 1], in_offset=None).then_inc(scattered, 16)

        @block.scalar
        def _(act):
            act.wait_ge(exp_in, 1)
            act.activation(eg, eg, ACT.Exp).then_inc(exp_out, 1)
            act.wait_ge(exp_in, 2)
            act.activation(tm, tm, ACT.Exp).then_inc(exp_out, 1)

        @block.tensor
        def _(pe):
            pe.wait_ge(counted, 1)
            m = M.rearrange("p a b -> p (a b)")
            pe.matmul(psum[:, 0, 0:NT * E], strict, m, start=True, stop=True)
            pe.matmul(psum[:, 1, 0:NT * E], ones, m, start=True, stop=True).then_inc(prefixed, 1)
            pe.wait_ge(table_in, 16)
            pe.transpose(psum[:, 2, 0:SLOTS], rows[0:SLOTS, :], K["ident"][0:SLOTS, 0:SLOTS]).then_inc(t_turned, 1)

        @block.vector
        def _(dve):
            D_ = dve.drain
            dve.memset(zero, 0.0).then_inc(setup, 1)
            dve.memset(ones, 1.0)
            dve.wait_ge(c_in, 16 * 7)
            L = K["logit"]
            dve.tensor_tensor(L, L, bias.unsqueeze(1).to_broadcast([P, NT, 20]), ALU.add)
            D_()

            def first_of(dst, x, m, n):
                dve.tensor_tensor(dst, x, m.unsqueeze(2).to_broadcast([P, NT, n]), ALU.is_equal)
                D_()
                dve.tensor_tensor(dst, dst, pri.unsqueeze(1).to_broadcast([P, NT, n]), ALU.mult)
                D_()
                dve.tensor_reduce(gs, dst, AX_X, ALU.max)
                D_()
                dve.tensor_tensor(dst, dst, gs.unsqueeze(2).to_broadcast([P, NT, n]), ALU.is_equal)
                D_()

            gl = L[:, :, 0:4]
            dve.tensor_reduce(gm, gl, AX_X, ALU.max)
            D_()
            dve.tensor_tensor(eg, gl, gm.unsqueeze(2).to_broadcast([P, NT, G]), ALU.subtract).then_inc(exp_in, 1)
            first_of(ohg, gl, gm, G)
            dve.tensor_tensor(es16.rearrange("p n (g e) -> p n g e", g=G), L[:, :, 4:20].rearrange("p n (g e) -> p n g e", g=G),
                              ohg.unsqueeze(3).to_broadcast([P, NT, G, PE_]), ALU.mult)
            D_()
            dve.tensor_reduce(es, es16.rearrange("p n (g e) -> p n e g", g=G), AX_X, ALU.add)
            D_()
            dve.tensor_reduce(mx[:, 0, :], es, AX_X, ALU.max)
            D_()
            first_of(oh[0], es, mx[:, 0, :], PE_)
            dve.scalar_tensor_tensor(e2, oh[0], NEG, es, ALU.mult, ALU.add)
            D_()
            dve.tensor_reduce(mx[:, 1, :], e2, AX_X, ALU.max)
            D_()
            first_of(oh[1], e2, mx[:, 1, :], PE_)
            dve.tensor_tensor(tm, mx[:, 1, :], mx[:, 0, :], ALU.subtract).then_inc(exp_in, 1)
            dve.tensor_tensor(ohg, ohg, valid.unsqueeze(2).to_broadcast([P, NT, G]), ALU.mult)
            D_()
            for j in range(2):
                dve.tensor_tensor(OH[j].rearrange("p n (g e) -> p n g e", g=G), ohg.unsqueeze(3).to_broadcast([P, NT, G, PE_]),
                                  oh[j].unsqueeze(2).to_broadcast([P, NT, G, PE_]), ALU.mult)
            D_()
            dve.tensor_tensor(M, OH[0], OH[1], ALU.add).then_inc(counted, 1)
            dve.wait_ge(exp_out, 2)
            dve.tensor_reduce(gs, eg, AX_X, ALU.add)
            D_()
            dve.tensor_scalar(gm, tm, 1.0, None, ALU.add)
            D_()
            dve.tensor_tensor(gm, gm, gs, ALU.mult)
            D_()
            dve.reciprocal(K["weight"][:, 0, :], gm)
            D_()
            dve.tensor_tensor(K["weight"][:, 1, :], K["weight"][:, 0, :], tm, ALU.mult)
            dve.wait_ge(prefixed, 1)
            dve.tensor_copy(tot, psum[:, 1, 0:NT * E].rearrange("p (n e) -> p e n", e=E))
            D_()
            flat = lambda x: x.rearrange("p a b -> p (a b)")
            dve.tensor_tensor_scan(flat(inc), flat(emask), flat(tot), 0.0, ALU.mult, ALU.add)
            D_()
            dve.tensor_tensor(cmp9, inc[:, :, NT - 1:NT].to_broadcast([P, E, NT]), steps128.unsqueeze(1).to_broadcast([P, E, NT]), ALU.is_gt)
            D_()
            dve.tensor_reduce(ntile, cmp9, AX_X, ALU.add)
            D_()
            dve.tensor_tensor_scan(incl, ones[:, 0:E], ntile, 0.0, ALU.mult, ALU.add)
            dve.tensor_tensor(inc, inc, tot, ALU.subtract)
            D_()
            dve.tensor_tensor(excl, incl, ntile, ALU.subtract)
            dve.tensor_tensor(sm, psum[:, 0, 0:NT * E].rearrange("p (n e) -> p n e", e=E), inc.rearrange("p e n -> p n e"), ALU.add)
            D_()
            dve.tensor_scalar(excl, excl, float(P), None, ALU.mult)
            D_()
            dve.tensor_tensor(sm, sm, excl.unsqueeze(1).to_broadcast([P, NT, E]), ALU.add)
            D_()
            for j in range(2):
                dve.tensor_tensor(OH[j], OH[j], sm, ALU.mult)
                D_()
                dve.tensor_reduce(sl, OH[j], AX_X, ALU.add)
                D_()
                ins = dve.tensor_copy(K["slot"][:, NT * j:NT * j + NT], sl)
                D_()
            ins.then_inc(slots_done, 1)
            dve.tensor_tensor(lt, incl.unsqueeze(1).to_broadcast([P, SLOTS, E]), jj.unsqueeze(2).to_broadcast([P, SLOTS, E]), ALU.is_le)
            D_()
            dve.tensor_reduce(eid, lt, AX_X, ALU.add)
            D_()
            dve.tensor_scalar(eid, eid, float(E - 1), None, ALU.min)
            D_()
            dve.tensor_copy(K["expert"], eid)
            dve.tensor_copy(K["ends"], incl)
            dve.tensor_tensor(step[:, 0:SLOTS // 2 - 1], consts[:, 15:13 + SLOTS:2], incl[:, E - 1:E].to_broadcast([P, SLOTS // 2 - 1]), ALU.is_lt)
            D_()
            dve.tensor_reduce(last, step[:, 0:SLOTS // 2 - 1], AX_X, ALU.add)
            D_()
            dve.tensor_scalar(last, last, -1.0, None, ALU.add)
            D_()
            dve.tensor_copy(K["before_last"], last)
            dve.tensor_copy(eidb, eid)
            D_()
            for n in range(BUFFERS, E, BUFFERS):
                dve.tensor_scalar(step, eid, float(n), -float(BUFFERS), ALU.is_ge, ALU.mult)
                D_()
                dve.tensor_tensor(eidb, eidb, step, ALU.add)
                D_()
            dve.tensor_copy(K["buffer"], eidb)
            dve.wait_ge(t_turned, 1)
            dve.tensor_copy(K["token"], psum[:, 2, 0:SLOTS])


def load_expert(sp, A, K, e, b):
    for c, n in enumerate(("w_gate", "w_up")):
        sp.dma_start(K["GU"][:, KC * b:KC * b + KC, FF * c:FF * c + FF], A[n][0, e].rearrange("(k p) n -> p k n", p=P)).then_inc(K["w_in"][b], 16)
    sp.dma_start(K["Wd"][:, 2 * b:2 * b + 2, :], A["w_down"][0, e].rearrange("(k p) n -> p k n", p=P)).then_inc(K["w_in"][b], 16)


def phase_experts(nc, A, K, sb, psum):
    with ExitStack() as st:
        st.enter_context(nc.cleanup_on_exit())
        sem = lambda n: nc.alloc_semaphore(name="experts_" + n)
        pair = lambda n: [sem(n + "0"), sem(n + "1")]
        x_in, y_out = pair("x_in"), pair("y_out")
        weights_ready = sem("weights_ready")
        turned, xt_done, gu_done, silu_done, h_done, h_turned, ht_done, y_made, y_act, y_dve = (
            sem(n) for n in ("turned", "xt_done", "gu_done", "silu_done", "h_done", "h_turned", "ht_done", "y_made", "y_act", "y_dve"))
        X, XT = [sb(D) for _ in range(2)], [sb(KC, P) for _ in range(2)]
        hg, hT, Y = [sb(FF) for _ in range(2)], [sb(2, P) for _ in range(2)], [sb(D) for _ in range(2)]
        block = st.enter_context(nc.Block())
        PAIRS = SLOTS // 2

        def last_pair(e):
            return e.value_load(K["before_last"][0:1, 0:1], min_val=FEWEST // 2 - 2, max_val=PAIRS - 2) + 1

        @block.sync
        def _(sp):
            def say_ready(e):
                sp.wait_ge(K["w_in"][e % BUFFERS], 48 * (e // BUFFERS + 1))
                sp.sem_inc(weights_ready, 1)

            for e in range(BUFFERS - 2):
                say_ready(e)
            for e in range(BUFFERS, E):
                say_ready(e - 2)
                ends = sp.value_load(K["ends"][0:1, e - BUFFERS:e - BUFFERS + 1], min_val=0, max_val=SLOTS)
                sp.wait_ge(y_made, ends + 1)
                load_expert(sp, A, K, e, e % BUFFERS)
            for e in range(E - 2, E):
                say_ready(e)

        @block.gpsimd
        def _(pool):
            def gather(j, par):
                pool.indirect_dma_start(out=X[par], out_offset=None, in_=K["hn_dram"],
                                        in_offset=bass.IndirectOffsetOnAxis(ap=K["token"][:, j:j + 1], axis=0)).then_inc(x_in[par], 16)

            def store(j, par):
                pool.wait_ge(y_act, j + 1)
                pool.wait_ge(y_dve, j + 1)
                pool.dma_start(K["y_dram"][bass.ds(j * P, P), :], Y[par]).then_inc(y_out[par], 16)

            def pair_of_tiles(i):
                for par in range(2):
                    j = 2 * i + par
                    pool.wait_ge(turned, j - 1)
                    gather(j, par)
                    if par or i > 1:
                        store(j - 3, 1 - par)

            last = last_pair(pool)
            for j in range(2):
                gather(j, j)
            for i in range(1, FEWEST // 2):
                pair_of_tiles(i)
            for i in range(FEWEST // 2, PAIRS):
                with pool.If(last > i - 1):
                    pair_of_tiles(i)
            for n in (-1, 0, 1):
                store(2 * last + n, n % 2)

        @block.tensor
        def _(pe):
            def buffer_of(j):
                return pe.value_load(K["buffer"][0:1, bass.ds(j, 1)], min_val=0, max_val=BUFFERS - 1)

            def turn_hidden(j, par):
                pe.wait_ge(h_done, j + 1)
                for k in range(2):
                    mm = pe.transpose(psum[:, 4, P * k:P * k + P], hg[par][:, P * k:P * k + P], K["ident"])
                mm.then_inc(h_turned, 1)

            def turn(i, par):
                pe.wait_ge(x_in[par], 16 * i + 16)
                for k in range(KC):
                    mm = pe.transpose(psum[:, k // 4, P * (k % 4):P * (k % 4) + P], X[par][:, P * k:P * k + P], K["ident"])
                mm.then_inc(turned, 1)

            def down(j, par, first, b):
                pe.wait_ge(ht_done, j + 1)
                if not first:
                    pe.wait_ge(y_act, j)
                    pe.wait_ge(y_dve, j)
                for n in range(2):
                    for k in range(2):
                        mm = pe.matmul(psum[:, 5 + n, :], hT[par][:, k, :], K["Wd"][:, bass.ds(2 * b + k, 1), 512 * n:512 * n + 512], start=(k == 0), stop=(k == 1))
                mm.then_inc(y_made, 1)

            def step(i, par, first=False, end=False):
                j = 2 * i + par
                e = pe.value_load(K["expert"][0:1, bass.ds(j, 1)], min_val=0, max_val=E - 1)
                b = buffer_of(j)
                before = buffer_of(j - 1) if not (first and par == 0) else None
                pe.wait_ge(xt_done, j + 1)
                pe.wait_ge(weights_ready, e + 1)
                for k in range(KC):
                    mm = pe.matmul(psum[:, 2 + par, :], XT[par][:, k, :], K["GU"][:, bass.ds(KC * b + k, 1), :], start=(k == 0), stop=(k == KC - 1))
                mm.then_inc(gu_done, 1)
                if not end:
                    turn(i + par, 1 - par)
                if before is not None:
                    down(j - 1, 1 - par, first, before)
                turn_hidden(j, par)

            last = last_pair(pe)
            pe.sem_inc(y_made, 1)
            turn(0, 0)
            for par in range(2):
                step(0, par, first=True)
            with pe.Fori(1, PAIRS - 1) as i:
                with pe.If(i < last):
                    for par in range(2):
                        step(i, par)
            for par in range(2):
                step(last, par, end=par == 1)
            j = 2 * last + 1
            b = buffer_of(j)
            down(j, 1, False, b)

        @block.scalar
        def _(act):
            def silu(j, par):
                act.wait_ge(gu_done, j + 1)
                act.activation(hg[par], psum[:, 2 + par, 0:FF], ACT.Silu).then_inc(silu_done, 1)

            def result(j, par, i):
                act.wait_ge(y_made, j + 2)
                if i is not None:
                    act.wait_ge(y_out[par], 16 * i)
                act.activation(Y[par][:, 0:512], psum[:, 5, :], ACT.Copy).then_inc(y_act, 1)

            def hidden(j, par):
                act.wait_ge(h_turned, j + 1)
                act.activation(hT[par].rearrange("p a b -> p (a b)"), psum[:, 4, 0:2 * P], ACT.Copy).then_inc(ht_done, 1)

            silu(0, 0)
            hidden(0, 0)
            silu(1, 1)
            result(0, 0, None)
            hidden(1, 1)
            silu(2, 0)
            result(1, 1, None)
            hidden(2, 0)
            last = last_pair(act)
            with act.Fori(1, PAIRS - 1) as i:
                with act.If(i < last):
                    silu(2 * i + 1, 1)
                    result(2 * i, 0, i)
                    hidden(2 * i + 1, 1)
                    silu(2 * i + 2, 0)
                    result(2 * i + 1, 1, i)
                    hidden(2 * i + 2, 0)
            silu(2 * last + 1, 1)
            result(2 * last, 0, last)
            hidden(2 * last + 1, 1)
            result(2 * last + 1, 1, last)

        @block.vector
        def _(dve):
            def place(j, par, first):
                dve.wait_ge(turned, j + 1)
                if not first:
                    dve.wait_ge(gu_done, j - 1)
                dve.tensor_copy(XT[par].rearrange("p a b -> p (a b)"), psum[:, 0:2, :].rearrange("p a b -> p (a b)")).then_inc(xt_done, 1)

            def hidden(j, par):
                dve.wait_ge(silu_done, j + 1)
                dve.tensor_tensor(hg[par], hg[par], psum[:, 2 + par, FF:2 * FF], ALU.mult).then_inc(h_done, 1)

            def result(j, par, i):
                dve.wait_ge(y_made, j + 2)
                if i is not None:
                    dve.wait_ge(y_out[par], 16 * i)
                dve.tensor_copy(Y[par][:, 512:], psum[:, 6, :]).then_inc(y_dve, 1)

            place(0, 0, True)
            hidden(0, 0)
            place(1, 1, True)
            hidden(1, 1)
            place(2, 0, False)
            result(0, 0, None)
            hidden(2, 0)
            place(3, 1, False)
            result(1, 1, None)
            last = last_pair(dve)
            with dve.Fori(1, PAIRS - 1) as i:
                with dve.If(i < last):
                    hidden(2 * i + 1, 1)
                    place(2 * i + 2, 0, False)
                    result(2 * i, 0, i)
                    hidden(2 * i + 2, 0)
                    place(2 * i + 3, 1, False)
                    result(2 * i + 1, 1, i)
            hidden(2 * last + 1, 1)
            result(2 * last, 0, last)
            result(2 * last + 1, 1, last)
            for par in range(2):
                dve.wait_ge(y_out[par], 16 * last + 16)
                dve.tensor_copy(Y[par][:, 0:1], Y[par][:, 1:2])


def phase_combine(nc, A, K, out, sb, psum):
    with ExitStack() as st:
        st.enter_context(nc.cleanup_on_exit())
        sem = lambda n: nc.alloc_semaphore(name="combine_" + n)
        y_in, y_out = [sem("y_in0"), sem("y_in1")], [sem("y_out0"), sem("y_out1")]
        summed = sem("summed")
        Y, O = [sb(2, D) for _ in range(2)], [sb(D) for _ in range(2)]
        block = st.enter_context(nc.Block())

        @block.gpsimd
        def _(pool):
            for i in range(NT):
                if i >= 2:
                    pool.wait_ge(summed, i - 1)
                for j in range(2):
                    pool.indirect_dma_start(out=Y[i % 2][:ROWS[i], j, :], out_offset=None, in_=K["y_dram"],
                                            in_offset=bass.IndirectOffsetOnAxis(ap=K["slot"][:ROWS[i], NT * j + i:NT * j + i + 1], axis=0)).then_inc(y_in[i % 2], 16)

        @block.vector
        def _(dve):
            for i in range(NT):
                r, q = ROWS[i], i % 2
                dve.wait_ge(y_in[q], 32 * (i // 2 + 1))
                if i >= 2:
                    dve.wait_ge(y_out[q], 16 * (i // 2))
                dve.scalar_tensor_tensor(O[q][:r], Y[q][:r, 0, :], K["weight"][:r, 0, i:i + 1], K["h"][:r, i, :], ALU.mult, ALU.add)
                dve.drain()
                dve.scalar_tensor_tensor(O[q][:r], Y[q][:r, 1, :], K["weight"][:r, 1, i:i + 1], O[q][:r], ALU.mult, ALU.add).then_inc(summed, 1)

        @block.sync
        def _(sp):
            for i in range(NT):
                sp.wait_ge(summed, i + 1)
                if i == 0:
                    sp.dma_start(out["y_sample"].rearrange("a b d -> (a b) d"), O[0][META:FIRST]).then_inc(y_out[0], 16)
                else:
                    sp.dma_start(out["y_prompt"][0, P * (i - 1):P * i, :], O[i % 2]).then_inc(y_out[i % 2], 16)
            for q in range(2):
                sp.wait_ge(y_out[q], 16 * (5 - q))


INPUTS = ("x_prompt", "x_sample", "cache_k", "cache_v", "state_hgrn", "page_table", "meta_tokens", "rel_bias", "hg_lb_logits",
          "norm1_w", "w_in", "hg_onorm_w", "w_hg_out", "q_norm_w", "k_norm_w", "da_lambda", "da_onorm_w", "w_da_out", "w_o",
          "norm2_w", "w_router_group", "b_router_group", "w_router_expert", "b_router_expert", "w_gate", "w_up", "w_down")
OUTPUTS = {"y_prompt": (1, SEQ, D), "y_sample": (DB, DS, D),
           "new_k_prompt": (1, 1, META + SEQ, HEADS, P), "new_v_prompt": (1, 1, META + SEQ, HEADS, P),
           "new_state_prompt": (1, 1, HEADS, P, P),
           "new_k_sample": (1, DB, DS, HEADS, P), "new_v_sample": (1, DB, DS, HEADS, P),
           "new_state_sample": (1, DB, HEADS, P, P)}


def kernel(**inputs):
    import concourse.bacc as bacc
    from concourse.bass_utils import run_bass_kernel_spmd

    nc = bacc.Bacc("TRN2", target_bir_lowering=False, num_devices=1)
    arrays = {n: np.ascontiguousarray(inputs[n]) for n in INPUTS}
    arrays.update(constants())
    A = {n: nc.dram_tensor(n, a.shape, mybir.dt.from_np(a.dtype), kind="ExternalInput").ap() for n, a in arrays.items()}
    out = {n: nc.dram_tensor(n, shape, F32, kind="ExternalOutput").ap() for n, shape in OUTPUTS.items()}
    build(nc, A, out)
    result = run_bass_kernel_spmd(nc, [arrays], core_ids=[0]).results[0]
    return tuple(result[n] for n in OUTPUTS)
```
